# Optimizing a Trainium2 kernel written in Bass

```python
import jax, jax.numpy as jnp
from jax import lax
import numpy as np

D_MODEL = 1024
BATCH = 1
SEQ = 256
DEPTH = 1

MEM_LEN = 256
GLA_HEADS = 4
GLA_DK = 64
GLA_DV = 128
GLA_RANK = 16
GLA_TAU = 16.0
GLA_CHUNK = 64
GLA_QK = GLA_HEADS * GLA_DK
GLA_V = GLA_HEADS * GLA_DV
FOX_HEADS = 4
FOX_HD = 128
FOX_W = FOX_HEADS * FOX_HD
FOX_BLOCK = 128
MEM_HEADS = 4
MEM_HD = 128
MEM_W = MEM_HEADS * MEM_HD
N_BRANCH = 3
BRANCH_W = 512
D_FF = -(-8 * D_MODEL // (3 * 256)) * 256
EPS = 1e-6

IN_SIZES = (GLA_QK, GLA_QK, GLA_V, GLA_V, GLA_RANK,
            FOX_W, FOX_W, FOX_W, FOX_HEADS,
            MEM_W,
            N_BRANCH * D_MODEL)
IN_WIDTH = sum(IN_SIZES)
IN_OFFSETS = tuple(int(o) for o in np.cumsum(IN_SIZES)[:-1])


def _rmsnorm(x, g):
    xf = x.astype(jnp.float32)
    y = xf * lax.rsqrt(jnp.mean(xf * xf, axis=-1, keepdims=True) + EPS)
    return (y * g.astype(jnp.float32)).astype(x.dtype)

def _heads(t, n):
    b, s, w = t.shape
    return t.reshape(b, s, n, w // n).transpose(0, 2, 1, 3)

def _merge(t):
    b, h, s, d = t.shape
    return t.transpose(0, 2, 1, 3).reshape(b, s, h * d)

def _gla(q, k, v, log_a):
    out_dtype = v.dtype
    b, h, s, dk = q.shape
    dv = v.shape[-1]
    c = GLA_CHUNK
    n = s // c
    qc = (q.astype(jnp.float32) * (GLA_DK ** -0.5)).reshape(b, h, n, c, dk)
    kc = k.astype(jnp.float32).reshape(b, h, n, c, dk)
    vc = v.astype(jnp.float32).reshape(b, h, n, c, dv)
    cum = jnp.cumsum(log_a.astype(jnp.float32).reshape(b, h, n, c, dk), axis=-2)
    cum_last = cum[..., -1:, :]
    q_in = qc * jnp.exp(cum)
    k_in = kc * jnp.exp(-cum)
    k_out = kc * jnp.exp(cum_last - cum)
    tril = jnp.tril(jnp.ones((c, c), dtype=bool))
    attn = jnp.where(tril, jnp.einsum('bhncd,bhnsd->bhncs', q_in, k_in), 0.0)
    o_intra = jnp.einsum('bhncs,bhnsv->bhncv', attn, vc)
    chunk_state = jnp.einsum('bhncd,bhncv->bhndv', k_out, vc)
    decay = jnp.exp(cum_last[..., 0, :])

    def step(state, inp):
        d, cs = inp
        return d[..., None] * state + cs, state

    _, s_in = lax.scan(step, jnp.zeros((b, h, dk, dv), jnp.float32),
                       (jnp.moveaxis(decay, 2, 0), jnp.moveaxis(chunk_state, 2, 0)))
    s_in = jnp.moveaxis(s_in, 0, 2)
    o_inter = jnp.einsum('bhncd,bhndv->bhncv', q_in, s_in)
    return (o_intra + o_inter).reshape(b, h, s, dv).astype(out_dtype)

def _fox(q, k, v, log_f):
    b, h, s, hd = q.shape
    nb = s // FOX_BLOCK
    scale = hd ** -0.5
    cum = jnp.cumsum(log_f, axis=-1)
    qb = jnp.moveaxis(q.reshape(b, h, nb, FOX_BLOCK, hd), 2, 0)
    cb = jnp.moveaxis(cum.reshape(b, h, nb, FOX_BLOCK), 2, 0)
    starts = jnp.arange(nb, dtype=jnp.int32) * FOX_BLOCK
    kpos = jnp.arange(s, dtype=jnp.int32)

    def block(args):
        q_i, c_i, i0 = args
        logits = (jnp.einsum('bhqd,bhkd->bhqk', q_i, k).astype(jnp.float32) * scale
                  + c_i[..., None] - cum[:, :, None, :])
        qpos = i0 + jnp.arange(FOX_BLOCK, dtype=jnp.int32)
        mask = kpos[None, :] <= qpos[:, None]
        p = jax.nn.softmax(jnp.where(mask, logits, -jnp.inf), axis=-1)
        return jnp.einsum('bhqk,bhkd->bhqd', p.astype(v.dtype), v)

    out = lax.map(block, (qb, cb, starts))
    return jnp.moveaxis(out, 0, 2).reshape(b, h, s, hd)

def _cross(q, k, v):
    logits = jnp.einsum('bhqd,bhkd->bhqk', q, k).astype(jnp.float32) * (q.shape[-1] ** -0.5)
    p = jax.nn.softmax(logits, axis=-1)
    return jnp.einsum('bhqk,bhkd->bhqd', p.astype(v.dtype), v)

def first_inputs(seed: int = 0) -> dict:
    key = jax.random.key(seed)
    ks = jax.random.split(key, 24)
    L, D = DEPTH, D_MODEL

    def nrm(k, shape, scale):
        return jax.random.normal(k, shape, jnp.float32) * scale

    def gain(k, shape):
        return 1.0 + 0.02 * jax.random.normal(k, shape, jnp.float32)

    return {
        "x": nrm(ks[0], (BATCH, SEQ, D), 1.0),
        "mem": nrm(ks[1], (BATCH, MEM_LEN, D), 1.0),
        "g_mix": gain(ks[2], (L, D)),
        "w_in": nrm(ks[3], (L, D, IN_WIDTH), D ** -0.5),
        "w_gla_a2": nrm(ks[4], (L, GLA_RANK, GLA_QK), GLA_RANK ** -0.5),
        "b_gla_a": nrm(ks[5], (L, GLA_QK), 0.1),
        "g_gla_out": gain(ks[6], (L, GLA_V)),
        "b_fox_f": nrm(ks[7], (L, FOX_HEADS), 0.1),
        "g_fox_q": gain(ks[8], (L, FOX_HD)),
        "g_fox_k": gain(ks[9], (L, FOX_HD)),
        "g_mem": gain(ks[10], (L, D)),
        "w_mem_kv": nrm(ks[11], (L, D, 2 * MEM_W), D ** -0.5),
        "g_mem_q": gain(ks[12], (L, MEM_HD)),
        "g_mem_k": gain(ks[13], (L, MEM_HD)),
        "b_gate": nrm(ks[14], (L, N_BRANCH * D), 0.1),
        "w_branch": nrm(ks[15], (L, N_BRANCH, BRANCH_W, D), BRANCH_W ** -0.5),
        "w_out": nrm(ks[16], (L, D, D), D ** -0.5),
        "g_ffn": gain(ks[17], (L, D)),
        "w_ffn_gate": nrm(ks[18], (L, D, D_FF), D ** -0.5),
        "w_ffn_up": nrm(ks[19], (L, D, D_FF), D ** -0.5),
        "w_ffn_down": nrm(ks[20], (L, D_FF, D), D_FF ** -0.5),
    }

def first_block(x, mem, g_mix, w_in, w_gla_a2, b_gla_a, g_gla_out, b_fox_f, g_fox_q, g_fox_k,
              g_mem, w_mem_kv, g_mem_q, g_mem_k, b_gate, w_branch, w_out,
              g_ffn, w_ffn_gate, w_ffn_up, w_ffn_down):
    for l in range(DEPTH):
        h = _rmsnorm(x, g_mix[l])
        proj = h @ w_in[l]
        (gq, gk, gv, gg, ga1, fq, fk, fv, ff, mq, bg) = jnp.split(proj, IN_OFFSETS, axis=-1)

        log_a = jax.nn.log_sigmoid((ga1 @ w_gla_a2[l] + b_gla_a[l]).astype(jnp.float32)) / GLA_TAU
        o_gla = _gla(_heads(gq, GLA_HEADS), _heads(gk, GLA_HEADS), _heads(gv, GLA_HEADS),
                     _heads(log_a, GLA_HEADS))
        o_gla = _rmsnorm(o_gla, g_gla_out[l].reshape(GLA_HEADS, 1, GLA_DV))
        y_gla = _merge(o_gla) * jax.nn.silu(gg)

        log_f = jax.nn.log_sigmoid((ff + b_fox_f[l]).astype(jnp.float32)).transpose(0, 2, 1)
        o_fox = _fox(_rmsnorm(_heads(fq, FOX_HEADS), g_fox_q[l]),
                     _rmsnorm(_heads(fk, FOX_HEADS), g_fox_k[l]),
                     _heads(fv, FOX_HEADS), log_f)
        y_fox = _merge(o_fox)

        mkv = _rmsnorm(mem, g_mem[l]) @ w_mem_kv[l]
        mk, mv = jnp.split(mkv, 2, axis=-1)
        o_mem = _cross(_rmsnorm(_heads(mq, MEM_HEADS), g_mem_q[l]),
                       _rmsnorm(_heads(mk, MEM_HEADS), g_mem_k[l]),
                       _heads(mv, MEM_HEADS))
        y_mem = _merge(o_mem)

        gates = jax.nn.sigmoid(bg + b_gate[l])
        merged = None
        for i, y_b in enumerate((y_gla, y_fox, y_mem)):
            term = gates[..., i * D_MODEL:(i + 1) * D_MODEL] * (y_b @ w_branch[l, i])
            merged = term if merged is None else merged + term
        x = x + merged @ w_out[l]

        h2 = _rmsnorm(x, g_ffn[l])
        x = x + (jax.nn.silu(h2 @ w_ffn_gate[l]) * (h2 @ w_ffn_up[l])) @ w_ffn_down[l]
    return x


DEPTH_2 = 2

N_MIXERS = 2
NORM_EPS = 1e-6
NEG = -1e30
D_FF_2 = 4 * D_MODEL
RET_HEADS = 4
RET_DK = D_MODEL // RET_HEADS
RET_DV = 2 * RET_DK
RET_CHUNK = 128
RET_THETA = 10000.0
RET_IN = 2 * RET_HEADS * RET_DK + 2 * RET_HEADS * RET_DV
MOBA_HEADS = 8
MOBA_DH = D_MODEL // MOBA_HEADS
MOBA_BLOCK = 256
MOBA_TOPK = 3
MOBA_QCHUNK = 8
ROPE_THETA = 500000.0
ROPE_DIM = MOBA_DH // 4
MOBA_IN = 3 * MOBA_HEADS * MOBA_DH


def rms_norm(x, g):
    xf = x.astype(jnp.float32)
    y = xf * lax.rsqrt(jnp.mean(xf * xf, axis=-1, keepdims=True) + NORM_EPS)
    return (y * g.astype(jnp.float32)).astype(x.dtype)

def sq_relu_mlp(x, w_up, w_down):
    h = jax.nn.relu(x @ w_up)
    return (h * h) @ w_down

def retnet_rotary(x, pos):
    d = x.shape[-1]
    freq = 1.0 / (RET_THETA ** jnp.linspace(0.0, 1.0, d // 2, dtype=jnp.float32))
    ang = pos[:, None].astype(jnp.float32) * freq[None, :]
    cos, sin = jnp.cos(ang), jnp.sin(ang)
    x1 = x[..., 0::2].astype(jnp.float32)
    x2 = x[..., 1::2].astype(jnp.float32)
    y = jnp.stack([x1 * cos - x2 * sin, x1 * sin + x2 * cos], axis=-1)
    return y.reshape(x.shape).astype(x.dtype)

def partial_rope(x, pos):
    half = ROPE_DIM // 2
    inv = ROPE_THETA ** (-jnp.arange(0, ROPE_DIM, 2, dtype=jnp.float32) / ROPE_DIM)
    ang = pos[:, None].astype(jnp.float32) * inv[None, :]
    cos, sin = jnp.cos(ang), jnp.sin(ang)
    x1 = x[..., :half].astype(jnp.float32)
    x2 = x[..., half:ROPE_DIM].astype(jnp.float32)
    rot = jnp.concatenate([x1 * cos - x2 * sin, x2 * cos + x1 * sin], axis=-1)
    return jnp.concatenate([rot.astype(x.dtype), x[..., ROPE_DIM:]], axis=-1)

def retention(h, w_in, w_out):
    B, S, _ = h.shape
    H, DK, DV, L = RET_HEADS, RET_DK, RET_DV, RET_CHUNK
    C = S // L
    q, k, v, g = jnp.split(h @ w_in, [H * DK, 2 * H * DK, 2 * H * DK + H * DV], axis=-1)
    q = q.reshape(B, S, H, DK).transpose(0, 2, 1, 3)
    k = k.reshape(B, S, H, DK).transpose(0, 2, 1, 3)
    v = v.reshape(B, S, H, DV).transpose(0, 2, 1, 3)
    pos = jnp.arange(S)
    q = retnet_rotary(q, pos)
    k = retnet_rotary(k, pos) * (DK ** -0.5)

    log_gamma = jnp.log(1.0 - 2.0 ** (-5.0 - jnp.arange(H, dtype=jnp.float32)))
    idx = jnp.arange(L, dtype=jnp.float32)
    diff = idx[:, None] - idx[None, :]
    d_intra = jnp.where(diff >= 0, jnp.exp(log_gamma[:, None, None] * jnp.maximum(diff, 0.0)), 0.0)
    q_decay = jnp.exp(log_gamma[:, None] * (idx + 1.0))[None, :, :, None]
    k_decay = jnp.exp(log_gamma[:, None] * (L - 1.0 - idx))[None, :, :, None]
    chunk_decay = jnp.exp(log_gamma * L)[None, :, None, None]

    qc = q.reshape(B, H, C, L, DK)
    kc = k.reshape(B, H, C, L, DK)
    vc = v.reshape(B, H, C, L, DV)
    scores = jnp.einsum('bhcid,bhcjd->bhcij', qc, kc).astype(jnp.float32) * d_intra[None, :, None]
    o_intra = jnp.einsum('bhcij,bhcje->bhcie', scores, vc)

    def step(state, inp):
        q_c, k_c, v_c = inp
        cross = jnp.einsum('bhid,bhde->bhie', q_c, state) * q_decay
        state = state * chunk_decay + jnp.einsum('bhjd,bhje->bhde', k_c * k_decay, v_c)
        return state, cross

    init = jnp.zeros((B, H, DK, DV), jnp.float32)
    xs = (qc.transpose(2, 0, 1, 3, 4), kc.transpose(2, 0, 1, 3, 4), vc.transpose(2, 0, 1, 3, 4))
    _, o_cross = lax.scan(step, init, xs)
    o = (o_intra + o_cross.transpose(1, 2, 0, 3, 4)).reshape(B, H, S, DV)
    o = o * lax.rsqrt(jnp.mean(o * o, axis=-1, keepdims=True) + NORM_EPS)
    o = o.transpose(0, 2, 1, 3).reshape(B, S, H * DV)
    o = o * jax.nn.silu(g.astype(jnp.float32))
    return o.astype(h.dtype) @ w_out

def moba_attention(h, w_in, w_out):
    B, S, _ = h.shape
    H, Dh, BS, QC = MOBA_HEADS, MOBA_DH, MOBA_BLOCK, MOBA_QCHUNK
    nb = -(-S // BS)
    Sp = nb * BS
    K_SEL = min(MOBA_TOPK, nb)
    q, k, v = jnp.split(h @ w_in, 3, axis=-1)
    q = q.reshape(B, S, H, Dh).transpose(0, 2, 1, 3)
    k = k.reshape(B, S, H, Dh).transpose(0, 2, 1, 3)
    v = v.reshape(B, S, H, Dh).transpose(0, 2, 1, 3)
    pos = jnp.arange(S)
    q = partial_rope(q, pos) * (Dh ** -0.5)
    k = partial_rope(k, pos)
    pad = ((0, 0), (0, 0), (0, Sp - S), (0, 0))
    q, k, v = jnp.pad(q, pad), jnp.pad(k, pad), jnp.pad(v, pad)
    qb = q.reshape(B, H, nb, BS, Dh)
    kb = k.reshape(B, H, nb, BS, Dh)
    vb = v.reshape(B, H, nb, BS, Dh)

    causal = jnp.tril(jnp.ones((BS, BS), dtype=bool))
    s_own = jnp.einsum('bhnid,bhnjd->bhnij', qb, kb).astype(jnp.float32)
    s_own = jnp.where(causal, s_own, NEG)
    m_own = jnp.max(s_own, axis=-1)
    p_own = jnp.exp(s_own - m_own[..., None])
    l_own = jnp.sum(p_own, axis=-1)
    o_own = jnp.einsum('bhnij,bhnjd->bhnid', p_own, vb)
    m_own, l_own = m_own.reshape(B, H, Sp), l_own.reshape(B, H, Sp)
    o_own = o_own.reshape(B, H, Sp, Dh)

    k_mean = jnp.mean(kb.astype(jnp.float32), axis=3)
    gate = jnp.einsum('bhsd,bhnd->bhsn', q.astype(jnp.float32), k_mean)
    q_blk = jnp.arange(Sp) // BS
    past = jnp.arange(nb)[None, :] < q_blk[:, None]
    gate = jnp.where(past, gate, NEG)
    _, sel = lax.top_k(gate, K_SEL)
    valid = sel < q_blk[:, None]

    nq = Sp // QC
    q_ch = q.reshape(B, H, nq, QC, Dh).transpose(2, 0, 1, 3, 4)
    sel_ch = sel.reshape(B, H, nq, QC, K_SEL).transpose(2, 0, 1, 3, 4)
    val_ch = valid.reshape(B, H, nq, QC, K_SEL).transpose(2, 0, 1, 3, 4)
    bi = jnp.arange(B)[:, None, None, None]
    hi = jnp.arange(H)[None, :, None, None]

    def attend_selected(args):
        qc, sc, vc = args
        k_sel = kb[bi, hi, sc]
        v_sel = vb[bi, hi, sc]
        s = jnp.einsum('bhqd,bhqkjd->bhqkj', qc, k_sel).astype(jnp.float32)
        s = jnp.where(vc[..., None], s, NEG)
        m = jnp.max(s, axis=(3, 4))
        p = jnp.exp(s - m[..., None, None])
        l = jnp.sum(p, axis=(3, 4))
        o = jnp.einsum('bhqkj,bhqkjd->bhqd', p, v_sel)
        return m, l, o

    m_sel, l_sel, o_sel = lax.map(attend_selected, (q_ch, sel_ch, val_ch))
    m_sel = m_sel.transpose(1, 2, 0, 3).reshape(B, H, Sp)
    l_sel = l_sel.transpose(1, 2, 0, 3).reshape(B, H, Sp)
    o_sel = o_sel.transpose(1, 2, 0, 3, 4).reshape(B, H, Sp, Dh)

    m = jnp.maximum(m_own, m_sel)
    a = jnp.exp(m_own - m)
    b = jnp.exp(m_sel - m)
    o = (o_own * a[..., None] + o_sel * b[..., None]) / (l_own * a + l_sel * b)[..., None]
    o = o[:, :, :S].transpose(0, 2, 1, 3).reshape(B, S, H * Dh)
    return o.astype(h.dtype) @ w_out

def second_inputs(seed: int = 0) -> dict:
    key = jax.random.key(seed)
    ks = jax.random.split(key, 32)
    f32 = jnp.float32

    def w(k, shape):
        return jax.random.normal(k, shape, f32) * (shape[0] ** -0.5)

    def gain(k):
        return 1.0 + 0.05 * jax.random.normal(k, (D_MODEL,), f32)

    return {
        "x": jax.random.normal(ks[0], (BATCH, SEQ, D_MODEL), f32),
        "ln_mix_pre_0": gain(ks[1]),
        "ln_mix_post_0": gain(ks[2]),
        "w_in_0": w(ks[3], (D_MODEL, RET_IN)),
        "w_out_0": w(ks[4], (RET_HEADS * RET_DV, D_MODEL)),
        "ln_mlp_pre_0": gain(ks[5]),
        "ln_mlp_post_0": gain(ks[6]),
        "w_up_0": w(ks[7], (D_MODEL, D_FF_2)),
        "w_down_0": w(ks[8], (D_FF_2, D_MODEL)),
        "ln_mix_pre_1": gain(ks[9]),
        "ln_mix_post_1": gain(ks[10]),
        "w_in_1": w(ks[11], (D_MODEL, MOBA_IN)),
        "w_out_1": w(ks[12], (MOBA_HEADS * MOBA_DH, D_MODEL)),
        "ln_mlp_pre_1": gain(ks[13]),
        "ln_mlp_post_1": gain(ks[14]),
        "w_up_1": w(ks[15], (D_MODEL, D_FF_2)),
        "w_down_1": w(ks[16], (D_FF_2, D_MODEL)),
    }

def second_block(x, ln_mix_pre_0, ln_mix_post_0, w_in_0, w_out_0, ln_mlp_pre_0, ln_mlp_post_0, w_up_0, w_down_0,
              ln_mix_pre_1, ln_mix_post_1, w_in_1, w_out_1, ln_mlp_pre_1, ln_mlp_post_1, w_up_1, w_down_1):
    mixers = (retention, moba_attention)
    layers = (
        (ln_mix_pre_0, ln_mix_post_0, w_in_0, w_out_0, ln_mlp_pre_0, ln_mlp_post_0, w_up_0, w_down_0),
        (ln_mix_pre_1, ln_mix_post_1, w_in_1, w_out_1, ln_mlp_pre_1, ln_mlp_post_1, w_up_1, w_down_1),
    )
    h = x
    for i in range(DEPTH_2):
        pre, post, w_in, w_out, mpre, mpost, w_up, w_down = layers[i]
        h = h + rms_norm(mixers[i % N_MIXERS](rms_norm(h, pre), w_in, w_out), post)
        h = h + rms_norm(sq_relu_mlp(rms_norm(h, mpre), w_up, w_down), mpost)
    return h


def setup_inputs(seed=0):
    out = dict(first_inputs(seed))
    for name, value in second_inputs(seed + 1).items():
        if name != "x":
            out[name + "_2"] = value
    return out


def reference(
    x, mem, g_mix, w_in, w_gla_a2, b_gla_a, g_gla_out, b_fox_f, g_fox_q, g_fox_k, g_mem,
    w_mem_kv, g_mem_q, g_mem_k, b_gate, w_branch, w_out, g_ffn, w_ffn_gate, w_ffn_up,
    w_ffn_down, ln_mix_pre_0_2, ln_mix_post_0_2, w_in_0_2, w_out_0_2, ln_mlp_pre_0_2,
    ln_mlp_post_0_2, w_up_0_2, w_down_0_2, ln_mix_pre_1_2, ln_mix_post_1_2, w_in_1_2, w_out_1_2,
    ln_mlp_pre_1_2, ln_mlp_post_1_2, w_up_1_2, w_down_1_2,
):
    x = first_block(
        x, mem, g_mix, w_in, w_gla_a2, b_gla_a, g_gla_out, b_fox_f, g_fox_q, g_fox_k, g_mem,
        w_mem_kv, g_mem_q, g_mem_k, b_gate, w_branch, w_out, g_ffn, w_ffn_gate, w_ffn_up,
        w_ffn_down,
    )
    return second_block(
        x, ln_mix_pre_0_2, ln_mix_post_0_2, w_in_0_2, w_out_0_2, ln_mlp_pre_0_2,
        ln_mlp_post_0_2, w_up_0_2, w_down_0_2, ln_mix_pre_1_2, ln_mix_post_1_2, w_in_1_2,
        w_out_1_2, ln_mlp_pre_1_2, ln_mlp_post_1_2, w_up_1_2, w_down_1_2,
    )


_drawn_inputs = setup_inputs


def setup_inputs(seed=0):
    import zlib

    import numpy as np

    out = dict(_drawn_inputs(seed))
    spreads = {}
    factors = {'g_gla_out': 35.448,
     'b_fox_f': 26.056,
     'g_fox_q': 104.588,
     'g_fox_k': 107.333,
     'g_mem': 8.0,
     'g_mem_q': 8.0,
     'g_mem_k': 8.0,
     'ln_mlp_post_1_2': 21.488,
     'b_gla_a': 3.072,
     'g_ffn': 8.0,
     'ln_mix_post_0_2': 42.184,
     'ln_mlp_pre_0_2': 37.408,
     'ln_mlp_post_0_2': 40.816,
     'ln_mix_pre_1_2': 3.489,
     'ln_mix_post_1_2': 44.016,
     'ln_mix_pre_0_2': 4.31,
     'ln_mlp_pre_1_2': 8.0}
    for name, (base, spread) in spreads.items():
        noise = np.random.default_rng([zlib.crc32(name.encode()), seed]).standard_normal(out[name].shape)
        drawn = base * np.exp(spread * noise) if base else spread * noise
        out[name] = __import__('jax').numpy.asarray(drawn.astype(out[name].dtype))
    for name, factor in factors.items():
        out[name] = (out[name] * factor).astype(out[name].dtype)
    return out
```

```python
from contextlib import ExitStack

import numpy as np
import concourse.bass as bass
from concourse import mybir

F32 = mybir.dt.float32
F32R = mybir.dt.float32r
U32 = mybir.dt.uint32
ALU = mybir.AluOpType
ACT = mybir.ActivationFunctionType
AX = mybir.AxisListType

P = 128
TOK = 256
D = 1024
DK = D // P
C = 512
EPS = 1e-6
NEG = -1e30
FFN = 2816
FFK = FFN // P
MLP = 4096
MLPK = MLP // P
HD = 128
RING = 4
GK = 4

A_UNITS = ["mk", "mv", "mq", "gqk", "gv", "gg", "fq", "fk", "fv"]
BRANCHES = ["mem", "gla", "fox"]
GATES = [f"gate_{b}{n}" for n in range(2) for b in BRANCHES]


def plan():
    G, U, kts = {}, {}, []

    def unit(name, widths):
        U[name] = len(U)
        G[name] = len(kts)
        kts.extend(widths)

    for n in A_UNITS:
        unit(n, [4, 4])
    for n in range(2):
        for b in BRANCHES:
            unit(f"gate_{b}{n}", [4, 4])
        for b in BRANCHES:
            unit(f"branch_{b}{n}", [4])
    for n in range(2):
        unit(f"wout{n}", [4, 4])
    for n in range(FFN // 256):
        unit(f"ffn{n}", [4, 4])
    for n in range(2):
        unit(f"ffd{n}", [4, 4, 4, 4, 4, 2])
    for n in range(12):
        unit(f"ret{n}", [4, 4])
    for n in range(2):
        unit(f"reto{n}", [4] * 4)
    for n in range(8):
        unit(f"up0_{n}", [4, 4])
    for n in range(2):
        unit(f"down0_{n}", [4] * 8)
    for n in range(6):
        unit(f"moba{n}", [4, 4])
    for n in range(2):
        unit(f"mobao{n}", [4, 4])
    for n in range(8):
        unit(f"up1_{n}", [4, 4])
    for n in range(2):
        unit(f"down1_{n}", [4] * 8)
    return G, U, kts


G, U, KTS = plan()
NG = len(KTS)
UNITS = list(U)
GEND = {n: (G[UNITS[k + 1]] if k + 1 < len(UNITS) else NG) for k, n in enumerate(UNITS)}


def plan_drain():
    drain, count = {}, {"act": 0, "dve": 0}
    for n in UNITS:
        by = "dve" if n.startswith(("gate", "branch", "wout", "ffd", "reto", "down", "mobao")) else "act"
        drain[n] = (by, count[by])
        count[by] += 2
    return drain


DRAIN = plan_drain()

MOBA_COLS = [0, 1024, 512, 1536, 2048, 2560]
IN_COLS = {"gqk": 0, "gv": 512, "gg": 1024, "fq": 1552, "fk": 2064, "fv": 2576, "mq": 3092}
GATE_COL = {"gla": 3604, "fox": 3604 + D, "mem": 3604 + 2 * D}
BRANCH_ROW = {"gla": 0, "fox": 1, "mem": 2}


def plan_aux():
    plan, used = {}, [0] * 4

    def use(name, banks, first=0):
        for b, bank in enumerate(banks):
            used[bank] += 1
            plan[(name, first + b)] = (bank, used[bank])

    use("memT", [0, 1, 2, 3])
    use("xT", [0, 1, 2, 3])
    use("small", [0])
    use("gaT", [1])
    use("mkT", [2, 3])
    use("z", [0])
    use("foxcum", [1])
    use("cum", [2])
    use("suf", [3])
    use("dec", [0])
    use("mqT", [1, 2])
    use("gqT", [3])
    use("gkT", [0])
    use("attn", [1, 2])
    use("cs", [3, 0])
    use("o", [1, 2])
    use("gyT", [3, 0])
    use("msc", [0, 1, 2, 3])
    use("mpT", [0, 1, 2, 3])
    use("moT", [0, 1, 2, 3])
    use("fqT", [0, 1])
    use("fkT", [2, 3])
    use("fsc", [0, 1, 2, 3])
    use("fpT", [0, 1, 2, 3])
    use("foT", [0, 1, 2, 3])
    use("mgT", [0, 1, 2, 3])
    use("x1T", [0, 1, 2, 3])
    for n in range(FFN // 256):
        use(f"ffT{n}", [n % 2])
    use("x2T", [0, 1, 2, 3])
    use("rqT0", [0, 1])
    use("rqT1", [2, 3])
    use("rkT0", [0, 1])
    use("rkT1", [2, 3])
    use("rsc", [0, 1, 2, 3])
    for h in range(4):
        use(f"ro{h}", [2 * h % 4, 2 * h % 4 + 1])
    for h in range(4):
        use(f"ryT{h}", [2 * h % 4, 2 * h % 4 + 1])
    use("x3T", [0, 1, 2, 3])
    for n in range(8):
        use(f"h0T{n}", [2 * n % 4, 2 * n % 4 + 1])
    use("x4T", [0, 1, 2, 3])
    use("bqT0", [0, 1])
    use("bkT0", [2, 3])
    use("bsc", [0, 1, 2, 3])
    use("bqT1", [0, 1])
    use("bkT1", [2, 3])
    use("bpT", [0, 1, 2, 3])
    use("boT", [0, 1, 2, 3])
    use("bsc", [0, 1, 2, 3], 4)
    use("bpT", [0, 1, 2, 3], 4)
    use("boT", [0, 1, 2, 3], 4)
    use("x5T", [0, 1, 2, 3])
    for n in range(8):
        use(f"h1T{n}", [2 * n % 4, 2 * n % 4 + 1])
    return plan


AUX = plan_aux()

CONST = {}


def pack_constants():
    s = np.arange(P)[:, None]
    i = np.arange(P)[None, :]
    same = (s // 64) == (i // 64)
    parts = {
        "ident": np.eye(P),
        "chunk_upto": (s <= i) & same,
        "chunk_after": (s > i) & same,
        "upto": s <= i,
        "ones": np.ones((P, P)),
        "zero_mask": np.zeros((P, P)),
        "tri_mask": np.where(i <= s, 0.0, NEG),
        "full_mask": np.full((P, P), NEG),
        "half": np.concatenate([s < 64, s >= 64], axis=1),
        "minus_half": np.full((P, 1), -0.5),
        "eps": np.full((P, 1), EPS),
    }
    at = 0
    for k, v in parts.items():
        CONST[k] = (at, v.shape[1])
        at += v.shape[1]
    return np.concatenate([np.asarray(v, np.float32) for v in parts.values()], axis=1)


def rotary_tables():
    f = np.float32
    pos = np.arange(TOK, dtype=f)[:, None]
    freq = (1.0 / (f(10000.0) ** np.linspace(0.0, 1.0, 128, dtype=f))).astype(f)
    ang = (pos * freq[None, :]).astype(f)
    cos, sin = np.cos(ang), np.sin(ang)
    cc = np.repeat(cos, 2, axis=1)
    ss = np.stack([-sin, sin], axis=-1).reshape(TOK, 256)
    inv = (f(500000.0) ** (-np.arange(0, 32, 2, dtype=f) / f(32))).astype(f)
    ang = (pos * inv[None, :]).astype(f)
    mc, ms = np.cos(ang), np.sin(ang)
    tiles = lambda a: a.reshape(2, P, -1).transpose(1, 0, 2)
    ret = np.concatenate([tiles(cc), tiles(ss)], axis=2)
    moba = np.concatenate([tiles(mc), tiles(ms)], axis=2)
    lg = np.log(f(1.0) - f(2.0) ** (f(-5.0) - np.arange(4, dtype=f))).astype(f)
    j = np.arange(P, dtype=f)[:, None]
    i = np.arange(P, dtype=f)[None, :]
    dm = []
    for h in range(4):
        own = np.where(i >= j, np.exp(lg[h] * np.maximum(i - j, 0)), 0)
        cross = np.exp(lg[h] * (P - 1.0 - j)) * np.exp(lg[h] * (i + 1.0))
        dm.append(np.concatenate([own, cross, own], axis=1))
    return ret.astype(f), moba.astype(f), np.stack(dm, axis=1).astype(f)


CPACK = pack_constants()

GAIN_COLS = {}
_at = 0
for _n, _w in (("g_mix", 8), ("g_mem", 8), ("g_ffn", 8), ("pre0", 8), ("mpre0", 8), ("pre1", 8), ("mpre1", 8),
               ("g_gla", 4), ("g_fq", 1), ("g_fk", 1), ("g_mq", 1), ("g_mk", 1)):
    GAIN_COLS[_n] = (_at, _w)
    _at += _w
NGAIN = _at

SCAL = {}
_at = 0
for _n, _w in (
    [("b_fox", 4), ("gfq_s", 1), ("gmq_s", 1)]
    + [(f"{k}{w}", 2) for k in ("mem", "x0", "x1", "x2", "x3", "x4", "x5", "x6") for w in ("_ss", "_var", "_rstd")]
    + [("x0_nrstd", 2), ("x1_nrstd", 2), ("x2_nrstd", 2)]
    + [(f"{k}{w}", 8) for k in ("mk", "mq", "fq", "fk", "go", "ro") for w in ("_ss", "_var", "_rstd")]
    + [(f"{k}_{w}", n) for k in ("p2", "p3", "p4", "p5") for w, n in (("ss", 4), ("tot", 2), ("var", 2), ("rstd", 2))]
    + [("ga", 32), ("ffz", 8), ("ffa", 8), ("ffl", 8), ("lf", 8), ("nlf", 8), ("foxc", 8), ("dec", 8)]
    + [(f"{k}_{w}", 8) for k in ("ms", "fs") for w in ("nm", "sum", "rec")]
    + [(f"bs_{w}", 16) for w in ("nm", "sum", "b", "l", "rec")]
):
    SCAL[_n] = (_at, _w)
    _at += _w
NSCAL = _at


def build(nc, wstream, x_in, mem_in, cpack, gpack, wsmall, w_a2, b_a, b_fox, b_gate, post, rett, mobat, dmask, out):
    ctx = ExitStack()
    with ctx:
        KB = 1024
        BASE = 16640

        def at(name, shape, kb, dt=F32):
            return nc.alloc_sbuf_tensor_at(name, shape, dt, offset=BASE + int(kb * KB))

        raw = at("raw", [P, RING, GK, C], 0)
        Wh = at("Wh", [P, RING, GK, C], 32, F32R)
        Wl = at("Wl", [P, RING, GK, C], 64, F32R)
        x = at("x", [P, 2, D], 96)
        xTh = at("xTh", [P, DK, TOK], 104, F32R)
        xTl = at("xTl", [P, DK, TOK], 112, F32R)
        cst = at("cst", [P, CPACK.shape[1]], 120)
        gains = at("gains", [P, NGAIN], 124.25)
        sc = at("sc", [P, NSCAL], 124.5)
        grow = at("grow", [P, D], 127)
        R = 131
        memTh = at("memTh", [P, DK, TOK], R, F32R)
        memTl = at("memTl", [P, DK, TOK], R + 8, F32R)
        yT = {b: (at(f"yTh_{b}", [P, 4, TOK], R + 8 * n, F32R), at(f"yTl_{b}", [P, 4, TOK], R + 8 * n + 4, F32R))
              for n, b in enumerate(("mem", "fox", "gla"))}
        gla_e = at("gla_e", [P, 4, 2, 256], R + 16)
        MK = at("MK", [P, 2, C], R + 24)
        MQ = at("MQ", [P, 2, C], R + 28)
        GQK = at("GQK", [P, 2, C], R + 32)
        FQ = at("FQ", [P, 2, C], R + 24)
        FK = at("FK", [P, 2, C], R + 28)
        state = at("state", [P, 3, 2, P], R + 28)
        merged = at("merged", [P, 2, D], R + 24)
        MV = at("MV", [P, 2, C], R + 36)
        FV = at("FV", [P, 2, C], R + 40)
        GV = at("GV", [P, 2, C], R + 44)
        GG = at("GG", [P, 2, C], R + 48)
        gate = {"mem": at("gate_mem", [P, 2, C], R + 32), "gla": at("gate_gla", [P, 2, C], R + 48),
                "fox": at("gate_fox", [P, 2, C], R + 44)}
        wsm = at("wsm", [P, DK, 20], R + 40)
        wsmh = at("wsmh", [P, DK, 20], R + 40.75, F32R)
        wsml = at("wsml", [P, DK, 20], R + 41.5, F32R)
        wa2 = at("wa2", [16, 256], R + 42.25)
        brow = at("brow", [1, 256], R + 43.25)
        gaT = at("gaT", [16, TOK], R + 48)
        mqT = at("mqT", [P, 4, TOK], R + 52)
        mkT = at("mkT", [P, 4, TOK], R + 56)
        fpT = at("fpT", [P, 4, 2, TOK], R + 52)
        fqT = at("fqT", [P, 4, TOK], R + 60)
        fkT = at("fkT", [P, 4, TOK], R + 64)
        mpT = at("mpT", [P, 4, 2, TOK], R + 60)
        gqT = at("gqT", [P, 2, TOK], R + 60)
        gkT = at("gkT", [P, 2, TOK], R + 62)
        gattn = at("gattn", [P, 2, 4, P], R + 64)
        prob = at("prob", [P, 4, 2, TOK], R + 68)
        gexp = at("gexp", [P, 2, C], R + 68)
        go = at("go", [P, 2, C], R + 72)
        mrows = at("mrows", [P, 2, D], R + 52)
        sq = at("sq", [P, 2, C], 127)
        ffTh = at("ffTh", [P, FFK, TOK], R, F32R)
        ffTl = at("ffTl", [P, FFK, TOK], R + 22, F32R)
        gu = at("gu", [P, 2, 2, C], R + 44)
        fe = at("fe", [P, 2, 2, 256], R + 52)
        RQ = at("RQ", [P, 2, D], R)
        RK = at("RK", [P, 2, D], R + 8)
        RO = at("RO", [P, 2, 4, C], R)
        rqT = at("rqT", [P, 8, TOK], R + 16)
        rkT = at("rkT", [P, 8, TOK], R + 24)
        ryTh = at("ryTh", [P, 16, TOK], R + 16, F32R)
        RV = at("RV", [P, 4, 2, C], R + 32)
        ryTl = at("ryTl", [P, 16, TOK], R + 32, F32R)
        RG = at("RG", [P, 4, 2, C], R + 48)
        rtab = at("rtab", [P, 2, 2, 256], R + 64)
        rscT = at("rscT", [P, 4, 384], R + 64)
        rdm = at("rdm", [P, 4, 384], R + 70)
        rtmp = at("rtmp", [P, 2, C], 127)
        rge = at("rge", [P, 2, C], 127)
        hTh = at("hTh", [P, MLPK, TOK], R, F32R)
        hTl = at("hTl", [P, MLPK, TOK], R + 32, F32R)
        hrow = at("hrow", [P, 2, 2, C], R + 64)
        junk = at("junk", [P, D], R + 72)
        junk2 = at("junk2", [P, D], R + 44)
        yg = at("yg", [P, 2, D], R + 64)
        ygr = at("ygr", [P, 2, D], R + 48)
        BQ = at("BQ", [P, 2, 2, C], R)
        BK = at("BK", [P, 2, 2, C], R + 8)
        byTh = at("byTh", [P, 8, TOK], R, F32R)
        byTl = at("byTl", [P, 8, TOK], R + 8, F32R)
        BV = at("BV", [P, 2, 2, C], R + 16)
        bqT = at("bqT", [P, 8, TOK], R + 24)
        bkT = at("bkT", [P, 8, TOK], R + 32)
        bprob = at("bprob", [P, 4, 2, TOK], R + 40)
        bprob2 = at("bprob2", [P, 4, 2, TOK], R + 48)
        bpT = at("bpT", [P, 4, 2, TOK], R + 56)
        btab = at("btab", [P, 2, 2, 16], R + 64)
        btmp = at("btmp", [P, 4, 2, 4, 16], R + 65)

        ps = [ctx.enter_context(nc.psum_tensor(f"ps{i}", [P, C], F32)) for i in range(4)]
        aux = [ctx.enter_context(nc.psum_tensor(f"aux{i}", [P, C], F32)) for i in range(4)]

        def K(name, a=0, b=None):
            o, w = CONST[name]
            return cst[:, o + a:o + (w if b is None else b)]

        def gcol(name, k=0):
            o, _ = GAIN_COLS[name]
            return gains[:, o + k:o + k + 1]

        def S(name, a=0, b=None):
            o, w = SCAL[name]
            return sc[:, o + a:o + (w if b is None else b)]

        ident = K("ident")

        sems = {}

        def sem(name):
            if name not in sems:
                sems[name] = ctx.enter_context(nc.semaphore(name))
            return sems[name]

        landed = [sem(f"landed{i}") for i in range(RING)]
        hi_ready = sem("hi_ready")
        lo_ready = sem("lo_ready")
        gran_used = sem("gran_used")
        half_done = sem("half_done")
        drained = {"act": sem("drained_act"), "dve": sem("drained_dve")}
        aux_ready = [sem(f"aux_ready{i}") for i in range(4)]
        aux_free = [sem(f"aux_free{i}") for i in range(4)]

        x_rows = x_in.rearrange("(t p) d -> p t d", p=P)
        out_rows = out.rearrange("(t p) d -> p t d", p=P)
        mem_rows = mem_in.rearrange("(t p) d -> p t d", p=P)

        block = ctx.enter_context(nc.Block())

        def wait_unit(eng, name, t):
            if t == 0:
                eng.wait_ge(half_done, U[name] + 1)
            else:
                eng.wait_ge(gran_used, GEND[name])

        def wait_drained(eng, name, t):
            by, n = DRAIN[name]
            eng.wait_ge(drained[by], n + t + 1)

        def bank(name, t):
            return ps[2 * (U[name] % 2) + t][:, :]

        def wait_aux(eng, name, b=0):
            k, n = AUX[(name, b)]
            eng.wait_ge(aux_ready[k], n)
            return aux[k]

        def wait_read(eng, name, b=0):
            k, n = AUX[(name, b)]
            eng.wait_ge(aux_free[k], n)

        def free(ins, name, b=0):
            return ins.then_inc(aux_free[AUX[(name, b)][0]], 1)

        @block.sync
        def _(sp):
            sp.dma_start(mrows[:, :, :], mem_rows).then_inc(sem("mem_in"), 16)
            sp.dma_start(raw[:, 0, :, :], wstream[0]).then_inc(landed[0], 16)
            sp.dma_start(x[:, :, :], x_rows).then_inc(sem("x_in"), 16)
            for g in range(1, RING):
                sp.dma_start(raw[:, g, :, :], wstream[g]).then_inc(landed[g], 16)
            by_ring = wstream[0:NG // RING * RING].rearrange("(i j) p k c -> i j p k c", j=RING)
            with sp.Fori(1, NG // RING) as i:
                for j in range(RING):
                    sp.wait_ge(lo_ready, i * RING + (j + 1 - RING))
                    sp.dma_start(raw[:, j, :, :], by_ring[i, j]).then_inc(landed[j], 16)
            for g in range(NG // RING * RING, NG):
                sp.wait_ge(lo_ready, g + 1 - RING)
                sp.dma_start(raw[:, g % RING, :, :], wstream[g]).then_inc(landed[g % RING], 16)
            for t in range(2):
                sp.wait_ge(sem("x6_rows"), 2 * t + 2)
                sp.dma_start(out_rows[:, t, :], x[:, t, :]).then_inc(sem("out_done"), 16)
            sp.wait_ge(sem("out_done"), 32)

        @block.gpsimd
        def _(pool):
            def power(key, n):
                pool.wait_ge(sem(f"{key}_var"), 1)
                nc.gpsimd.tensor_tensor(S(f"{key}_rstd", 0, n), S(f"{key}_var", 0, n),
                                        K("minus_half").broadcast_to([P, n]), ALU.pow).then_inc(sem(f"{key}_rstd"), 1)

            def per_head(rows):
                return rows[:, :, :].rearrange("p t (h d) -> p (t h) d", d=HD)

            def times_head(rows, key):
                pool.wait_ge(sem(f"{key}_rstd"), 1)
                v = per_head(rows)
                return nc.gpsimd.tensor_tensor(v, v, S(f"{key}_rstd").unsqueeze(2).broadcast_to([P, 8, HD]), ALU.mult)

            def head_norm(key, unit, rows, before):
                wait_drained(pool, unit, 1)
                if before:
                    pool.wait_ge(sem(before), 1)
                nc.gpsimd.tensor_tensor(sq[:, :, :], rows[:, :, :], rows[:, :, :], ALU.mult).then_inc(sem(f"{key}_sq"), 1)
                power(key, 8)
                times_head(rows, key).then_inc(sem(f"{key}_unit"), 1)

            pool.dma_start(cst[:, :], cpack).then_inc(sem("cst_in"), 16)
            pool.dma_start(gains[:, :], gpack).then_inc(sem("gains_in"), 16)
            pool.dma_start(wsm[:, :, :], wsmall).then_inc(sem("wsm_in"), 16)
            pool.dma_start(wa2[:, :], w_a2).then_inc(sem("small_in"), 16)
            pool.dma_start(brow[:, :], b_a).then_inc(sem("small_in"), 16)
            pool.dma_start(S("b_fox"), b_fox.broadcast_to([P, 4])).then_inc(sem("b_fox_in"), 16)
            pool.wait_ge(sem("cst_in"), 16)
            power("mem", 2)
            power("x0", 2)
            head_norm("mk", "mk", MK, None)
            head_norm("mq", "mq", MQ, "mk_var")
            wait_drained(pool, "gqk", 1)
            wait_read(pool, "cum")
            wait_read(pool, "suf")
            for e in range(3):
                nc.gpsimd.tensor_tensor(gla_e[:, 1 + e, :, :], gla_e[:, 1 + e, :, :],
                                        GQK[:, :, 0:256] if e == 0 else GQK[:, :, 256:512],
                                        ALU.mult).then_inc(sem("gla_in"), 1)
            pool.wait_ge(sem("gg_rec"), 1)
            wait_drained(pool, "gg", 1)
            nc.gpsimd.tensor_tensor(GG[:, :, :], GG[:, :, :], gexp[:, :, :], ALU.mult).then_inc(sem("gg_silu"), 1)
            for t in range(2):
                wait_read(pool, "o", t)
            pool.wait_ge(sem("mq_var"), 1)
            nc.gpsimd.tensor_tensor(sq[:, :, :], go[:, :, :], go[:, :, :], ALU.mult).then_inc(sem("go_sq"), 1)
            power("go", 8)
            pool.wait_ge(sem("gg_silu"), 1)
            nc.gpsimd.tensor_tensor(go[:, :, :], go[:, :, :], GG[:, :, :], ALU.mult).then_inc(sem("go_gated"), 1)
            pool.wait_ge(sem("go_gated"), 1)
            times_head(go, "go").then_inc(sem("go_unit"), 1)
            head_norm("fq", "fq", FQ, "go_var")
            head_norm("fk", "fk", FK, "fq_var")
            pool.wait_ge(sem("fk_var"), 1)
            for n in range(2):
                for q, b in enumerate(BRANCHES):
                    k = 3 * n + q
                    if k >= 2:
                        wait_drained(pool, GATES[k - 2], 1)
                    c0 = BRANCH_ROW[b] * D + n * C
                    pool.dma_start(grow[:, (k % 2) * C:(k % 2 + 1) * C], b_gate[:, c0:c0 + C].broadcast_to([P, C]))\
                        .then_inc(sem(f"bias{k % 2}"), 16)
            power("x1", 2)

            def swiglu(n, count):
                pool.wait_ge(drained["act"], 2 * count + (DRAIN["ffn0"][1] + 2))
                gup = gu[:, n % 2, :, 0:256]
                nc.gpsimd.tensor_tensor(gup, gup, gu[:, n % 2, :, 256:512], ALU.mult).then_inc(sem("ff_prod"), 1)
                pool.wait_ge(sem("ff_prod"), count + 1)
                pool.wait_ge(sem("ff_rec"), count + 1)
                nc.gpsimd.tensor_tensor(gup, gup, fe[:, n % 2, :, :], ALU.mult).then_inc(sem("ff_h"), 1)

            swiglu(0, 0)
            with pool.Fori(0, 5) as i:
                for n in (1, 2):
                    swiglu(n, i * 2 + n)
            power("x2", 2)
            pool.wait_ge(gran_used, G["ret0"])
            pool.dma_start(rtab[:, :, :, :], rett).then_inc(sem("rtab_in"), 16)
            pool.dma_start(rdm[:, :, :], dmask).then_inc(sem("rdm_in"), 16)
            for h in range(4):
                wait_drained(pool, f"ret{8 + h}", 1)
                pool.wait_ge(sem("rg_rec"), h + 1)
                nc.gpsimd.tensor_tensor(RG[:, h, :, :], RG[:, h, :, :], rge[:, :, :], ALU.mult).then_inc(sem("rg_silu"), 1)
                if h == 0:
                    power("ro", 8)
            pool.wait_ge(sem("rg_silu"), 4)
            pool.dma_start(grow[:, :], post[0:1, :].broadcast_to([P, D])).then_inc(sem("post_in"), 16)

            def after_mix(p, xk, nxt):
                for t in range(2):
                    pool.wait_ge(sem(f"{p}_var"), t + 1)
                    nc.gpsimd.tensor_tensor(S(f"{p}_rstd", t, t + 1), S(f"{p}_var", t, t + 1),
                                            K("minus_half"), ALU.pow).then_inc(sem(f"{p}_rstd"), 1)
                if nxt is not None:
                    pool.wait_ge(drained["dve"], nxt[1])
                    pool.dma_start(grow[:, :], post[nxt[0]:nxt[0] + 1, :].broadcast_to([P, D])).then_inc(sem("post_in"), 16)
                    power(xk, 2)

            def squares(m):
                def one(n, count):
                    pool.wait_ge(drained["act"], 2 * count + (DRAIN[f"up{m}_0"][1] + 2))
                    h = hrow[:, n % 2, :, :]
                    nc.gpsimd.tensor_tensor(h, h, h, ALU.mult).then_inc(sem(f"h{m}_rows"), 1)
                one(0, 0)
                one(1, 1)
                with pool.Fori(1, 4) as i:
                    for n in range(2):
                        one(n, i * 2 + n)

            after_mix("p2", "x3", (1, DRAIN["reto1"][1] + 2))
            squares(0)
            after_mix("p3", "x4", (2, DRAIN["down0_1"][1] + 2))
            pool.wait_ge(gran_used, G["moba0"])
            pool.dma_start(btab[:, :, :, :], mobat).then_inc(sem("btab_in"), 16)
            pool.wait_ge(sem("btab_in"), 16)

            def rope(k, unit, rows, key):
                wait_drained(pool, unit, 1)
                v = rows.rearrange("p t (h d) -> p t h d", d=HD)
                halves = v[:, :, :, 0:16], v[:, :, :, 16:32]
                cos, sin = (btab[:, :, f, :].unsqueeze(2).broadcast_to([P, 2, 4, 16]) for f in range(2))
                for m, (half, f) in enumerate(((0, cos), (1, sin), (1, cos), (0, sin))):
                    nc.gpsimd.tensor_tensor(btmp[:, m, :, :, :], halves[half], f, ALU.mult).then_inc(sem("rope_part"), 1)
                pool.wait_ge(sem("rope_part"), 4 * k + 4)
                nc.gpsimd.tensor_tensor(halves[0], btmp[:, 0, :, :, :], btmp[:, 1, :, :, :], ALU.subtract).then_inc(sem("rope_half"), 1)
                nc.gpsimd.tensor_tensor(halves[1], btmp[:, 2, :, :, :], btmp[:, 3, :, :, :], ALU.add).then_inc(sem(key), 1)
                pool.wait_ge(sem("rope_half"), k + 1)
                pool.wait_ge(sem(key), k // 2 + 1)

            for j in range(2):
                rope(2 * j, f"moba{2 * j}", BQ[:, j, :, :], "bq_rot")
                rope(2 * j + 1, f"moba{2 * j + 1}", BK[:, j, :, :], "bk_rot")
            after_mix("p4", "x5", (3, DRAIN["mobao1"][1] + 2))
            squares(1)
            after_mix("p5", None, None)

        @block.tensor
        def _(pe):
            def granule(slot, lo_value, th, tl, kts, pair, first, last, read_out):
                pe.wait_ge(lo_ready, lo_value)
                for t in range(2):
                    if first and read_out is not None:
                        pe.wait_ge(read_out[0], read_out[1] + t)
                    for j, kt in enumerate(kts):
                        for q, (a, w) in enumerate(((th, Wh), (th, Wl), (tl, Wh))):
                            mm = nc.tensor.matmul(ps[2 * pair + t][:, :], a[:, kt, t * P:(t + 1) * P], w[:, slot, j, :],
                                                  start=(first and j == 0 and q == 0),
                                                  stop=(last and j == len(kts) - 1 and q == 2))
                    if t == 0 and last:
                        mm.then_inc(half_done, 1)
                mm.then_inc(gran_used, 1)

            def product(name, operand, kt0=0, before=None):
                th, tl = operand
                g0, kt = G[name], kt0
                read_out = None
                if U[name] >= 2:
                    by, n = DRAIN[UNITS[U[name] - 2]]
                    read_out = (drained[by], n + 1)
                for g in range(g0, GEND[name]):
                    if before and g - g0 in before:
                        before[g - g0]()
                    granule(g % RING, g + 1, th, tl, range(kt, kt + KTS[g]), U[name] % 2, g == g0, g == GEND[name] - 1, read_out)
                    kt += KTS[g]

            def open_aux(name, b=0):
                k, n = AUX[(name, b)]
                if n > 1:
                    pe.wait_ge(aux_free[k], n - 1)
                return aux[k]

            def done(ins, name, b=0):
                ins.then_inc(aux_ready[AUX[(name, b)][0]], 1)

            def turn(name, b, blocks):
                o = open_aux(name, b)
                for at, src in blocks:
                    tr = nc.tensor.transpose(o[0:src.shape[1], at:at + P], src, ident)
                done(tr, name, b)

            def turn_rows(name, rows, b):
                turn(name, b, [(kk * TOK + t * P, rows[:, t, (2 * b + kk) * P:(2 * b + kk + 1) * P])
                               for kk in range(2) for t in range(2)])

            def wait_operand(name, banks):
                for b in banks:
                    wait_read(pe, name, b)

            pe.wait_ge(sem("cst_in"), 16)
            pe.wait_ge(sem("mem_in"), 16)
            for b in range(4):
                turn_rows("memT", mrows, b)
            pe.wait_ge(sem("x_in"), 16)
            for b in range(4):
                turn_rows("xT", x, b)
            wait_operand("memT", range(4))
            product("mk", (memTh, memTl))
            wait_operand("xT", range(4))
            pe.wait_ge(sem("wsm_lo"), 1)
            o = open_aux("small")
            for t in range(2):
                for k in range(DK):
                    for q, (a, w) in enumerate(((xTh, wsmh), (xTh, wsml), (xTl, wsmh))):
                        mm = nc.tensor.matmul(o[:, 32 * t:32 * t + 20], a[:, k, t * P:(t + 1) * P], w[:, k, :],
                                              start=(k == 0 and q == 0), stop=(k == DK - 1 and q == 2))
            done(mm, "small")
            product("mv", (memTh, memTl))
            pe.wait_ge(sem("ga_rows"), 2)
            turn("gaT", 0, [(t * P, S("ga", 16 * t, 16 * t + 16)) for t in range(2)])
            pe.wait_ge(sem("mk_unit"), 1)
            for b in range(2):
                turn_rows("mkT", MK, b)
            product("mq", (xTh, xTl))
            wait_read(pe, "gaT")
            pe.wait_ge(sem("small_in"), 32)
            o = open_aux("z")
            for t in range(2):
                nc.tensor.matmul(o[:, t * 256:(t + 1) * 256], gaT[:, t * P:(t + 1) * P], wa2[:, :], start=True, stop=False)
                mm = nc.tensor.matmul(o[:, t * 256:(t + 1) * 256], K("ones")[0:1, :], brow[:, :], start=False, stop=True)
            done(mm, "z")
            pe.wait_ge(sem("lf"), 2)
            o = open_aux("foxcum")
            nc.tensor.matmul(o[:, 0:4], K("upto"), S("lf", 0, 4), start=True, stop=True)
            nc.tensor.matmul(o[:, 4:8], K("upto"), S("lf", 4, 8), start=True, stop=False)
            mm = nc.tensor.matmul(o[:, 4:8], K("ones"), S("lf", 0, 4), start=False, stop=True)
            done(mm, "foxcum")
            product("gqk", (xTh, xTl))
            wait_read(pe, "z")
            for name, mat in (("cum", "chunk_upto"), ("suf", "chunk_after")):
                o = open_aux(name)
                for t in range(2):
                    mm = nc.tensor.matmul(o[:, t * 256:(t + 1) * 256], K(mat), gla_e[:, 0, t, :], start=True, stop=True)
                done(mm, name)
            o = open_aux("dec")
            for pr in range(2):
                for t in range(2):
                    mm = nc.tensor.matmul(o[:, 4 * pr + 2 * t:4 * pr + 2 * t + 2], gla_e[:, 0, t, pr * P:(pr + 1) * P],
                                          K("half"), start=True, stop=True)
            done(mm, "dec")
            pe.wait_ge(sem("mq_unit"), 1)
            for b in range(2):
                turn_rows("mqT", MQ, b)
            product("gv", (xTh, xTl))
            for name, e in (("gqT", 1), ("gkT", 2)):
                pe.wait_ge(sem("gla_in"), e)
                turn_rows(name, gla_e[:, e, :, :], 0)
            product("gg", (xTh, xTl))
            wait_read(pe, "gqT")
            wait_read(pe, "gkT")
            for odd in range(2):
                o = open_aux("attn", odd)
                r = 64 * odd
                for t in range(2):
                    for pr in range(2):
                        at0 = (2 * t + pr) * P
                        mm = nc.tensor.matmul(o[:, at0:at0 + P], gkT[r:r + 64, pr, t * P:(t + 1) * P],
                                              gqT[r:r + 64, pr, t * P:(t + 1) * P], start=True, stop=True)
                done(mm, "attn", odd)
            pe.wait_ge(sem("gla_in"), 3)
            wait_drained(pe, "gv", 1)
            for b, chunks in enumerate(((0, 2), (1,))):
                o = open_aux("cs", b)
                for c in chunks:
                    t, s0 = c // 2, 64 * (c % 2)
                    for h in range(4):
                        r, pr = 64 * (h % 2), h // 2
                        at0 = (c // 2) * 256 + pr * P
                        mm = nc.tensor.matmul(o[r:r + 64, at0:at0 + P], gla_e[s0:s0 + 64, 3, t, 64 * h:64 * h + 64],
                                              GV[s0:s0 + 64, t, h * P:(h + 1) * P], start=True, stop=True)
                done(mm, "cs", b)
            product("fq", (xTh, xTl))
            wait_read(pe, "cs", 0)
            for odd in range(2):
                wait_read(pe, "attn", odd)
                o = open_aux("o", odd)
                r = 64 * odd
                for t in range(2):
                    for pr in range(2):
                        h, at0 = 2 * pr + odd, (2 * t + pr) * P
                        nc.tensor.matmul(o[:, at0:at0 + P], gattn[:, odd, 2 * t + pr, :], GV[:, t, h * P:(h + 1) * P],
                                         start=True, stop=False, skip_group_check=True)
                        for half in range(2):
                            c = 2 * t + half
                            if c:
                                i0 = t * P + 64 * half
                                mm = nc.tensor.matmul(o[64 * half:64 * half + 64, at0:at0 + P], gqT[r:r + 64, pr, i0:i0 + 64],
                                                      state[r:r + 64, c - 1, pr, :], start=False, stop=(half == 1),
                                                      skip_group_check=True)
                done(mm, "o", odd)
            product("fk", (xTh, xTl))
            pe.wait_ge(sem("go_unit"), 1)
            for b in range(2):
                turn_rows("gyT", go, b)

            def scores(name, h, qT, kT, h0=0):
                o = open_aux(name, h + h0)
                for t in range(2):
                    mm = nc.tensor.matmul(o[:, t * TOK:(t + 1) * TOK], qT[:, h + h0, t * P:(t + 1) * P], kT[:, h + h0, :],
                                          start=True, stop=True)
                done(mm, name, h + h0)

            def turn_probs(name, h, pr, key, causal=False):
                pe.wait_ge(sem(key), 2 * h + 2)
                turn(name, h, [(ks * TOK + t * P, pr[:, h % 4, t, ks * P:(ks + 1) * P])
                               for ks in range(2) for t in range(2) if not (causal and ks > t)])

            def attend(name, h, v, pT, causal=False):
                o = open_aux(name, h)
                for ks in range(2):
                    q0 = P if causal and ks else 0
                    mm = nc.tensor.matmul(o[:, q0:TOK], v(ks), pT[:, h % 4, ks, q0:TOK], start=(ks == 0), stop=(ks == 1))
                done(mm, name, h)

            wait_operand("mkT", range(2))
            wait_operand("mqT", range(2))
            for h in range(4):
                scores("msc", h, mqT, mkT)
            product("fv", (xTh, xTl))
            for h in range(4):
                turn_probs("mpT", h, prob, "m_prob")
            product("gate_mem0", (xTh, xTl))
            wait_drained(pe, "mv", 1)
            for h in range(4):
                wait_read(pe, "mpT", h)
                attend("moT", h, lambda ks: MV[:, ks, h * HD:(h + 1) * HD], mpT)
            pe.wait_ge(sem("fq_unit"), 1)
            for b in range(2):
                turn_rows("fqT", FQ, b)
            pe.wait_ge(sem("fk_unit"), 1)
            for b in range(2):
                turn_rows("fkT", FK, b)
            product("gate_gla0", (xTh, xTl))
            wait_operand("fqT", range(2))
            wait_operand("fkT", range(2))
            pe.wait_ge(sem("nlf"), 1)
            triangle_and_ones = cst[:, CONST["upto"][0]:CONST["upto"][0] + 2 * P]
            for h in range(4):
                o = open_aux("fsc", h)
                lf0 = S("nlf", h, h + 1).broadcast_to([P, P])
                lf1 = S("nlf", 4 + h, 5 + h).broadcast_to([P, P])
                nc.tensor.matmul(o[:, 0:P], fqT[:, h, 0:P], fkT[:, h, 0:P], start=True, stop=False)
                nc.tensor.matmul(o[:, 0:P], lf0, K("upto"), start=False, stop=True)
                nc.tensor.matmul(o[:, TOK:2 * TOK], fqT[:, h, P:TOK], fkT[:, h, :], start=True, stop=False)
                nc.tensor.matmul(o[:, TOK:2 * TOK], lf0, triangle_and_ones, start=False, stop=False)
                mm = nc.tensor.matmul(o[:, TOK + P:2 * TOK], lf1, K("upto"), start=False, stop=True)
                done(mm, "fsc", h)
            product("gate_fox0", (xTh, xTl))
            for h in range(4):
                turn_probs("fpT", h, prob, "f_prob", causal=True)
            wait_operand("moT", range(4))
            product("branch_mem0", yT["mem"])
            wait_drained(pe, "fv", 1)
            for h in range(4):
                wait_read(pe, "fpT", h)
                attend("foT", h, lambda ks: FV[:, ks, h * HD:(h + 1) * HD], fpT, causal=True)
            wait_operand("gyT", range(2))
            product("branch_gla0", yT["gla"])
            wait_operand("foT", range(4))
            product("branch_fox0", yT["fox"])
            for b in BRANCHES:
                product(f"gate_{b}1", (xTh, xTl))
            for b in BRANCHES:
                product(f"branch_{b}1", yT[b])

            def turn_all(name, rows, ready):
                for b in range(4):
                    ready(b // 2)
                    turn_rows(name, rows, b)

            def rows_ready(name):
                def wait(half):
                    pe.wait_ge(sem(f"{name}_rows"), 3 + half)
                return wait

            def merged_ready(half):
                pe.wait_ge(sem("merged"), 4 * (half + 1))

            turn_all("mgT", merged, merged_ready)

            def by_half(name):
                return {0: lambda: wait_operand(name, (0, 1)), 1: lambda: wait_operand(name, (2, 3))}

            for n in range(2):
                product(f"wout{n}", (xTh, xTl), before=by_half("mgT"))

            def by_unit(name):
                return lambda half: wait_drained(pe, f"{name}{half}", 1)

            turn_all("x1T", x, by_unit("wout"))

            def ff_unit(n, i=None):
                name = f"ffn{n}"
                by, d = DRAIN[UNITS[U[name] - 2]]
                if i is not None:
                    by, d = "act", DRAIN[name][1] - 4
                for q in range(2):
                    g = G[name] + q
                    gv, dv = (g + 1, d + 1) if i is None else (i * 4 + (g + 1), i * 4 + (d + 1))
                    granule(g % RING, gv, xTh, xTl, range(4 * q, 4 * q + 4), U[name] % 2, q == 0, q == 1,
                            (drained[by], dv))

            def ff_turned(n, i=None):
                pe.wait_ge(sem("ff_h"), n + 1 if i is None else i * 2 + (n + 1))
                k, use = AUX[(f"ffT{n}", 0)]
                pe.wait_ge(aux_free[k], use - 1 if i is None else i + (use - 1))
                for kk in range(2):
                    for t in range(2):
                        tr = nc.tensor.transpose(aux[k][:, kk * TOK + t * P:kk * TOK + (t + 1) * P],
                                                 gu[:, n % 2, t, kk * P:(kk + 1) * P], ident)
                tr.then_inc(aux_ready[k], 1)

            product("ffn0", (xTh, xTl), before=by_half("x1T"))
            ff_unit(1)
            ff_turned(0)
            ff_unit(2)
            ff_turned(1)
            with pe.Fori(1, 5) as i:
                for n in (1, 2):
                    ff_unit(n, i)
                    ff_turned(n - 1, i)

            def ff_ready(q):
                def go_on():
                    if q == 1:
                        ff_turned(10)
                    for n in range(2 * q, min(2 * q + 2, FFN // 256)):
                        wait_operand(f"ffT{n}", (0,))
                return go_on

            product("ffd0", (ffTh, ffTl), before={q: ff_ready(q) for q in range(6)})
            product("ffd1", (ffTh, ffTl))
            turn_all("x2T", x, by_unit("ffd"))
            product("ret0", (xTh, xTl), before=by_half("x2T"))
            product("ret1", (xTh, xTl))
            product("ret2", (xTh, xTl))

            def turn_rot(name, rows, key, j):
                pe.wait_ge(sem(key), j + 1)
                for b in range(2):
                    turn(f"{name}{j}", b, [(kk * TOK + t * P, rows[:, t, j * C + (2 * b + kk) * P:j * C + (2 * b + kk + 1) * P])
                                           for kk in range(2) for t in range(2)])

            turn_rot("rqT", RQ, "rq_rot", 0)
            product("ret3", (xTh, xTl))
            turn_rot("rqT", RQ, "rq_rot", 1)
            product("ret4", (xTh, xTl))
            turn_rot("rkT", RK, "rk_rot", 0)
            product("ret5", (xTh, xTl))
            turn_rot("rkT", RK, "rk_rot", 1)
            product("ret6", (xTh, xTl))
            for j in range(2):
                wait_operand(f"rqT{j}", range(2))
                wait_operand(f"rkT{j}", range(2))
            for h in range(4):
                o = open_aux("rsc", h)
                for j, (q0, at0) in enumerate(((0, 0), (P, TOK))):
                    for kk in range(2):
                        mm = nc.tensor.matmul(o[:, at0:at0 + TOK - q0], rkT[:, 2 * h + kk, j * P:(j + 1) * P],
                                              rqT[:, 2 * h + kk, q0:TOK], start=(kk == 0), stop=(kk == 1))
                done(mm, "rsc", h)
            product("ret7", (xTh, xTl))

            def ret_out(h):
                wait_drained(pe, f"ret{4 + h}", 1)
                wait_read(pe, "rsc", h)
                for t in range(2):
                    o = open_aux(f"ro{h}", t)
                    if t == 0:
                        mm = nc.tensor.matmul(o[:, :], rscT[:, h, 0:P], RV[:, h, 0, :], start=True, stop=True)
                    else:
                        nc.tensor.matmul(o[:, :], rscT[:, h, P:TOK], RV[:, h, 0, :], start=True, stop=False)
                        mm = nc.tensor.matmul(o[:, :], rscT[:, h, TOK:384], RV[:, h, 1, :], start=False, stop=True)
                    done(mm, f"ro{h}", t)

            ret_out(0)
            ret_out(1)
            product("ret8", (xTh, xTl))
            ret_out(2)
            ret_out(3)
            product("ret9", (xTh, xTl))
            product("ret10", (xTh, xTl))

            def turn_ret(h):
                pe.wait_ge(sem("ry_rows"), 2 * h + 2)
                for b in range(2):
                    turn(f"ryT{h}", b, [(kk * TOK + t * P, RO[:, t, h, (2 * b + kk) * P:(2 * b + kk + 1) * P])
                                        for kk in range(2) for t in range(2)])

            turn_ret(0)
            product("ret11", (xTh, xTl))
            turn_ret(1)

            def ret_half0(h):
                def go_on():
                    if 1 <= h < 3:
                        turn_ret(h + 1)
                    wait_operand(f"ryT{h}", range(2))
                return go_on

            product("reto0", (ryTh, ryTl), before={h: ret_half0(h) for h in range(4)})
            product("reto1", (ryTh, ryTl))

            def mlp(m, xname):
                turn_all(f"{xname}T", x, rows_ready(xname))
                product(f"up{m}_0", (xTh, xTl), before=by_half(f"{xname}T"))

                def up(n, i=None):
                    name = f"up{m}_{n}"
                    prev = DRAIN[UNITS[U[name] - 2]]
                    for q in range(2):
                        g = G[name] + q
                        gv, dv = (g + 1, prev[1] + 1) if i is None else (i * 4 + (g + 1), i * 4 + (DRAIN[name][1] - 3))
                        granule(g % RING, gv, xTh, xTl, range(4 * q, 4 * q + 4), U[name] % 2, q == 0, q == 1,
                                (drained[prev[0]] if i is None else drained["act"], dv))

                def turned(n, i=None):
                    pe.wait_ge(sem(f"h{m}_rows"), n + 1 if i is None else i * 2 + (n + 1))
                    for b in range(2):
                        k, use = AUX[(f"h{m}T{n % 2}", b)]
                        base = use - 1 + (n - n % 2) // 2
                        pe.wait_ge(aux_free[k], base if i is None else i + base)
                        for kk in range(2):
                            for t in range(2):
                                c0 = (2 * b + kk) * P
                                tr = nc.tensor.transpose(aux[k][:, kk * TOK + t * P:kk * TOK + (t + 1) * P],
                                                         hrow[:, n % 2, t, c0:c0 + P], ident)
                        tr.then_inc(aux_ready[k], 1)

                up(1)
                turned(0)
                with pe.Fori(1, 4) as i:
                    up(0, i)
                    turned(-1, i)
                    up(1, i)
                    turned(0, i)

                def before(q):
                    def go_on():
                        if q == 1:
                            turned(7)
                        wait_operand(f"h{m}T{q}", range(2))
                    return go_on

                product(f"down{m}_0", (hTh, hTl), before={q: before(q) for q in range(8)})
                product(f"down{m}_1", (hTh, hTl))

            mlp(0, "x3")
            turn_all("x4T", x, rows_ready("x4"))
            product("moba0", (xTh, xTl), before=by_half("x4T"))
            product("moba1", (xTh, xTl))
            product("moba2", (xTh, xTl))

            def turn_moba(name, rows, key, j):
                pe.wait_ge(sem(key), j + 1)
                for b in range(2):
                    turn_rows(f"{name}{j}", rows[:, j, :, :], b)

            turn_moba("bqT", BQ, "bq_rot", 0)
            turn_moba("bkT", BK, "bk_rot", 0)
            product("moba3", (xTh, xTl))
            wait_operand("bqT0", range(2))
            wait_operand("bkT0", range(2))
            for h in range(4):
                scores("bsc", h, bqT, bkT)
            product("moba4", (xTh, xTl))
            turn_moba("bqT", BQ, "bq_rot", 1)
            turn_moba("bkT", BK, "bk_rot", 1)
            for h in range(4):
                turn_probs("bpT", h, bprob, "b_prob")
            product("moba5", (xTh, xTl))

            def moba_out(h):
                wait_read(pe, "bpT", h)
                attend("boT", h, lambda ks: BV[:, h // 4, ks, (h % 4) * HD:(h % 4 + 1) * HD], bpT)

            wait_drained(pe, "moba4", 1)
            for h in range(4):
                moba_out(h)
            wait_operand("bqT1", range(2))
            wait_operand("bkT1", range(2))
            for h in range(4):
                scores("bsc", h, bqT, bkT, 4)

            def second_heads():
                for h in range(4, 8):
                    turn_probs("bpT", h, bprob2, "b_prob")
                wait_drained(pe, "moba5", 1)
                for h in range(4, 8):
                    moba_out(h)
                wait_operand("boT", range(4, 8))

            product("mobao0", (byTh, byTl), before={0: lambda: wait_operand("boT", range(4)), 1: second_heads})
            product("mobao1", (byTh, byTl))
            mlp(1, "x5")

        @block.scalar
        def _(act):
            chain = [0]

            def link(ins):
                chain[0] += 1
                ins.then_inc(sem("act_chain"), 1)
                act.wait_ge(sem("act_chain"), chain[0])

            def split(g, i=None):
                if g >= NG:
                    return
                slot, nk = g % RING, KTS[g]
                land, used = 16 * (g // RING + 1), g + 1 - RING
                act.wait_ge(landed[slot], land if i is None else i * 16 + land)
                if g >= RING:
                    act.wait_ge(gran_used, used if i is None else i * RING + used)
                nc.scalar.activation(Wh[:, slot, 0:nk, :], raw[:, slot, 0:nk, :], ACT.Copy).then_inc(hi_ready, 1)

            def unit(name, read_out=None):
                for g in range(G[name], GEND[name] - 1):
                    split(g + RING)
                if read_out:
                    read_out()
                split(GEND[name] - 1 + RING)

            def rows(name, dst, key):
                def go():
                    act.wait_ge(sem(f"{key}_rstd"), 1)
                    for t in range(2):
                        wait_unit(act, name, t)
                        nc.scalar.activation(dst(t), bank(name, t), ACT.Copy,
                                             scale=S(f"{key}_rstd", t, t + 1)).then_inc(drained["act"], 1)
                return go

            def high(name, b, dst, kts, gain=None):
                o = wait_aux(act, name, b)
                if gain is None:
                    nc.scalar.activation(dst[:, kts[0]:kts[-1] + 1, :], o[:, 0:TOK * len(kts)], ACT.Copy)\
                        .then_inc(sem(f"{name}_hi"), 1)
                    return
                for j, kt in enumerate(kts):
                    nc.scalar.activation(dst[:, kt, :], o[:, j * TOK:(j + 1) * TOK], ACT.Copy,
                                         scale=gcol(gain, kt)).then_inc(sem(f"{name}_hi"), 1)

            squared = []

            def square(scratch, src, total, signal, count):
                if squared:
                    act.wait_ge(*squared.pop())
                nc.scalar.activation(scratch, src, ACT.Square, accum_out=total).then_inc(signal, 1)
                squared.append((signal, count))

            def square_sums(key, rows_of, scratch):
                for t in range(2):
                    square(scratch, rows_of[:, t, :], S(f"{key}_ss", t, t + 1), sem(f"{key}_ss"), t + 1)

            act.wait_ge(sem("gains_in"), 16)
            for b in range(4):
                high("memT", b, memTh, (2 * b, 2 * b + 1), "g_mem")
            split(0)
            split(1)
            for b in range(4):
                high("xT", b, xTh, (2 * b, 2 * b + 1), "g_mix")
            square_sums("mem", mrows, junk[:, :])
            split(2)
            act.wait_ge(sem("wsm_in"), 16)
            nc.scalar.activation(wsmh[:, :, :], wsm[:, :, :], ACT.Copy).then_inc(sem("wsm_hi"), 1)
            split(3)
            square_sums("x0", x, junk[:, :])
            unit("mk", rows("mk", lambda t: MK[:, t, :], "mem"))
            wait_read(act, "small")
            link(nc.scalar.activation(S("ffa"), S("ffz"), ACT.Abs))
            link(nc.scalar.activation(S("ffa"), S("ffa"), ACT.Exp, scale=-1.0))
            nc.scalar.activation(S("ffl"), S("ffa"), ACT.Ln, bias=1.0).then_inc(sem("ffl"), 1)
            unit("mv", rows("mv", lambda t: MV[:, t, :], "mem"))
            o = wait_aux(act, "gaT")
            free(nc.scalar.activation(gaT[:, :], o[0:16, 0:TOK], ACT.Copy), "gaT")
            for b in range(2):
                o = wait_aux(act, "mkT", b)
                free(nc.scalar.activation(mkT[:, 2 * b:2 * b + 2, :], o[:, :], ACT.Copy, scale=gcol("g_mk")), "mkT", b)
            unit("mq", rows("mq", lambda t: MQ[:, t, :], "x0"))
            o = wait_aux(act, "z")
            link(nc.scalar.activation(gla_e[:, 1, :, :], o[:, :], ACT.Abs))
            link(nc.scalar.activation(gla_e[:, 2, :, :], gla_e[:, 1, :, :], ACT.Exp, scale=-1.0))
            nc.scalar.activation(gla_e[:, 3, :, :], gla_e[:, 2, :, :], ACT.Ln, bias=1.0).then_inc(sem("gla_l"), 1)
            unit("gqk", rows("gqk", lambda t: GQK[:, t, :], "x0"))
            tau = 1.0 / 16.0
            o = wait_aux(act, "cum")
            nc.scalar.activation(gla_e[:, 1, :, :], o[:, :], ACT.Exp, scale=tau)
            free(nc.scalar.activation(gla_e[:, 2, :, :], o[:, :], ACT.Exp, scale=-tau), "cum")
            o = wait_aux(act, "suf")
            free(nc.scalar.activation(gla_e[:, 3, :, :], o[:, :], ACT.Exp, scale=tau), "suf")
            o = wait_aux(act, "dec")
            free(nc.scalar.activation(S("dec"), o[:, 0:8], ACT.Exp, scale=tau), "dec")
            act.wait_ge(sem("gmq_s"), 1)
            for b in range(2):
                o = wait_aux(act, "mqT", b)
                free(nc.scalar.activation(mqT[:, 2 * b:2 * b + 2, :], o[:, :], ACT.Copy, scale=S("gmq_s")), "mqT", b)
            unit("gv", rows("gv", lambda t: GV[:, t, :], "x0"))
            o = wait_aux(act, "gqT")
            free(nc.scalar.activation(gqT[:, :, :], o[:, :], ACT.Copy, scale=64.0 ** -0.5), "gqT")

            def gg_rows():
                act.wait_ge(sem("x0_nrstd"), 1)
                for t in range(2):
                    wait_unit(act, "gg", t)
                    nc.scalar.activation(gexp[:, t, :], bank("gg", t), ACT.Exp,
                                         scale=S("x0_nrstd", t, t + 1)).then_inc(sem("gg_exp"), 1)
                    nc.scalar.activation(GG[:, t, :], bank("gg", t), ACT.Copy,
                                         scale=S("x0_rstd", t, t + 1)).then_inc(drained["act"], 1)

            unit("gg", gg_rows)
            unit("fq", rows("fq", lambda t: FQ[:, t, :], "x0"))
            for t in range(2):
                o = wait_aux(act, "o", t)
                by_parity = go[:, :, :].rearrange("p t (r q c) -> p t r q c", r=2, q=2)
                free(nc.scalar.activation(by_parity[:, :, :, t, :], o[:, :].rearrange("p (t r c) -> p t r c", t=2, r=2),
                                          ACT.Copy), "o", t)
            unit("fk", rows("fk", lambda t: FK[:, t, :], "x0"))
            for b in range(2):
                high("gyT", b, yT["gla"][0], (2 * b, 2 * b + 1), "g_gla")

            def exps(k, name, h, pr, src, nm, total):
                act.wait_ge(sem(f"{k}_max"), h + 1)
                for t in range(2):
                    i = nc.scalar.activation(pr[:, h % 4, t, 0:src(t).shape[1]], src(t), ACT.Exp, bias=nm(t), accum_out=total(t))
                    if name == "msc" and t == 1:
                        free(i, name, h)
                    elif name != "msc":
                        i.then_inc(sem(f"{k}_exp"), 1)

            for h in range(4):
                o = aux[AUX[("msc", h)][0]]
                exps("m", "msc", h, prob, lambda t: o[:, t * TOK:(t + 1) * TOK],
                     lambda t: S("ms_nm", 2 * h + t, 2 * h + t + 1), lambda t: S("ms_sum", 2 * h + t, 2 * h + t + 1))
            unit("fv", rows("fv", lambda t: FV[:, t, :], "x0"))

            def probs_T(name, h, dst, causal=False):
                o = wait_aux(act, name, h)
                if causal:
                    nc.scalar.activation(dst[:, h % 4, 0, :], o[:, 0:TOK], ACT.Copy)
                    i = nc.scalar.activation(dst[:, h % 4, 1, P:TOK], o[:, TOK + P:2 * TOK], ACT.Copy)
                else:
                    i = nc.scalar.activation(dst[:, h % 4, :, :], o[:, :], ACT.Copy)
                free(i, name, h)

            for h in (0, 2):
                probs_T("mpT", h, mpT)

            def gate_exp(b, n):
                def go():
                    for t in range(2):
                        wait_drained(act, f"gate_{b}{n}", t)
                        nc.scalar.activation(gate[b][:, t, :], gate[b][:, t, :], ACT.Exp, scale=-1.0).then_inc(sem("gate_exp"), 1)
                return go

            unit("gate_mem0", gate_exp("mem", 0))
            for h in range(4):
                high("moT", h, yT["mem"][0], (h,))
            act.wait_ge(sem("gfq_s"), 1)
            for b in range(2):
                o = wait_aux(act, "fqT", b)
                free(nc.scalar.activation(fqT[:, 2 * b:2 * b + 2, :], o[:, :], ACT.Copy, scale=S("gfq_s")), "fqT", b)
            unit("gate_gla0", gate_exp("gla", 0))
            for h in range(4):
                exps("f", "fsc", h, prob, lambda t: prob[:, h, t, 0:P * (t + 1)],
                     lambda t: S("fs_nm", 2 * h + t, 2 * h + t + 1), lambda t: S("fs_sum", 2 * h + t, 2 * h + t + 1))
            unit("gate_fox0", gate_exp("fox", 0))
            for h in (0, 2):
                probs_T("fpT", h, fpT, causal=True)
            unit("branch_mem0")
            for h in range(4):
                high("foT", h, yT["fox"][0], (h,))
            unit("branch_gla0")
            unit("branch_fox0")
            for b in BRANCHES:
                unit(f"gate_{b}1", gate_exp(b, 1))
            for b in BRANCHES:
                unit(f"branch_{b}1")
            for b in range(4):
                high("mgT", b, xTh, (2 * b, 2 * b + 1))
            unit("wout0")
            unit("wout1")

            def next_norm(k, gain, rows_ready, scratch):
                for b in range(4):
                    high(f"{k}T", b, xTh, (2 * b, 2 * b + 1), gain)
                rows_ready()
                square_sums(k, x, scratch)

            next_norm("x1", "g_ffn", lambda: wait_drained(act, "wout1", 1), junk[:, :])

            def ff(n, i=None):
                name = f"ffn{n}"
                split(G[name] + RING, i)
                count = n if i is None else i * 2 + n
                if n >= 2 or i is not None:
                    act.wait_ge(sem("ff_h"), count - 1)
                for t in range(2):
                    if t == 0:
                        act.wait_ge(half_done, count + (U["ffn0"] + 1))
                    else:
                        act.wait_ge(gran_used, GEND[name] if i is None else i * RING + GEND[name])
                    o = bank(name, t)
                    nc.scalar.activation(fe[:, n % 2, t, :], o[:, 0:256], ACT.Exp,
                                         scale=S("x1_nrstd", t, t + 1)).then_inc(sem("ff_exp"), 1)
                    nc.scalar.activation(gu[:, n % 2, t, :], o[:, :], ACT.Copy,
                                         scale=S("x1_rstd", t, t + 1)).then_inc(drained["act"], 1)
                split(GEND[name] - 1 + RING, i)

            def ff_high(n, i=None):
                k, use = AUX[(f"ffT{n}", 0)]
                act.wait_ge(aux_ready[k], use if i is None else i + use)
                dst = ffTh[:, :, :].rearrange("p (n k) t -> p n k t", k=2)
                nc.scalar.activation(dst[:, n if i is None else i * 2 + n, :, :], aux[k][:, :], ACT.Copy)\
                    .then_inc(sem("ffT_hi"), 1)

            act.wait_ge(sem("x1_nrstd"), 1)
            ff(0)
            ff(1)
            ff_high(0)
            ff(2)
            ff_high(1)
            with act.Fori(1, 5) as i:
                for n in (1, 2):
                    ff(n, i)
                    ff_high(n - 1, i)
            split(G["ffd0"] + RING)
            ff_high(10)
            for g in range(G["ffd0"] + 1, GEND["ffd0"]):
                split(g + RING)
            unit("ffd1")
            next_norm("x2", "pre0", lambda: wait_drained(act, "ffd1", 1), junk2[:, :])
            for j in range(2):
                unit(f"ret{j}", rows(f"ret{j}", lambda t: RQ[:, t, j * C:(j + 1) * C], "x2"))
            unit("ret2", rows("ret2", lambda t: RK[:, t, 0:C], "x2"))

            def rq_turned(j):
                for b in range(2):
                    o = wait_aux(act, f"rqT{j}", b)
                    nc.scalar.activation(rqT[:, 4 * j + 2 * b:4 * j + 2 * b + 2, :], o[:, :], ACT.Copy)\
                        .then_inc(aux_free[AUX[(f"rqT{j}", b)][0]], 1)

            rq_turned(0)
            unit("ret3", rows("ret3", lambda t: RK[:, t, C:D], "x2"))
            rq_turned(1)
            for h in range(4):
                unit(f"ret{4 + h}", rows(f"ret{4 + h}", lambda t: RV[:, h, t, :], "x2"))

            def gate_rows(h):
                def go():
                    act.wait_ge(sem("rk_rot"), 2)
                    if h:
                        act.wait_ge(sem("rg_silu"), h)
                    for t in range(2):
                        wait_unit(act, f"ret{8 + h}", t)
                        o = bank(f"ret{8 + h}", t)
                        nc.scalar.activation(rge[:, t, :], o[:, :], ACT.Exp,
                                             scale=S("x2_nrstd", t, t + 1)).then_inc(sem("rg_exp"), 1)
                        nc.scalar.activation(RG[:, h, t, :], o[:, :], ACT.Copy,
                                             scale=S("x2_rstd", t, t + 1)).then_inc(drained["act"], 1)
                return go

            def ret_rows(h):
                for t in range(2):
                    o = wait_aux(act, f"ro{h}", t)
                    nc.scalar.activation(RO[:, t, h, :], o[:, :], ACT.Copy)
                    k, n = AUX[(f"ro{h}", t)]
                    square(junk[:, 0:C], o[:, :], S("ro_ss", 2 * h + t, 2 * h + t + 1), aux_free[k], n)

            act.wait_ge(sem("x2_nrstd"), 1)
            for h in range(4):
                wait_read(act, "rsc", h)
            ret_rows(0)
            ret_rows(1)
            unit("ret8", gate_rows(0))
            ret_rows(2)
            ret_rows(3)
            unit("ret9", gate_rows(1))
            unit("ret10", gate_rows(2))

            def ry_high(h):
                for b in range(2):
                    k, use = AUX[(f"ryT{h}", b)]
                    act.wait_ge(aux_ready[k], use)
                    nc.scalar.activation(ryTh[:, 4 * h + 2 * b:4 * h + 2 * b + 2, :], aux[k][:, :], ACT.Copy)\
                        .then_inc(sem("ryT_hi"), 1)

            ry_high(0)
            unit("ret11", gate_rows(3))
            ry_high(1)
            for h in range(4):
                if 1 <= h < 3:
                    ry_high(h + 1)
                if h < 3:
                    split(G["reto0"] + h + RING)

            def down_squares(p, name, n):
                for t in range(2):
                    wait_unit(act, name, t)
                    square(junk[:, 0:C], bank(name, t), S(f"{p}_ss", 2 * t + n, 2 * t + n + 1), sem(f"{p}_ss"), 2 * n + t + 1)

            down_squares("p2", "reto0", 0)
            split(G["reto0"] + 3 + RING)
            unit("reto1", lambda: down_squares("p2", "reto1", 1))

            def mlp(m, xname, gain, p):
                next_norm(xname, gain, lambda: act.wait_ge(sem(f"{xname}_rows"), 4), junk[:, :])

                def up(n, i=None):
                    name = f"up{m}_{n}"
                    split(G[name] + RING, i)
                    count = n if i is None else i * 2 + n
                    for t in range(2):
                        if t == 0:
                            act.wait_ge(half_done, count + (U[f"up{m}_0"] + 1))
                        else:
                            act.wait_ge(gran_used, GEND[name] if i is None else i * RING + GEND[name])
                        nc.scalar.activation(hrow[:, n % 2, t, :], bank(name, t), ACT.Relu,
                                             scale=S(f"{xname}_rstd", t, t + 1)).then_inc(drained["act"], 1)
                    split(GEND[name] - 1 + RING, i)

                def h_high(n, i=None):
                    dst = hTh[:, :, :].rearrange("p (n b k) t -> p n b k t", b=2, k=2)
                    for b in range(2):
                        k, use = AUX[(f"h{m}T{n % 2}", b)]
                        use += (n - n % 2) // 2
                        act.wait_ge(aux_ready[k], use if i is None else i + use)
                        nc.scalar.activation(dst[:, n if i is None else i * 2 + n, b, :, :], aux[k][:, :], ACT.Copy)\
                            .then_inc(sem(f"h{m}T_hi"), 1)

                act.wait_ge(sem(f"{xname}_rstd"), 1)
                up(0)
                up(1)
                h_high(0)
                with act.Fori(1, 4) as i:
                    up(0, i)
                    h_high(-1, i)
                    up(1, i)
                    h_high(0, i)
                split(G[f"down{m}_0"] + RING)
                h_high(7)
                for g in range(G[f"down{m}_0"] + 1, GEND[f"down{m}_0"] - 1):
                    split(g + RING)
                down_squares(p, f"down{m}_0", 0)
                split(GEND[f"down{m}_0"] - 1 + RING)
                unit(f"down{m}_1", lambda: down_squares(p, f"down{m}_1", 1))

            mlp(0, "x3", "mpre0", "p3")
            next_norm("x4", "pre1", lambda: act.wait_ge(sem("x4_rows"), 4), junk[:, :])
            unit("moba0", rows("moba0", lambda t: BQ[:, 0, t, :], "x4"))
            unit("moba1", rows("moba1", lambda t: BK[:, 0, t, :], "x4"))
            unit("moba2", rows("moba2", lambda t: BQ[:, 1, t, :], "x4"))

            def bq_turned(j):
                for b in range(2):
                    o = wait_aux(act, f"bqT{j}", b)
                    free(nc.scalar.activation(bqT[:, 4 * j + 2 * b:4 * j + 2 * b + 2, :], o[:, :], ACT.Copy,
                                              scale=float(HD) ** -0.5), f"bqT{j}", b)

            bq_turned(0)
            unit("moba3", rows("moba3", lambda t: BK[:, 1, t, :], "x4"))

            def moba_exps(h):
                pr = bprob if h < 4 else bprob2
                act.wait_ge(sem("b_max"), h + 1)
                nc.scalar.activation(S("bs_b", 2 * h, 2 * h + 2), S("bs_b", 2 * h, 2 * h + 2), ACT.Exp).then_inc(sem("b_past"), 1)
                for t in range(2):
                    k = 2 * h + t
                    nc.scalar.activation(pr[:, h % 4, t, :], pr[:, h % 4, t, :], ACT.Exp, bias=S("bs_nm", k, k + 1),
                                         accum_out=S("bs_sum", k, k + 1)).then_inc(sem("b_exp"), 1)

            for h in range(4):
                moba_exps(h)
            unit("moba4", rows("moba4", lambda t: BV[:, 0, t, :], "x4"))
            bq_turned(1)

            def moba_probs(hs):
                for h in hs:
                    if h >= 4:
                        wait_aux(act, "boT", h - 4)
                    probs_T("bpT", h, bpT)

            moba_probs((0, 2))
            unit("moba5", rows("moba5", lambda t: BV[:, 1, t, :], "x4"))
            for h in range(4):
                high("boT", h, byTh, (h,))
            for h in range(4, 8):
                moba_exps(h)
            split(G["mobao0"] + RING)
            moba_probs((4, 6))
            for h in range(4, 8):
                high("boT", h, byTh, (h,))
            down_squares("p4", "mobao0", 0)
            split(G["mobao0"] + 1 + RING)
            unit("mobao1", lambda: down_squares("p4", "mobao1", 1))
            mlp(1, "x5", "mpre1", "p5")

        @block.vector
        def _(dve):
            chain = [0]

            def link(ins):
                chain[0] += 1
                ins.then_inc(sem("dve_chain"), 1)
                dve.wait_ge(sem("dve_chain"), chain[0])

            def split(g, i=None):
                if g >= NG:
                    return
                slot, nk = g % RING, KTS[g]
                dve.wait_ge(hi_ready, g + 1 if i is None else i * RING + (g + 1))
                nc.vector.tensor_tensor(Wl[:, slot, 0:nk, :], raw[:, slot, 0:nk, :], Wh[:, slot, 0:nk, :].bitcast(F32),
                                        ALU.subtract).then_inc(lo_ready, 1)

            def unit(name, read_out=None):
                for g in range(G[name], GEND[name] - 1):
                    split(g + RING)
                if read_out:
                    read_out()
                split(GEND[name] - 1 + RING)

            def low(name, b, dst, hi, kts, gain=None):
                k, _ = AUX[(name, b)]
                o = aux[k]
                hb = f32(hi)
                if gain is None:
                    dve.wait_ge(sem(f"{name}_hi"), b + 1)
                    i = nc.vector.tensor_tensor(dst[:, kts[0]:kts[-1] + 1, :], per_kt(o, len(kts)), hb[:, kts[0]:kts[-1] + 1, :],
                                                ALU.subtract)
                else:
                    dve.wait_ge(sem(f"{name}_hi"), kts[-1] + 1)
                    for j, kt in enumerate(kts):
                        i = nc.vector.scalar_tensor_tensor(out=dst[:, kt, :], in0=o[:, j * TOK:(j + 1) * TOK],
                                                           scalar=gcol(gain, kt), in1=hb[:, kt, :],
                                                           op0=ALU.mult, op1=ALU.subtract)
                i.then_inc(aux_free[k], 1)

            def f32(t):
                return t[:, :, :].bitcast(F32)

            def per_kt(o, n):
                return o[:, 0:n * TOK].rearrange("p (k t) -> p k t", t=TOK)

            def power_in(key, n, width, need):
                dve.wait_ge(sem(f"{key}_ss"), need)
                nc.vector.tensor_scalar(S(f"{key}_var", 0, n), S(f"{key}_ss", 0, n), 1.0 / width, EPS, ALU.mult, ALU.add)\
                    .then_inc(sem(f"{key}_var"), 1)

            def head_sums(key):
                dve.wait_ge(sem(f"{key}_sq"), 1)
                link(nc.vector.tensor_reduce(S(f"{key}_ss"), sq[:, :, :].rearrange("p t (h d) -> p (t h) d", d=HD), AX.X, ALU.add))
                nc.vector.tensor_scalar(S(f"{key}_var"), S(f"{key}_ss"), 1.0 / HD, EPS, ALU.mult, ALU.add)\
                    .then_inc(sem(f"{key}_var"), 1)

            def x_stats(k, neg=False):
                power_in(k, 2, D, 2)
                if neg:
                    dve.wait_ge(sem(f"{k}_rstd"), 1)
                    nc.vector.tensor_scalar(S(f"{k}_nrstd"), S(f"{k}_rstd"), -1.0, None, ALU.mult).then_inc(sem(f"{k}_nrstd"), 1)

            def turned(name, b, dst, scale=None):
                o = wait_aux(dve, name, b)
                if scale is None:
                    free(nc.vector.tensor_copy(dst, o[:, :]), name, b)
                else:
                    free(nc.vector.tensor_scalar(dst, o[:, :], scale, None, ALU.mult), name, b)

            dve.wait_ge(sem("gains_in"), 16)
            for b in range(4):
                low("memT", b, memTl, memTh, (2 * b, 2 * b + 1), "g_mem")
            split(0)
            split(1)
            for b in range(4):
                low("xT", b, xTl, xTh, (2 * b, 2 * b + 1), "g_mix")
            power_in("mem", 2, D, 2)
            split(2)
            dve.wait_ge(sem("wsm_hi"), 1)
            nc.vector.tensor_tensor(wsml[:, :, :], wsm[:, :, :], f32(wsmh), ALU.subtract).then_inc(sem("wsm_lo"), 1)
            split(3)
            nc.vector.tensor_scalar(S("gmq_s"), gcol("g_mq"), float(HD) ** -0.5, None, ALU.mult).then_inc(sem("gmq_s"), 1)
            nc.vector.tensor_scalar(S("gfq_s"), gcol("g_fq"), float(HD) ** -0.5, None, ALU.mult).then_inc(sem("gfq_s"), 1)
            x_stats("x0", neg=True)
            unit("mk")
            o = wait_aux(dve, "small")
            dve.wait_ge(sem("b_fox_in"), 16)
            for t in range(2):
                nc.vector.tensor_scalar(S("ga", 16 * t, 16 * t + 16), o[:, 32 * t:32 * t + 16], S("x0_rstd", t, t + 1), None,
                                        ALU.mult).then_inc(sem("ga_rows"), 1)
            for t in range(2):
                i = nc.vector.scalar_tensor_tensor(out=S("ffz", 4 * t, 4 * t + 4), in0=o[:, 32 * t + 16:32 * t + 20],
                                                   scalar=S("x0_rstd", t, t + 1), in1=S("b_fox"), op0=ALU.mult, op1=ALU.add)
                if t == 1:
                    free(i, "small")
            head_sums("mk")
            dve.wait_ge(sem("ffl"), 1)
            nc.vector.scalar_tensor_tensor(out=S("lf"), in0=S("ffz"), scalar=0.0, in1=S("ffl"), op0=ALU.min,
                                           op1=ALU.subtract).then_inc(sem("lf"), 2)
            dve.wait_ge(sem("lf"), 2)
            nc.vector.tensor_scalar(S("nlf"), S("lf"), -1.0, None, ALU.mult).then_inc(sem("nlf"), 1)
            unit("mv")
            unit("mq")
            head_sums("mq")
            dve.wait_ge(sem("gla_l"), 1)
            o = wait_aux(dve, "z")
            free(nc.vector.scalar_tensor_tensor(out=gla_e[:, 0, :, :].rearrange("p t c -> p (t c)"), in0=o[:, :], scalar=0.0,
                                                in1=gla_e[:, 3, :, :].rearrange("p t c -> p (t c)"),
                                                op0=ALU.min, op1=ALU.subtract), "z")
            o = wait_aux(dve, "foxcum")
            free(nc.vector.tensor_copy(S("foxc"), o[:, 0:8]), "foxcum")
            nc.vector.memset(gattn[:, :, :, :], 0.0).then_inc(sem("gattn_zero"), 1)
            unit("gqk")
            unit("gv")
            turned("gkT", 0, gkT[:, :, :])
            unit("gg")
            dve.wait_ge(sem("gg_exp"), 2)
            link(nc.vector.tensor_scalar(gexp[:, :, :], gexp[:, :, :], 1.0, None, ALU.add))
            nc.vector.reciprocal(gexp[:, :, :], gexp[:, :, :]).then_inc(sem("gg_rec"), 1)
            dve.wait_ge(sem("gattn_zero"), 1)
            mask = K("chunk_upto").bitcast(U32).unsqueeze(1).broadcast_to([P, 4, P])
            for t in range(2):
                o = wait_aux(dve, "attn", t)
                free(nc.vector.copy_predicated(gattn[:, t, :, :], mask, o[:, :].rearrange("p (h i) -> p h i", h=4)), "attn", t)
            wait_read(dve, "dec")
            o = wait_aux(dve, "cs", 0)
            nc.vector.tensor_copy(state[:, 0, :, :], o[:, 0:256]).then_inc(sem("gla_state"), 1)
            dve.wait_ge(sem("gla_state"), 1)
            for c in (1, 2):
                o = wait_aux(dve, "cs", 2 - c)
                if c == 2:
                    dve.wait_ge(sem("gla_step"), 1)
                for pr in range(2):
                    at0 = (c // 2) * 256 + pr * P
                    i = nc.vector.scalar_tensor_tensor(out=state[:, c, pr, :], in0=state[:, c - 1, pr, :],
                                                       scalar=S("dec", 4 * pr + c, 4 * pr + c + 1), in1=o[:, at0:at0 + P],
                                                       op0=ALU.mult, op1=ALU.add)
                    if pr == 1:
                        free(i, "cs", 2 - c)
                if c == 1:
                    wait_read(dve, "cs", 1)
                    nc.vector.memset(S("ffa"), 0.0).then_inc(sem("gla_step"), 1)
            unit("fq")
            head_sums("go")
            head_sums("fq")
            unit("fk")
            for b in range(2):
                low("gyT", b, yT["gla"][1], yT["gla"][0], (2 * b, 2 * b + 1), "g_gla")
            head_sums("fk")
            for h in range(4):
                o = wait_aux(dve, "msc", h)
                nc.vector.tensor_reduce(S("ms_nm", 2 * h, 2 * h + 2), o[:, :].rearrange("p (t k) -> p t k", t=2), AX.X, ALU.max,
                                        negate=True).then_inc(sem("m_max"), 1)

            def normed(k, h, pr, nm, rec, total, widths):
                link(nc.vector.reciprocal(rec(0, 2), total(0, 2)))
                for t in range(2):
                    v = pr[:, h % 4, t, 0:widths[t]]
                    nc.vector.tensor_scalar(v, v, rec(t, t + 1), None, ALU.mult).then_inc(sem(f"{k}_prob"), 1)

            for h in range(4):
                wait_read(dve, "msc", h)
                normed("m", h, prob, None, lambda a, b: S("ms_rec", 2 * h + a, 2 * h + b),
                       lambda a, b: S("ms_sum", 2 * h + a, 2 * h + b), (TOK, TOK))
            unit("fv")
            for h in (1, 3):
                turned("mpT", h, mpT[:, h, :, :])

            def gate_rows(b, n):
                def go():
                    k = 3 * n + BRANCHES.index(b)
                    dve.wait_ge(sem(f"bias{k % 2}"), 16 * (k // 2 + 1))
                    for t in range(2):
                        wait_unit(dve, f"gate_{b}{n}", t)
                        nc.vector.scalar_tensor_tensor(out=gate[b][:, t, :], in0=bank(f"gate_{b}{n}", t),
                                                       scalar=S("x0_rstd", t, t + 1), in1=grow[:, (k % 2) * C:(k % 2 + 1) * C],
                                                       op0=ALU.mult, op1=ALU.add).then_inc(drained["dve"], 1)
                    dve.wait_ge(sem("gate_exp"), 2 * (k + 1))
                    link(nc.vector.tensor_scalar(gate[b][:, :, :], gate[b][:, :, :], 1.0, None, ALU.add))
                    link(nc.vector.reciprocal(gate[b][:, :, :], gate[b][:, :, :]))
                return go

            def branch_rows(b, n):
                def go():
                    for t in range(2):
                        wait_unit(dve, f"branch_{b}{n}", t)
                        m = merged[:, t, n * C:(n + 1) * C]
                        dst = m if b == "mem" else gate[b][:, t, :]
                        i = nc.vector.tensor_tensor(dst, bank(f"branch_{b}{n}", t), gate[b][:, t, :], ALU.mult)
                        i.then_inc(drained["dve"], 1)
                        if b != "mem":
                            wait_drained(dve, f"branch_{b}{n}", t)
                            if b == "fox":
                                dve.wait_ge(sem("merged"), 2 * n * 2 + t + 1)
                            nc.vector.tensor_tensor(m, m, gate[b][:, t, :], ALU.add).then_inc(sem("merged"), 1)
                        if b == "mem":
                            wait_drained(dve, f"branch_{b}{n}", t)
                return go

            unit("gate_mem0", gate_rows("mem", 0))
            for h in range(4):
                low("moT", h, yT["mem"][1], yT["mem"][0], (h,))
            for b in range(2):
                turned("fkT", b, fkT[:, 2 * b:2 * b + 2, :], gcol("g_fk"))
            unit("gate_gla0", gate_rows("gla", 0))
            for h in range(4):
                o = wait_aux(dve, "fsc", h)
                nc.vector.scalar_tensor_tensor(out=prob[:, h, 0, 0:P], in0=o[:, 0:P], scalar=S("foxc", h, h + 1),
                                               in1=K("tri_mask"), op0=ALU.add, op1=ALU.add)
                free(nc.vector.scalar_tensor_tensor(out=prob[:, h, 1, :], in0=o[:, TOK:2 * TOK], scalar=S("foxc", 4 + h, 5 + h),
                                                    in1=cst[:, CONST["zero_mask"][0]:CONST["zero_mask"][0] + TOK],
                                                    op0=ALU.add, op1=ALU.add), "fsc", h)
                wait_read(dve, "fsc", h)
                nc.vector.tensor_reduce(S("fs_nm", 2 * h, 2 * h + 1), prob[:, h, 0, 0:P], AX.X, ALU.max, negate=True)
                nc.vector.tensor_reduce(S("fs_nm", 2 * h + 1, 2 * h + 2), prob[:, h, 1, :], AX.X, ALU.max, negate=True)\
                    .then_inc(sem("f_max"), 1)
            for h in range(4):
                dve.wait_ge(sem("f_exp"), 2 * h + 2)
                normed("f", h, prob, None, lambda a, b: S("fs_rec", 2 * h + a, 2 * h + b),
                       lambda a, b: S("fs_sum", 2 * h + a, 2 * h + b), (P, TOK))
            unit("gate_fox0", gate_rows("fox", 0))
            for h in (1, 3):
                o = wait_aux(dve, "fpT", h)
                nc.vector.tensor_copy(fpT[:, h, 0, :], o[:, 0:TOK])
                free(nc.vector.tensor_copy(fpT[:, h, 1, P:TOK], o[:, TOK + P:2 * TOK]), "fpT", h)
            unit("branch_mem0", branch_rows("mem", 0))
            for h in range(4):
                low("foT", h, yT["fox"][1], yT["fox"][0], (h,))
            unit("branch_gla0", branch_rows("gla", 0))
            unit("branch_fox0", branch_rows("fox", 0))
            for b in BRANCHES:
                unit(f"gate_{b}1", gate_rows(b, 1))
            for b in BRANCHES:
                unit(f"branch_{b}1", branch_rows(b, 1))
            for b in range(4):
                low("mgT", b, xTl, xTh, (2 * b, 2 * b + 1))

            def add_rows(name, n):
                def go():
                    for t in range(2):
                        wait_unit(dve, name, t)
                        v = x[:, t, n * C:(n + 1) * C]
                        nc.vector.tensor_tensor(v, bank(name, t), v, ALU.add).then_inc(drained["dve"], 1)
                return go

            for n in range(2):
                unit(f"wout{n}", add_rows(f"wout{n}", n))

            def next_norm(k, gain, neg=False):
                for b in range(4):
                    low(f"{k}T", b, xTl, xTh, (2 * b, 2 * b + 1), gain)
                x_stats(k, neg)

            next_norm("x1", "g_ffn", neg=True)

            def ff(n, i=None):
                name = f"ffn{n}"
                split(G[name] + RING, i)
                count = n if i is None else i * 2 + n
                dve.wait_ge(sem("ff_exp"), count * 2 + 2)
                nc.vector.tensor_scalar(fe[:, n % 2, :, :], fe[:, n % 2, :, :], 1.0, None, ALU.add).then_inc(sem("ff_one"), 1)
                dve.wait_ge(sem("ff_one"), count + 1)
                nc.vector.reciprocal(fe[:, n % 2, :, :], fe[:, n % 2, :, :]).then_inc(sem("ff_rec"), 1)
                split(GEND[name] - 1 + RING, i)

            def ff_low(n, i=None):
                k, use = AUX[(f"ffT{n}", 0)]
                count = n if i is None else i * 2 + n
                dve.wait_ge(sem("ffT_hi"), count + 1)
                lo = ffTl[:, :, :].rearrange("p (n k) t -> p n k t", k=2)
                hi = f32(ffTh).rearrange("p (n k) t -> p n k t", k=2)
                nc.vector.tensor_tensor(lo[:, count, :, :], per_kt(aux[k], 2), hi[:, count, :, :], ALU.subtract)\
                    .then_inc(aux_free[k], 1)

            ff(0)
            ff(1)
            ff_low(0)
            ff(2)
            ff_low(1)
            with dve.Fori(1, 5) as i:
                for n in (1, 2):
                    ff(n, i)
                    ff_low(n - 1, i)
            split(G["ffd0"] + RING)
            ff_low(10)
            for g in range(G["ffd0"] + 1, GEND["ffd0"] - 1):
                split(g + RING)
            add_rows("ffd0", 0)()
            split(GEND["ffd0"] - 1 + RING)
            unit("ffd1", add_rows("ffd1", 1))
            next_norm("x2", "pre0", neg=True)
            dve.wait_ge(sem("rtab_in"), 16)

            def rotate(rows, j, key):
                def go():
                    wait_drained(dve, f"ret{j + (2 if key == 'rk_rot' else 0)}", 1)
                    xs = rows[:, :, j * C:(j + 1) * C].rearrange("p t (h c) -> p t h c", c=256)
                    ts = rtmp[:, :, :].rearrange("p t (h c) -> p t h c", c=256)
                    sn = rtab[:, :, 1, :].unsqueeze(2).broadcast_to([P, 2, 2, 256])
                    cs = rtab[:, :, 0, :].unsqueeze(2).broadcast_to([P, 2, 2, 256])
                    for t in range(2):
                        nc.vector.tensor_tensor(ts[:, t, :, 0::2], xs[:, t, :, 1::2], sn[:, t, :, 0::2], ALU.mult)
                        i = nc.vector.tensor_tensor(ts[:, t, :, 1::2], xs[:, t, :, 0::2], sn[:, t, :, 1::2], ALU.mult)
                    link(i)
                    link(nc.vector.tensor_tensor(xs, xs, cs, ALU.mult))
                    nc.vector.tensor_tensor(xs, xs, ts, ALU.add).then_inc(sem(key), 1)
                    dve.wait_ge(sem(key), j + 1)
                return go

            def rk_turned(j):
                for b in range(2):
                    turned(f"rkT{j}", b, rkT[:, 4 * j + 2 * b:4 * j + 2 * b + 2, :], 256.0 ** -0.5)

            unit("ret0", rotate(RQ, 0, "rq_rot"))
            unit("ret1", rotate(RQ, 1, "rq_rot"))
            unit("ret2", rotate(RK, 0, "rk_rot"))
            unit("ret3", rotate(RK, 1, "rk_rot"))
            unit("ret4")
            rk_turned(0)
            unit("ret5")
            rk_turned(1)
            unit("ret6")
            dve.wait_ge(sem("rdm_in"), 16)
            for h in range(4):
                o = wait_aux(dve, "rsc", h)
                free(nc.vector.tensor_tensor(rscT[:, h, :], o[:, 0:384], rdm[:, h, :], ALU.mult), "rsc", h)
            unit("ret7")

            def gate_recip(h):
                def go():
                    dve.wait_ge(sem("rg_exp"), 2 * h + 2)
                    link(nc.vector.tensor_scalar(rge[:, :, :], rge[:, :, :], 1.0, None, ALU.add))
                    nc.vector.reciprocal(rge[:, :, :], rge[:, :, :]).then_inc(sem("rg_rec"), 1)
                return go

            def ry_rows(h):
                dve.wait_ge(sem("rg_silu"), h + 1)
                for t in range(2):
                    nc.vector.scalar_tensor_tensor(out=RO[:, t, h, :], in0=RO[:, t, h, :],
                                                   scalar=S("ro_rstd", 2 * h + t, 2 * h + t + 1), in1=RG[:, h, t, :],
                                                   op0=ALU.mult, op1=ALU.mult).then_inc(sem("ry_rows"), 1)

            def ry_low(h):
                for b in range(2):
                    k, _ = AUX[(f"ryT{h}", b)]
                    dve.wait_ge(sem("ryT_hi"), 2 * h + b + 1)
                    kt = 4 * h + 2 * b
                    nc.vector.tensor_tensor(ryTl[:, kt:kt + 2, :], per_kt(aux[k], 2), f32(ryTh)[:, kt:kt + 2, :],
                                            ALU.subtract).then_inc(aux_free[k], 1)

            unit("ret8", gate_recip(0))
            for h in range(4):
                for t in range(2):
                    wait_read(dve, f"ro{h}", t)
            nc.vector.tensor_scalar(S("ro_var"), S("ro_ss"), 1.0 / C, EPS, ALU.mult, ALU.add).then_inc(sem("ro_var"), 1)
            unit("ret9", gate_recip(1))
            dve.wait_ge(sem("ro_rstd"), 1)
            ry_rows(0)
            unit("ret10", gate_recip(2))
            ry_rows(1)
            ry_low(0)
            unit("ret11", gate_recip(3))
            ry_low(1)
            ry_rows(2)
            ry_rows(3)
            for h in range(3):
                if h:
                    ry_low(h + 1)
                split(G["reto0"] + h + RING)

            def gained(p, name, n, k):
                def go():
                    dve.wait_ge(sem("post_in"), 16 * k)
                    for t in range(2):
                        dve.wait_ge(sem(f"{p}_ss"), 2 * n + t + 1)
                        nc.vector.tensor_tensor(ygs(p)[:, t, n * C:(n + 1) * C], bank(name, t), grow[:, n * C:(n + 1) * C],
                                                ALU.mult).then_inc(drained["dve"], 1)
                return go

            def ygs(p):
                return ygr if p in ("p2", "p4") else yg

            def residual(p, name, xname):
                for t in range(2):
                    dve.wait_ge(sem(f"{p}_ss"), 3 + t)
                    link(nc.vector.tensor_tensor(S(f"{p}_tot", t, t + 1), S(f"{p}_ss", 2 * t, 2 * t + 1),
                                                 S(f"{p}_ss", 2 * t + 1, 2 * t + 2), ALU.add))
                    nc.vector.tensor_scalar(S(f"{p}_var", t, t + 1), S(f"{p}_tot", t, t + 1), 1.0 / D, EPS, ALU.mult, ALU.add)\
                        .then_inc(sem(f"{p}_var"), 1)
                wait_drained(dve, name, 1)
                for t in range(2):
                    dve.wait_ge(sem(f"{p}_rstd"), t + 1)
                    for n in range(2):
                        v = x[:, t, n * C:(n + 1) * C]
                        nc.vector.scalar_tensor_tensor(out=v, in0=ygs(p)[:, t, n * C:(n + 1) * C], scalar=S(f"{p}_rstd", t, t + 1),
                                                       in1=v, op0=ALU.mult, op1=ALU.add).then_inc(sem(f"{xname}_rows"), 1)

            gained("p2", "reto0", 0, 1)()
            split(G["reto0"] + 3 + RING)
            unit("reto1", gained("p2", "reto1", 1, 1))
            residual("p2", "reto1", "x3")

            def mlp(m, xname, gain, p, after, post_k):
                next_norm(xname, gain)

                def up(n, i=None):
                    name = f"up{m}_{n}"
                    split(G[name] + RING, i)
                    split(GEND[name] - 1 + RING, i)

                def h_low(n, i=None):
                    lo = hTl[:, :, :].rearrange("p (n b k) t -> p n b k t", b=2, k=2)
                    hi = f32(hTh).rearrange("p (n b k) t -> p n b k t", b=2, k=2)
                    at_n = n if i is None else i * 2 + n
                    for b in range(2):
                        k, _ = AUX[(f"h{m}T{n % 2}", b)]
                        dve.wait_ge(sem(f"h{m}T_hi"), 2 * n + b + 1 if i is None else i * 4 + (2 * n + b + 1))
                        nc.vector.tensor_tensor(lo[:, at_n, b, :, :], per_kt(aux[k], 2), hi[:, at_n, b, :, :], ALU.subtract)\
                            .then_inc(aux_free[k], 1)

                up(0)
                up(1)
                h_low(0)
                with dve.Fori(1, 4) as i:
                    up(0, i)
                    h_low(-1, i)
                    up(1, i)
                    h_low(0, i)
                split(G[f"down{m}_0"] + RING)
                h_low(7)
                for g in range(G[f"down{m}_0"] + 1, GEND[f"down{m}_0"] - 1):
                    split(g + RING)
                gained(p, f"down{m}_0", 0, post_k)()
                split(GEND[f"down{m}_0"] - 1 + RING)
                unit(f"down{m}_1", gained(p, f"down{m}_1", 1, post_k))
                residual(p, f"down{m}_1", after)

            mlp(0, "x3", "mpre0", "p3", "x4", 2)
            next_norm("x4", "pre1")
            unit("moba0")
            unit("moba1")
            unit("moba2")

            def bk_turned(j):
                for b in range(2):
                    turned(f"bkT{j}", b, bkT[:, 4 * j + 2 * b:4 * j + 2 * b + 2, :])

            def masked_max(h):
                pr = bprob if h < 4 else bprob2
                o = wait_aux(dve, "bsc", h)
                z0 = CONST["zero_mask"][0]
                nc.vector.tensor_tensor(pr[:, h % 4, 0, :], o[:, 0:TOK], cst[:, z0 + P:z0 + 3 * P], ALU.add)
                free(nc.vector.tensor_tensor(pr[:, h % 4, 1, :], o[:, TOK:2 * TOK], cst[:, z0:z0 + 2 * P], ALU.add), "bsc", h)
                wait_read(dve, "bsc", h)
                nm, b = S("bs_nm", 2 * h, 2 * h + 2), S("bs_b", 2 * h, 2 * h + 2)
                link(nc.vector.tensor_reduce(nm, pr[:, h % 4, :, :], AX.X, ALU.max, negate=True))
                link(nc.vector.tensor_scalar(nm, nm, -NEG, None, ALU.min))
                nc.vector.tensor_scalar(b, nm, NEG, None, ALU.add).then_inc(sem("b_max"), 1)

            def moba_probs(h):
                pr = bprob if h < 4 else bprob2
                dve.wait_ge(sem("b_exp"), 2 * h + 2)
                ks = (2 * h, 2 * h + 2)
                link(nc.vector.scalar_tensor_tensor(out=S("bs_l", *ks), in0=S("bs_b", *ks), scalar=float(TOK), in1=S("bs_sum", *ks),
                                                    op0=ALU.mult, op1=ALU.add))
                link(nc.vector.reciprocal(S("bs_rec", *ks), S("bs_l", *ks)))
                for t in range(2):
                    v = pr[:, h % 4, t, :]
                    nc.vector.tensor_scalar(v, v, S("bs_b", 2 * h + t, 2 * h + t + 1), S("bs_rec", 2 * h + t, 2 * h + t + 1),
                                            ALU.add, ALU.mult).then_inc(sem("b_prob"), 1)

            bk_turned(0)
            unit("moba3")
            for h in range(4):
                masked_max(h)
            for h in range(4):
                moba_probs(h)
            unit("moba4")
            bk_turned(1)
            for h in (1, 3):
                turned("bpT", h, bpT[:, h, :, :])
            unit("moba5")
            for h in range(4):
                low("boT", h, byTl, byTh, (h,))
            for h in range(4, 8):
                masked_max(h)
            for h in range(4, 8):
                moba_probs(h)
            split(G["mobao0"] + RING)
            for h in (5, 7):
                wait_aux(dve, "boT", h - 4)
                turned("bpT", h, bpT[:, h % 4, :, :])
            for h in range(4, 8):
                low("boT", h, byTl, byTh, (h,))
            gained("p4", "mobao0", 0, 3)()
            split(G["mobao0"] + 1 + RING)
            unit("mobao1", gained("p4", "mobao1", 1, 3))
            residual("p4", "mobao1", "x5")
            mlp(1, "x5", "mpre1", "p5", "x6", 4)



def kernel(**inputs):
    import concourse.bacc as _bacc
    from concourse.bass_utils import run_bass_kernel_spmd as _run

    I = {k: np.asarray(v) for k, v in inputs.items()}
    stream = np.zeros((NG, P, GK, C), np.float32)

    def put(name, w):
        k0 = 0
        for g in range(G[name], GEND[name]):
            nk = KTS[g]
            stream[g, :, 0:nk] = w[k0 * P:(k0 + nk) * P].reshape(nk, P, C).transpose(1, 0, 2)
            k0 += nk

    w_in, mkv = I["w_in"][0], I["w_mem_kv"][0]
    put("mk", mkv[:, 0:C])
    put("mv", mkv[:, C:2 * C])
    for n, c0 in IN_COLS.items():
        put(n, w_in[:, c0:c0 + C])
    for n in range(2):
        for b in BRANCHES:
            put(f"gate_{b}{n}", w_in[:, GATE_COL[b] + n * C:GATE_COL[b] + (n + 1) * C])
            put(f"branch_{b}{n}", I["w_branch"][0, BRANCH_ROW[b]][:, n * C:(n + 1) * C])
        for name, w in (("wout", I["w_out"][0]), ("ffd", I["w_ffn_down"][0]), ("reto", I["w_out_0_2"]),
                        ("down0_", I["w_down_0_2"]), ("mobao", I["w_out_1_2"]), ("down1_", I["w_down_1_2"])):
            put(f"{name}{n}", w[:, n * C:(n + 1) * C])
    for n in range(FFN // 256):
        s = slice(n * 256, (n + 1) * 256)
        put(f"ffn{n}", np.concatenate([I["w_ffn_gate"][0][:, s], I["w_ffn_up"][0][:, s]], axis=1))
    for n in range(12):
        put(f"ret{n}", I["w_in_0_2"][:, n * C:(n + 1) * C])
    for n, c0 in enumerate(MOBA_COLS):
        put(f"moba{n}", I["w_in_1_2"][:, c0:c0 + C])
    for n in range(8):
        put(f"up0_{n}", I["w_up_0_2"][:, n * C:(n + 1) * C])
        put(f"up1_{n}", I["w_up_1_2"][:, n * C:(n + 1) * C])

    def cols(v):
        return v.reshape(-1, P).T

    gpack = np.concatenate([cols(I[k].reshape(-1)) for k in (
        "g_mix", "g_mem", "g_ffn", "ln_mix_pre_0_2", "ln_mlp_pre_0_2", "ln_mix_pre_1_2", "ln_mlp_pre_1_2",
        "g_gla_out", "g_fox_q", "g_fox_k", "g_mem_q", "g_mem_k")], axis=1)
    narrow = np.concatenate([w_in[:, 1536:1552], w_in[:, 3088:3092]], axis=1).reshape(DK, P, 20).transpose(1, 0, 2)
    rett, mobat, dmask = rotary_tables()
    arrays = {
        "wstream": stream, "x": I["x"][0], "mem": I["mem"][0], "constants": CPACK, "gain_cols": gpack, "w_narrow": narrow,
        "w_gla_a2": I["w_gla_a2"][0], "b_gla_a": I["b_gla_a"], "b_fox_f": I["b_fox_f"], "b_gate": I["b_gate"],
        "post_gains": np.stack([I[k] for k in ("ln_mix_post_0_2", "ln_mlp_post_0_2", "ln_mix_post_1_2", "ln_mlp_post_1_2")]),
        "ret_tables": rett.reshape(P, 2, 2, 256), "moba_tables": mobat.reshape(P, 2, 2, 16), "ret_decays": dmask,
    }
    nc = _bacc.Bacc("TRN2", target_bir_lowering=False, num_devices=1)
    arrays = {f"in_{k}": np.ascontiguousarray(v, dtype=np.float32) for k, v in arrays.items()}
    args = [nc.dram_tensor(k, v.shape, mybir.dt.float32, kind="ExternalInput").ap() for k, v in arrays.items()]
    args.append(nc.dram_tensor("out", (TOK, D), mybir.dt.float32, kind="ExternalOutput").ap())
    build(nc, *args)
    r = _run(nc, [arrays], core_ids=[0])
    return r.results[0]["out"].reshape(1, TOK, D)
```

```python
from contextlib import ExitStack

import numpy as np
import concourse.bass as bass
from concourse import mybir

F32 = mybir.dt.float32
F32R = mybir.dt.float32r
U32 = mybir.dt.uint32
EXP_AND_LN = 6
ALU = mybir.AluOpType
ACT = mybir.ActivationFunctionType
AX = mybir.AxisListType

P = 128
TOK = 256
D = 1024
DK = D // P
C = 512
EPS = 1e-6
NEG = -1e30
FFN = 2816
FFK = FFN // P
MLP = 4096
MLPK = MLP // P
HD = 128
RING = 4
GK = 4

A_UNITS = ["mk", "mv", "mq", "gqk", "gv", "gg", "fq", "fk", "fv"]
BRANCHES = ["mem", "gla", "fox"]
GATES = [f"gate_{b}{n}" for n in range(2) for b in BRANCHES]


def plan():
    G, U, kts = {}, {}, []

    def unit(name, widths):
        U[name] = len(U)
        G[name] = len(kts)
        kts.extend(widths)

    for n in A_UNITS:
        unit(n, [4, 4])
    for n in range(2):
        for b in BRANCHES:
            unit(f"gate_{b}{n}", [4, 4])
        for b in BRANCHES:
            unit(f"branch_{b}{n}", [4])
    for n in range(2):
        unit(f"wout{n}", [4, 4])
    for n in range(FFN // 256):
        unit(f"ffn{n}", [4, 4])
    for n in range(2):
        unit(f"ffd{n}", [4, 4, 4, 4, 4, 2])
    for n in range(12):
        unit(f"ret{n}", [4, 4])
    for n in range(2):
        unit(f"reto{n}", [4] * 4)
    for n in range(8):
        unit(f"up0_{n}", [4, 4])
    for n in range(2):
        unit(f"down0_{n}", [4] * 8)
    for n in range(6):
        unit(f"moba{n}", [4, 4])
    for n in range(2):
        unit(f"mobao{n}", [4, 4])
    for n in range(8):
        unit(f"up1_{n}", [4, 4])
    for n in range(2):
        unit(f"down1_{n}", [4] * 8)
    return G, U, kts


G, U, KTS = plan()
NG = len(KTS)
UNITS = list(U)
GEND = {n: (G[UNITS[k + 1]] if k + 1 < len(UNITS) else NG) for k, n in enumerate(UNITS)}


def plan_drain():
    drain, count = {}, {"act": 0, "dve": 0}
    for n in UNITS:
        by = "dve" if n.startswith(("gate", "branch", "wout", "ffd", "reto", "down", "mobao")) else "act"
        drain[n] = (by, count[by])
        count[by] += 2
    return drain


DRAIN = plan_drain()
TOGETHER = [("branch_gla1", "branch_fox1"), ("wout0", "wout1"), ("mobao0", "mobao1")]


def reads(name, t):
    for a, b in TOGETHER:
        if name in (a, b):
            return DRAIN[a][1] + 2 * t + (name == b) + 1
    return DRAIN[name][1] + t + 1


MOBA_COLS = [0, 1024, 512, 1536, 2048, 2560]
IN_COLS = {"gqk": 0, "gv": 512, "gg": 1024, "fq": 1552, "fk": 2064, "fv": 2576, "mq": 3092}
GATE_COL = {"gla": 3604, "fox": 3604 + D, "mem": 3604 + 2 * D}
BRANCH_ROW = {"gla": 0, "fox": 1, "mem": 2}


def plan_aux():
    plan, used = {}, [0] * 4

    def use(name, banks, first=0):
        for b, bank in enumerate(banks):
            used[bank] += 1
            plan[(name, first + b)] = (bank, used[bank])

    use("memT", [0, 1, 2, 3])
    use("xT", [0, 1, 2, 3])
    use("small", [0])
    use("gaT", [1])
    use("mkT", [2, 3])
    use("z", [0])
    use("foxcum", [1])
    use("cum", [2])
    use("suf", [3])
    use("dec", [0])
    use("mqT", [1, 2])
    use("gqT", [3])
    use("gkT", [0])
    use("attn", [1, 2])
    use("cs", [3, 0])
    use("o", [1, 2])
    use("msc", [0, 1, 2, 3])
    use("mpT", [0, 1, 2, 3])
    use("moT", [0, 1, 2, 3])
    use("fqT", [0, 1])
    use("fkT", [2, 3])
    use("gyT", [0, 1])
    use("fsc", [0, 1, 2, 3])
    use("fpT", [0, 1, 2, 3])
    use("foT", [0, 1, 2, 3])
    use("mgT", [0, 1, 2, 3])
    use("x1T", [0, 1, 2, 3])
    for n in range(FFN // 256):
        use(f"ffT{n}", [n % 2])
    use("x2T", [0, 1, 2, 3])
    use("rqT0", [0, 1])
    use("rqT1", [2, 3])
    use("rkT0", [0, 1])
    use("rkT1", [2, 3])
    use("rsc", [0, 1, 2, 3])
    for h in range(4):
        use(f"ro{h}", [2 * h % 4, 2 * h % 4 + 1])
    for h in range(4):
        use(f"ryT{h}", [2 * h % 4, 2 * h % 4 + 1])
    use("x3T", [0, 1, 2, 3])
    for n in range(8):
        use(f"h0T{n}", [2 * n % 4, 2 * n % 4 + 1])
    use("x4T", [0, 1, 2, 3])
    use("bqT0", [0, 1])
    use("bkT0", [2, 3])
    use("bsc", [0, 1, 2, 3])
    use("bqT1", [0, 1])
    use("bkT1", [2, 3])
    use("bpT", [0, 1, 2, 3])
    use("bsc", [0, 1, 2, 3], 4)
    use("boT", [0, 1, 2, 3])
    use("bpT", [0, 1, 2, 3], 4)
    use("boT", [0, 1, 2, 3], 4)
    use("x5T", [0, 1, 2, 3])
    for n in range(8):
        use(f"h1T{n}", [2 * n % 4, 2 * n % 4 + 1])
    return plan


AUX = plan_aux()

CONST = {}


def pack_constants():
    s = np.arange(P)[:, None]
    i = np.arange(P)[None, :]
    same = (s // 64) == (i // 64)
    parts = {
        "ident": np.eye(P),
        "chunk_upto": (s <= i) & same,
        "chunk_after": (s > i) & same,
        "upto": s <= i,
        "ones": np.ones((P, P)),
        "zero_mask": np.zeros((P, P)),
        "tri_mask": np.where(i <= s, 0.0, NEG),
        "full_mask": np.full((P, P), NEG),
        "half": np.concatenate([s < 64, s >= 64], axis=1),
        "minus_half": np.full((P, 1), -0.5),
        "eps": np.full((P, 1), EPS),
    }
    at = 0
    for k, v in parts.items():
        CONST[k] = (at, v.shape[1])
        at += v.shape[1]
    return np.concatenate([np.asarray(v, np.float32) for v in parts.values()], axis=1)


def rotary_tables():
    f = np.float32
    pos = np.arange(TOK, dtype=f)[:, None]
    freq = (1.0 / (f(10000.0) ** np.linspace(0.0, 1.0, 128, dtype=f))).astype(f)
    ang = (pos * freq[None, :]).astype(f)
    cos, sin = np.cos(ang), np.sin(ang)
    cc = np.repeat(cos, 2, axis=1)
    ss = np.stack([-sin, sin], axis=-1).reshape(TOK, 256)
    inv = (f(500000.0) ** (-np.arange(0, 32, 2, dtype=f) / f(32))).astype(f)
    ang = (pos * inv[None, :]).astype(f)
    mc, ms = np.cos(ang), np.sin(ang)
    tiles = lambda a: a.reshape(2, P, -1).transpose(1, 0, 2)
    ret = np.concatenate([tiles(cc), tiles(ss)], axis=2)
    moba = np.concatenate([tiles(mc), tiles(ms)], axis=2)
    lg = np.log(f(1.0) - f(2.0) ** (f(-5.0) - np.arange(4, dtype=f))).astype(f)
    j = np.arange(P, dtype=f)[:, None]
    i = np.arange(P, dtype=f)[None, :]
    dm = []
    for h in range(4):
        own = np.where(i >= j, np.exp(lg[h] * np.maximum(i - j, 0)), 0)
        cross = np.exp(lg[h] * (P - 1.0 - j)) * np.exp(lg[h] * (i + 1.0))
        dm.append(np.concatenate([own, cross, own], axis=1))
    return ret.astype(f), moba.astype(f), np.stack(dm, axis=1).astype(f)


CPACK = pack_constants()

GAIN_COLS = {}
_at = 0
for _n, _w in (("g_mix", 8), ("g_mem", 8), ("g_ffn", 8), ("pre0", 8), ("mpre0", 8), ("pre1", 8), ("mpre1", 8),
               ("g_gla", 4), ("g_fq", 1), ("g_fk", 1), ("g_mq", 1), ("g_mk", 1)):
    GAIN_COLS[_n] = (_at, _w)
    _at += _w
NGAIN = _at

SCAL = {}
_at = 0
for _n, _w in (
    [("b_fox", 4), ("gfq_s", 1), ("gmq_s", 1)]
    + [(f"{k}{w}", 2) for k in ("mem", "x0", "x1", "x2", "x3", "x4", "x5", "x6") for w in ("_ss", "_var", "_rstd")]
    + [(f"{k}{w}", 8) for k in ("mk", "mq", "fq", "fk", "go", "ro") for w in ("_ss", "_var", "_rstd")]
    + [(f"{k}_{w}", n) for k in ("p2", "p3", "p4", "p5") for w, n in (("ss", 4), ("var", 2), ("rstd", 2))]
    + [("ga", 32), ("ffz", 8), ("ffa", 8), ("ffl", 8), ("lf", 8), ("nlf", 8), ("foxc", 8), ("dec", 8)]
    + [(f"{k}_{w}", 8) for k in ("ms", "fs") for w in ("nm", "sum", "rec")]
    + [(f"bs_{w}", 16) for w in ("nm", "sum", "b", "l", "rec")]
):
    SCAL[_n] = (_at, _w)
    _at += _w
NSCAL = _at


def build(nc, wstream, x_in, mem_in, cpack, gpack, wsmall, w_a2, b_a, b_fox, b_gate, post, rett, mobat, dmask, out):
    ctx = ExitStack()
    with ctx:
        KB = 1024
        BASE = 16640

        def at(name, shape, kb, dt=F32):
            return nc.alloc_sbuf_tensor_at(name, shape, dt, offset=BASE + int(kb * KB))

        raw = at("raw", [P, RING, GK, C], 0)
        Wh = at("Wh", [P, RING, GK, C], 32, F32R)
        Wl = at("Wl", [P, RING, GK, C], 64, F32R)
        x = at("x", [P, 2, D], 96)
        xTh = at("xTh", [P, DK, TOK], 104, F32R)
        xTl = at("xTl", [P, DK, TOK], 112, F32R)
        cst = at("cst", [P, CPACK.shape[1]], 120)
        gains = at("gains", [P, NGAIN], 124.25)
        sc = at("sc", [P, NSCAL], 124.5)
        grow = at("grow", [P, D], 127)
        R = 131
        memTh = at("memTh", [P, DK, TOK], R, F32R)
        memTl = at("memTl", [P, DK, TOK], R + 8, F32R)
        yT = {b: (at(f"yTh_{b}", [P, 4, TOK], R + 8 * n, F32R), at(f"yTl_{b}", [P, 4, TOK], R + 8 * n + 4, F32R))
              for n, b in enumerate(("mem", "fox", "gla"))}
        gla_e = at("gla_e", [P, 4, 2, 256], R + 16)
        MK = at("MK", [P, 2, C], R + 24)
        MQ = at("MQ", [P, 2, C], R + 28)
        GQK = at("GQK", [P, 2, C], R + 32)
        FQ = at("FQ", [P, 2, C], R + 24)
        FK = at("FK", [P, 2, C], R + 28)
        state = at("state", [P, 3, 2, P], R + 28)
        merged = at("merged", [P, 2, D], R + 24)
        MV = at("MV", [P, 2, C], R + 36)
        FV = at("FV", [P, 2, C], R + 40)
        GV = at("GV", [P, 2, C], R + 44)
        GG = at("GG", [P, 2, C], R + 48)
        gate = {"mem": at("gate_mem", [P, 2, C], R + 32), "gla": at("gate_gla", [P, 2, C], R + 48),
                "fox": at("gate_fox", [P, 2, C], R + 44)}
        wsm = at("wsm", [P, DK, 20], R + 40)
        wsmh = at("wsmh", [P, DK, 20], R + 40.75, F32R)
        wsml = at("wsml", [P, DK, 20], R + 41.5, F32R)
        wa2 = at("wa2", [16, 256], R + 42.25)
        brow = at("brow", [1, 256], R + 43.25)
        gaT = at("gaT", [16, TOK], R + 48)
        mqT = at("mqT", [P, 4, TOK], R + 52)
        mkT = at("mkT", [P, 4, TOK], R + 56)
        fpT = at("fpT", [P, 4, 2, TOK], R + 52)
        fqT = at("fqT", [P, 4, TOK], R + 60)
        fkT = at("fkT", [P, 4, TOK], R + 64)
        mpT = at("mpT", [P, 4, 2, TOK], R + 60)
        gqT = at("gqT", [P, 2, TOK], R + 60)
        gkT = at("gkT", [P, 2, TOK], R + 62)
        gattn = at("gattn", [P, 2, 4, P], R + 64)
        prob = at("prob", [P, 4, 2, TOK], R + 68)
        gexp = at("gexp", [P, 2, C], R + 68)
        go = at("go", [P, 2, C], R + 72)
        mrows = at("mrows", [P, 2, D], R + 52)
        sq = at("sq", [P, 2, C], 127)
        ffTh = at("ffTh", [P, FFK, TOK], R, F32R)
        ffTl = at("ffTl", [P, FFK, TOK], R + 22, F32R)
        gu = at("gu", [P, 2, 2, C], R + 44)
        fe = at("fe", [P, 2, 2, 256], R + 52)
        RQ = at("RQ", [P, 2, D], R)
        RK = at("RK", [P, 2, D], R + 8)
        RO = at("RO", [P, 2, 4, C], R)
        rqT = at("rqT", [P, 8, TOK], R + 16)
        rkT = at("rkT", [P, 8, TOK], R + 24)
        ryTh = at("ryTh", [P, 16, TOK], R + 16, F32R)
        RV = at("RV", [P, 4, 2, C], R + 32)
        ryTl = at("ryTl", [P, 16, TOK], R + 32, F32R)
        RG = at("RG", [P, 4, 2, C], R + 48)
        rtab = at("rtab", [P, 2, 2, 256], R + 64)
        rscT = at("rscT", [P, 4, 384], R + 64)
        rdm = at("rdm", [P, 4, 384], R + 70)
        rtmp = at("rtmp", [P, 2, C], 127)
        rge = at("rge", [P, 2, C], 127)
        hTh = at("hTh", [P, MLPK, TOK], R, F32R)
        hTl = at("hTl", [P, MLPK, TOK], R + 32, F32R)
        hrow = at("hrow", [P, 2, 2, C], R + 64)
        junk = at("junk", [P, D], R + 72)
        junk2 = at("junk2", [P, D], R + 44)
        yg = at("yg", [P, 2, D], R + 64)
        ygr = at("ygr", [P, 2, D], R + 48)
        BQ = at("BQ", [P, 2, 2, C], R)
        BK = at("BK", [P, 2, 2, C], R + 8)
        byTh = at("byTh", [P, 8, TOK], R, F32R)
        byTl = at("byTl", [P, 8, TOK], R + 8, F32R)
        BV = at("BV", [P, 2, 2, C], R + 16)
        bqT = at("bqT", [P, 8, TOK], R + 24)
        bkT = at("bkT", [P, 8, TOK], R + 32)
        bprob = at("bprob", [P, 4, 2, TOK], R + 40)
        bprob2 = at("bprob2", [P, 4, 2, TOK], R + 48)
        bpT = at("bpT", [P, 4, 2, TOK], R + 56)
        btab = at("btab", [P, 2, 2, 16], R + 64)
        btmp = at("btmp", [P, 4, 2, 4, 16], R + 65)

        ps = [ctx.enter_context(nc.psum_tensor(f"ps{i}", [P, C], F32)) for i in range(4)]
        aux = [ctx.enter_context(nc.psum_tensor(f"aux{i}", [P, C], F32)) for i in range(4)]

        def K(name, a=0, b=None):
            o, w = CONST[name]
            return cst[:, o + a:o + (w if b is None else b)]

        def gcol(name, k=0):
            o, _ = GAIN_COLS[name]
            return gains[:, o + k:o + k + 1]

        def S(name, a=0, b=None):
            o, w = SCAL[name]
            return sc[:, o + a:o + (w if b is None else b)]

        ident = K("ident")

        sems = {}

        def sem(name):
            if name not in sems:
                sems[name] = ctx.enter_context(nc.semaphore(name))
            return sems[name]

        landed = [sem(f"landed{i}") for i in range(RING)]
        hi_ready = sem("hi_ready")
        lo_ready = sem("lo_ready")
        gran_used = sem("gran_used")
        half_done = sem("half_done")
        drained = {"act": sem("drained_act"), "dve": sem("drained_dve")}
        aux_ready = [sem(f"aux_ready{i}") for i in range(4)]
        aux_free = [sem(f"aux_free{i}") for i in range(4)]

        x_rows = x_in.rearrange("(t p) d -> p t d", p=P)
        out_rows = out.rearrange("(t p) d -> p t d", p=P)
        mem_rows = mem_in.rearrange("(t p) d -> p t d", p=P)

        block = ctx.enter_context(nc.Block())

        def wait_unit(eng, name, t):
            if t == 0:
                eng.wait_ge(half_done, U[name] + 1)
            else:
                eng.wait_ge(gran_used, GEND[name])

        def wait_drained(eng, name, t):
            eng.wait_ge(drained[DRAIN[name][0]], reads(name, t))

        def ss_count(p, n, t):
            return 2 * t + n + 1 if p == "p4" else 2 * n + t + 1

        def bank(name, t):
            return ps[2 * (U[name] % 2) + t][:, :]

        def wait_aux(eng, name, b=0):
            k, n = AUX[(name, b)]
            eng.wait_ge(aux_ready[k], n)
            return aux[k]

        def wait_read(eng, name, b=0):
            k, n = AUX[(name, b)]
            eng.wait_ge(aux_free[k], n)

        def free(ins, name, b=0):
            return ins.then_inc(aux_free[AUX[(name, b)][0]], 1)

        @block.sync
        def _(sp):
            sp.dma_start(cst[:, 0:P], cpack[:, 0:P]).then_inc(sem("ident_in"), 16)
            sp.dma_start(gains[:, :], gpack).then_inc(sem("gains_in"), 16)
            sp.dma_start(mrows[:, :, 0:C], mem_rows[:, :, 0:C]).then_inc(sem("mem_in0"), 16)
            sp.dma_start(raw[:, 0, :, :], wstream[0]).then_inc(landed[0], 16)
            sp.dma_start(mrows[:, :, C:D], mem_rows[:, :, C:D]).then_inc(sem("mem_in1"), 16)
            sp.dma_start(raw[:, 1, :, :], wstream[1]).then_inc(landed[1], 16)
            sp.dma_start(raw[:, 2, :, :], wstream[2]).then_inc(landed[2], 16)
            sp.dma_start(x[:, :, :], x_rows).then_inc(sem("x_in"), 16)
            sp.dma_start(cst[:, P:], cpack[:, P:]).then_inc(sem("cst_in"), 16)
            sp.dma_start(raw[:, 3, :, :], wstream[3]).then_inc(landed[3], 16)
            by_ring = wstream[0:NG // RING * RING].rearrange("(i j) p k c -> i j p k c", j=RING)
            with sp.Fori(1, NG // RING) as i:
                for j in range(RING):
                    sp.wait_ge(lo_ready, i * RING + (j + 1 - RING))
                    sp.dma_start(raw[:, j, :, :], by_ring[i, j]).then_inc(landed[j], 16)
            for g in range(NG // RING * RING, NG):
                sp.wait_ge(lo_ready, g + 1 - RING)
                sp.dma_start(raw[:, g % RING, :, :], wstream[g]).then_inc(landed[g % RING], 16)
            for t in range(2):
                for n in range(2):
                    sp.wait_ge(sem("x6_rows"), 2 * t + n + 1)
                    sp.dma_start(out_rows[:, t, n * C:(n + 1) * C], x[:, t, n * C:(n + 1) * C]).then_inc(sem("out_done"), 16)
            sp.wait_ge(sem("out_done"), 64)

        @block.gpsimd
        def _(pool):
            def power(key, n):
                pool.wait_ge(sem(f"{key}_var"), 1)
                nc.gpsimd.tensor_tensor(S(f"{key}_rstd", 0, n), S(f"{key}_var", 0, n),
                                        K("minus_half").broadcast_to([P, n]), ALU.pow).then_inc(sem(f"{key}_rstd"), 1)

            def per_head(rows):
                return rows[:, :, :].rearrange("p t (h d) -> p (t h) d", d=HD)

            def times_head(rows, key):
                pool.wait_ge(sem(f"{key}_rstd"), 1)
                v = per_head(rows)
                return nc.gpsimd.tensor_tensor(v, v, S(f"{key}_rstd").unsqueeze(2).broadcast_to([P, 8, HD]), ALU.mult)

            def head_norm(key, unit, rows, before):
                wait_drained(pool, unit, 1)
                if before:
                    pool.wait_ge(sem(before), 1)
                nc.gpsimd.tensor_tensor(sq[:, :, :], rows[:, :, :], rows[:, :, :], ALU.mult).then_inc(sem(f"{key}_sq"), 1)
                power(key, 8)
                times_head(rows, key).then_inc(sem(f"{key}_unit"), 1)

            pool.dma_start(wsm[:, :, :], wsmall).then_inc(sem("small_in"), 16)
            pool.dma_start(wa2[:, :], w_a2).then_inc(sem("small_in"), 16)
            pool.dma_start(brow[:, :], b_a).then_inc(sem("small_in"), 16)
            pool.dma_start(S("b_fox"), b_fox.broadcast_to([P, 4])).then_inc(sem("small_in"), 16)
            pool.wait_ge(sem("cst_in"), 16)
            power("mem", 2)
            power("x0", 2)
            head_norm("mk", "mk", MK, None)
            head_norm("mq", "mq", MQ, "mk_var")
            wait_drained(pool, "gqk", 1)
            wait_read(pool, "cum")
            wait_read(pool, "suf")
            for e in range(3):
                nc.gpsimd.tensor_tensor(gla_e[:, 1 + e, :, :], gla_e[:, 1 + e, :, :],
                                        GQK[:, :, 0:256] if e == 0 else GQK[:, :, 256:512],
                                        ALU.mult).then_inc(sem("gla_in"), 1)
            pool.wait_ge(sem("gg_rec"), 1)
            wait_drained(pool, "gg", 1)
            nc.gpsimd.tensor_tensor(GG[:, :, :], GG[:, :, :], gexp[:, :, :], ALU.mult).then_inc(sem("gg_silu"), 1)
            for t in range(2):
                wait_read(pool, "o", t)
            pool.wait_ge(sem("mq_var"), 1)
            nc.gpsimd.tensor_tensor(sq[:, :, :], go[:, :, :], go[:, :, :], ALU.mult).then_inc(sem("go_sq"), 1)
            power("go", 8)
            pool.wait_ge(sem("gg_silu"), 1)
            nc.gpsimd.tensor_tensor(GG[:, :, :], go[:, :, :], GG[:, :, :], ALU.mult).then_inc(sem("go_gated"), 1)
            pool.wait_ge(sem("go_gated"), 1)
            times_head(GG, "go").then_inc(sem("go_unit"), 1)
            head_norm("fq", "fq", FQ, "go_var")
            head_norm("fk", "fk", FK, "fq_var")
            pool.wait_ge(sem("fk_var"), 1)
            for n in range(2):
                for q, b in enumerate(BRANCHES):
                    k = 3 * n + q
                    if k >= 2:
                        wait_drained(pool, GATES[k - 2], 1)
                    c0 = BRANCH_ROW[b] * D + n * C
                    pool.dma_start(grow[:, (k % 2) * C:(k % 2 + 1) * C], b_gate[:, c0:c0 + C].broadcast_to([P, C]))\
                        .then_inc(sem(f"bias{k % 2}"), 16)
            power("x1", 2)

            def swiglu(n, count):
                pool.wait_ge(sem("lsig_ready"), count + 2)
                gup = gu[:, n % 2, :, 0:256]
                nc.gpsimd.tensor_tensor(gup, gup, gu[:, n % 2, :, 256:512], ALU.mult).then_inc(sem("ff_prod"), 1)
                pool.wait_ge(sem("ff_prod"), count + 1)
                pool.wait_ge(sem("ff_rec"), count + 1)
                nc.gpsimd.tensor_tensor(gup, gup, fe[:, n % 2, :, :], ALU.mult).then_inc(sem("ff_h"), 1)

            swiglu(0, 0)
            with pool.Fori(0, 5) as i:
                for n in (1, 2):
                    swiglu(n, i * 2 + n)
            power("x2", 2)
            pool.wait_ge(gran_used, G["ret0"])
            pool.dma_start(rtab[:, :, :, :], rett).then_inc(sem("rtab_in"), 16)
            pool.dma_start(rdm[:, :, :], dmask).then_inc(sem("rdm_in"), 16)
            for h in range(4):
                wait_drained(pool, f"ret{8 + h}", 1)
                pool.wait_ge(sem("rg_rec"), h + 1)
                nc.gpsimd.tensor_tensor(RG[:, h, :, :], RG[:, h, :, :], rge[:, :, :], ALU.mult).then_inc(sem("rg_silu"), 1)
                if h == 0:
                    power("ro", 8)
            pool.wait_ge(sem("rg_silu"), 4)
            pool.dma_start(grow[:, :], post[0:1, :].broadcast_to([P, D])).then_inc(sem("post_in"), 16)

            def after_mix(p, xk, nxt):
                for t in range(2):
                    pool.wait_ge(sem(f"{p}_var"), t + 1)
                    nc.gpsimd.tensor_tensor(S(f"{p}_rstd", t, t + 1), S(f"{p}_var", t, t + 1),
                                            K("minus_half"), ALU.pow).then_inc(sem(f"{p}_rstd"), 1)
                if nxt is not None:
                    pool.wait_ge(drained["dve"], nxt[1])
                    pool.dma_start(grow[:, :], post[nxt[0]:nxt[0] + 1, :].broadcast_to([P, D])).then_inc(sem("post_in"), 16)
                    power(xk, 2)

            def squares(m):
                def one(n, count):
                    pool.wait_ge(drained["act"], 2 * count + (DRAIN[f"up{m}_0"][1] + 2))
                    h = hrow[:, n % 2, :, :]
                    nc.gpsimd.tensor_tensor(h, h, h, ALU.mult).then_inc(sem(f"h{m}_rows"), 1)
                one(0, 0)
                one(1, 1)
                with pool.Fori(1, 4) as i:
                    for n in range(2):
                        one(n, i * 2 + n)

            after_mix("p2", "x3", (1, reads("reto1", 1)))
            squares(0)
            after_mix("p3", "x4", (2, reads("down0_1", 1)))
            pool.wait_ge(gran_used, G["moba0"])
            pool.dma_start(btab[:, :, :, :], mobat).then_inc(sem("btab_in"), 16)
            pool.wait_ge(sem("btab_in"), 16)

            def rope(k, unit, rows, key):
                wait_drained(pool, unit, 1)
                v = rows.rearrange("p t (h d) -> p t h d", d=HD)
                halves = v[:, :, :, 0:16], v[:, :, :, 16:32]
                cos, sin = (btab[:, :, f, :].unsqueeze(2).broadcast_to([P, 2, 4, 16]) for f in range(2))
                for m, (half, f) in enumerate(((0, cos), (1, sin), (1, cos), (0, sin))):
                    nc.gpsimd.tensor_tensor(btmp[:, m, :, :, :], halves[half], f, ALU.mult).then_inc(sem("rope_part"), 1)
                pool.wait_ge(sem("rope_part"), 4 * k + 4)
                nc.gpsimd.tensor_tensor(halves[0], btmp[:, 0, :, :, :], btmp[:, 1, :, :, :], ALU.subtract).then_inc(sem("rope_half"), 1)
                nc.gpsimd.tensor_tensor(halves[1], btmp[:, 2, :, :, :], btmp[:, 3, :, :, :], ALU.add).then_inc(sem(key), 1)
                pool.wait_ge(sem("rope_half"), k + 1)
                pool.wait_ge(sem(key), k // 2 + 1)

            for j in range(2):
                rope(2 * j, f"moba{2 * j}", BQ[:, j, :, :], "bq_rot")
                rope(2 * j + 1, f"moba{2 * j + 1}", BK[:, j, :, :], "bk_rot")
            after_mix("p4", "x5", (3, reads("mobao1", 1)))
            squares(1)
            after_mix("p5", None, None)

        @block.tensor
        def _(pe):
            def half_granule(slot, th, tl, kts, pair, t, first, last, ready=None):
                for j, kt in enumerate(kts):
                    if ready:
                        ready(kt)
                    for q, (a, w) in enumerate(((th, Wh), (th, Wl), (tl, Wh))):
                        mm = nc.tensor.matmul(ps[2 * pair + t][:, :], a[:, kt, t * P:(t + 1) * P], w[:, slot, j, :],
                                              start=(first and j == 0 and q == 0),
                                              stop=(last and j == len(kts) - 1 and q == 2))
                return mm

            def granule(slot, lo_value, th, tl, kts, pair, first, last, read_out):
                pe.wait_ge(lo_ready, lo_value)
                for t in range(2):
                    if first:
                        read_out(t)
                    mm = half_granule(slot, th, tl, kts, pair, t, first, last)
                    if t == 0 and last:
                        mm.then_inc(half_done, 1)
                mm.then_inc(gran_used, 1)

            def bank_read(name):
                def wait(t):
                    if U[name] >= 2:
                        wait_drained(pe, UNITS[U[name] - 2], t)
                return wait

            def kts_of(name, g):
                k0 = sum(KTS[G[name]:g])
                return range(k0, k0 + KTS[g])

            def product(name, operand, before=None, leave=0):
                th, tl = operand
                for g in range(G[name], GEND[name] - leave):
                    if before and g - G[name] in before:
                        before[g - G[name]]()
                    granule(g % RING, g + 1, th, tl, kts_of(name, g), U[name] % 2, g == G[name], g == GEND[name] - 1,
                            bank_read(name))

            def tile_by_tile(steps, before, steps0=None, ready=None):
                assert len(steps) <= RING
                for t in range(2):
                    for k, (name, g, (th, tl)) in enumerate(steps0 if steps0 and t == 0 else steps):
                        if (t, k) in before:
                            before[(t, k)]()
                        if t == 0:
                            pe.wait_ge(lo_ready, g + 1)
                        if g == G[name]:
                            bank_read(name)(t)
                        mm = half_granule(g % RING, th, tl, kts_of(name, g), U[name] % 2, t, g == G[name], g == GEND[name] - 1,
                                          ready if t == 0 and name == steps[0][0] else None)
                        if t == 1:
                            mm.then_inc(gran_used, 1)
                        elif g == GEND[name] - 1:
                            mm.then_inc(half_done, 1)

            def steps_of(names, operand, last=RING):
                all_of = [(n, g, operand) for n in names for g in range(G[n], GEND[n])]
                return all_of[-last:]

            def open_aux(name, b=0):
                k, n = AUX[(name, b)]
                if n > 1:
                    pe.wait_ge(aux_free[k], n - 1)
                return aux[k]

            def done(ins, name, b=0):
                ins.then_inc(aux_ready[AUX[(name, b)][0]], 1)

            def turn(name, b, blocks):
                o = open_aux(name, b)
                for at, src in blocks:
                    tr = nc.tensor.transpose(o[0:src.shape[1], at:at + P], src, ident)
                done(tr, name, b)

            def turn_rows(name, rows, b):
                turn(name, b, [(kk * TOK + t * P, rows[:, t, (2 * b + kk) * P:(2 * b + kk + 1) * P])
                               for kk in range(2) for t in range(2)])

            def turn_tile(name, rows, ready, t):
                for b in range(2):
                    ready(t, b)
                    turn(name, 2 * t + b, [(j * P, rows[:, t, (4 * b + j) * P:(4 * b + j + 1) * P]) for j in range(4)])

            def next_tile(name, rows, ready, t):
                return lambda: turn_tile(name, rows, ready, t)

            def half_ready(name, b):
                return lambda: wait_operand(name, (b,))

            def begin(names, name, rows, ready):
                tile_by_tile(steps_of(names, (xTh, xTl)),
                             {(0, 0): half_ready(name, 0), (0, 1): half_ready(name, 1), (0, 2): next_tile(name, rows, ready, 1),
                              (1, 0): half_ready(name, 2), (1, 1): half_ready(name, 3)})

            def wait_operand(name, banks):
                for b in banks:
                    wait_read(pe, name, b)

            pe.wait_ge(sem("ident_in"), 16)
            for b in range(4):
                pe.wait_ge(sem(f"mem_in{b // 2}"), 16)
                turn_rows("memT", mrows, b)

            def turn_x():
                wait_operand("memT", (2, 3))
                pe.wait_ge(sem("x_in"), 16)
                for b in range(4):
                    turn_rows("xT", x, b)

            product("mk", (memTh, memTl), before={0: lambda: wait_operand("memT", (0, 1)), 1: turn_x})
            def narrow():
                pe.wait_ge(sem("cst_in"), 16)
                wait_operand("xT", range(4))
                pe.wait_ge(sem("wsm_lo"), 1)
                o = open_aux("small")
                for t in range(2):
                    for k in range(DK):
                        for q, (a, w) in enumerate(((xTh, wsmh), (xTh, wsml), (xTl, wsmh))):
                            mm = nc.tensor.matmul(o[:, 32 * t:32 * t + 20], a[:, k, t * P:(t + 1) * P], w[:, k, :],
                                                  start=(k == 0 and q == 0), stop=(k == DK - 1 and q == 2))
                done(mm, "small")

            product("mv", (memTh, memTl), before={1: narrow})
            pe.wait_ge(sem("ga_rows"), 2)
            turn("gaT", 0, [(t * P, S("ga", 16 * t, 16 * t + 16)) for t in range(2)])
            pe.wait_ge(sem("mk_unit"), 1)
            for b in range(2):
                turn_rows("mkT", MK, b)
            product("mq", (xTh, xTl))
            wait_read(pe, "gaT")
            pe.wait_ge(sem("small_in"), 64)
            o = open_aux("z")
            for t in range(2):
                nc.tensor.matmul(o[:, t * 256:(t + 1) * 256], gaT[:, t * P:(t + 1) * P], wa2[:, :], start=True, stop=False)
                mm = nc.tensor.matmul(o[:, t * 256:(t + 1) * 256], K("ones")[0:1, :], brow[:, :], start=False, stop=True)
            done(mm, "z")
            pe.wait_ge(sem("lf"), 2)
            o = open_aux("foxcum")
            nc.tensor.matmul(o[:, 0:4], K("upto"), S("lf", 0, 4), start=True, stop=True)
            nc.tensor.matmul(o[:, 4:8], K("upto"), S("lf", 4, 8), start=True, stop=False)
            mm = nc.tensor.matmul(o[:, 4:8], K("ones"), S("lf", 0, 4), start=False, stop=True)
            done(mm, "foxcum")
            product("gqk", (xTh, xTl))
            wait_read(pe, "z")
            for name, mat in (("cum", "chunk_upto"), ("suf", "chunk_after")):
                o = open_aux(name)
                for t in range(2):
                    mm = nc.tensor.matmul(o[:, t * 256:(t + 1) * 256], K(mat), gla_e[:, 0, t, :], start=True, stop=True)
                done(mm, name)
            o = open_aux("dec")
            for pr in range(2):
                for t in range(2):
                    mm = nc.tensor.matmul(o[:, 4 * pr + 2 * t:4 * pr + 2 * t + 2], gla_e[:, 0, t, pr * P:(pr + 1) * P],
                                          K("half"), start=True, stop=True)
            done(mm, "dec")
            pe.wait_ge(sem("mq_unit"), 1)
            for b in range(2):
                turn_rows("mqT", MQ, b)
            product("gv", (xTh, xTl))
            for name, e in (("gqT", 1), ("gkT", 2)):
                pe.wait_ge(sem("gla_in"), e)
                turn_rows(name, gla_e[:, e, :, :], 0)
            product("gg", (xTh, xTl))
            wait_read(pe, "gqT")
            wait_read(pe, "gkT")
            for odd in range(2):
                o = open_aux("attn", odd)
                r = 64 * odd
                for t in range(2):
                    for pr in range(2):
                        at0 = (2 * t + pr) * P
                        mm = nc.tensor.matmul(o[:, at0:at0 + P], gkT[r:r + 64, pr, t * P:(t + 1) * P],
                                              gqT[r:r + 64, pr, t * P:(t + 1) * P], start=True, stop=True)
                done(mm, "attn", odd)
            pe.wait_ge(sem("gla_in"), 3)
            wait_drained(pe, "gv", 1)
            for b, chunks in enumerate(((0, 2), (1,))):
                o = open_aux("cs", b)
                for c in chunks:
                    t, s0 = c // 2, 64 * (c % 2)
                    for h in range(4):
                        r, pr = 64 * (h % 2), h // 2
                        at0 = (c // 2) * 256 + pr * P
                        mm = nc.tensor.matmul(o[r:r + 64, at0:at0 + P], gla_e[s0:s0 + 64, 3, t, 64 * h:64 * h + 64],
                                              GV[s0:s0 + 64, t, h * P:(h + 1) * P], start=True, stop=True)
                done(mm, "cs", b)
            product("fq", (xTh, xTl))
            wait_read(pe, "cs", 0)
            for odd in range(2):
                wait_read(pe, "attn", odd)
                o = open_aux("o", odd)
                r = 64 * odd
                for t in range(2):
                    for pr in range(2):
                        h, at0 = 2 * pr + odd, (2 * t + pr) * P
                        nc.tensor.matmul(o[:, at0:at0 + P], gattn[:, odd, 2 * t + pr, :], GV[:, t, h * P:(h + 1) * P],
                                         start=True, stop=False, skip_group_check=True)
                        for half in range(2):
                            c = 2 * t + half
                            if c:
                                i0 = t * P + 64 * half
                                mm = nc.tensor.matmul(o[64 * half:64 * half + 64, at0:at0 + P], gqT[r:r + 64, pr, i0:i0 + 64],
                                                      state[r:r + 64, c - 1, pr, :], start=False, stop=(half == 1),
                                                      skip_group_check=True)
                done(mm, "o", odd)
            product("fk", (xTh, xTl))

            def scores(name, h, qT, kT, h0=0):
                o = open_aux(name, h + h0)
                for t in range(2):
                    mm = nc.tensor.matmul(o[:, t * TOK:(t + 1) * TOK], qT[:, h + h0, t * P:(t + 1) * P], kT[:, h + h0, :],
                                          start=True, stop=True)
                done(mm, name, h + h0)

            def turn_probs(name, h, pr, key, causal=False):
                pe.wait_ge(sem(key), 2 * h + 2)
                turn(name, h, [(ks * TOK + t * P, pr[:, h % 4, t, ks * P:(ks + 1) * P])
                               for ks in range(2) for t in range(2) if not (causal and ks > t)])

            def attend(name, h, v, pT, causal=False):
                o = open_aux(name, h)
                for ks in range(2):
                    q0 = P if causal and ks else 0
                    mm = nc.tensor.matmul(o[:, q0:TOK], v(ks), pT[:, h % 4, ks, q0:TOK], start=(ks == 0), stop=(ks == 1))
                done(mm, name, h)

            wait_operand("mkT", range(2))
            wait_operand("mqT", range(2))
            for h in range(4):
                scores("msc", h, mqT, mkT)
            product("fv", (xTh, xTl))

            def turn_mem():
                for h in range(4):
                    turn_probs("mpT", h, prob, "m_prob")

            product("gate_mem0", (xTh, xTl), before={1: turn_mem})
            wait_drained(pe, "mv", 1)
            for h in range(4):
                wait_read(pe, "mpT", h)
                attend("moT", h, lambda ks: MV[:, ks, h * HD:(h + 1) * HD], mpT)
            pe.wait_ge(sem("fq_unit"), 1)
            for b in range(2):
                turn_rows("fqT", FQ, b)
            pe.wait_ge(sem("fk_unit"), 1)
            for b in range(2):
                turn_rows("fkT", FK, b)

            def turn_gla():
                pe.wait_ge(sem("go_unit"), 1)
                for b in range(2):
                    turn_rows("gyT", GG, b)

            product("gate_gla0", (xTh, xTl), before={1: turn_gla})
            wait_operand("fqT", range(2))
            wait_operand("fkT", range(2))
            pe.wait_ge(sem("nlf"), 1)
            triangle_and_ones = cst[:, CONST["upto"][0]:CONST["upto"][0] + 2 * P]
            for h in range(4):
                o = open_aux("fsc", h)
                lf0 = S("nlf", h, h + 1).broadcast_to([P, P])
                lf1 = S("nlf", 4 + h, 5 + h).broadcast_to([P, P])
                nc.tensor.matmul(o[:, 0:P], fqT[:, h, 0:P], fkT[:, h, 0:P], start=True, stop=False)
                nc.tensor.matmul(o[:, 0:P], lf0, K("upto"), start=False, stop=True)
                nc.tensor.matmul(o[:, TOK:2 * TOK], fqT[:, h, P:TOK], fkT[:, h, :], start=True, stop=False)
                nc.tensor.matmul(o[:, TOK:2 * TOK], lf0, triangle_and_ones, start=False, stop=False)
                mm = nc.tensor.matmul(o[:, TOK + P:2 * TOK], lf1, K("upto"), start=False, stop=True)
                done(mm, "fsc", h)
            product("gate_fox0", (xTh, xTl))
            for h in range(4):
                turn_probs("fpT", h, prob, "f_prob", causal=True)
            wait_operand("moT", range(4))
            product("branch_mem0", yT["mem"])
            wait_drained(pe, "fv", 1)
            for h in range(4):
                wait_read(pe, "fpT", h)
                attend("foT", h, lambda ks: FV[:, ks, h * HD:(h + 1) * HD], fpT, causal=True)
            wait_operand("gyT", range(2))
            product("branch_gla0", yT["gla"])
            wait_operand("foT", range(4))
            product("branch_fox0", yT["fox"])
            for b in BRANCHES:
                product(f"gate_{b}1", (xTh, xTl))
            product("branch_mem1", yT["mem"])

            def rows_ready(name):
                return lambda t, b: pe.wait_ge(sem(f"{name}_rows"), 2 * t + b + 1)

            def merged_ready(t, b):
                pe.wait_ge(sem("merged"), 6 + 2 * t)

            def added(name):
                return lambda t, b: wait_drained(pe, name, t)

            tile_by_tile([("branch_gla1", G["branch_gla1"], yT["gla"]), ("branch_fox1", G["branch_fox1"], yT["fox"])],
                         {(1, 1): next_tile("mgT", merged, merged_ready, 0)})
            tile_by_tile(steps_of(["wout0", "wout1"], (xTh, xTl)),
                         {(0, 0): half_ready("mgT", 0), (0, 1): half_ready("mgT", 1),
                          (0, 2): next_tile("mgT", merged, merged_ready, 1),
                          (1, 0): half_ready("mgT", 2), (1, 1): half_ready("mgT", 3), (1, 2): next_tile("x1T", x, added("wout1"), 0)})

            def ff_unit(n, i=None, between=None):
                name = f"ffn{n}"

                def read_out(t):
                    d = reads(f"ffn{n}", t) - 4
                    pe.wait_ge(drained["act"], d if i is None else i * 4 + d)

                for q in range(2):
                    g = G[name] + q
                    if q and between:
                        between()
                    granule(g % RING, g + 1 if i is None else i * 4 + (g + 1), xTh, xTl, range(4 * q, 4 * q + 4),
                            U[name] % 2, q == 0, q == 1, read_out)

            def ff_turned(n, i=None):
                pe.wait_ge(sem("ff_h"), n + 1 if i is None else i * 2 + (n + 1))
                k, use = AUX[(f"ffT{n}", 0)]
                pe.wait_ge(aux_free[k], use - 1 if i is None else i + (use - 1))
                for kk in range(2):
                    for t in range(2):
                        tr = nc.tensor.transpose(aux[k][:, kk * TOK + t * P:kk * TOK + (t + 1) * P],
                                                 gu[:, n % 2, t, kk * P:(kk + 1) * P], ident)
                tr.then_inc(aux_ready[k], 1)

            begin(["ffn0", "ffn1"], "x1T", x, added("wout1"))
            ff_unit(2, None, lambda: ff_turned(0))
            ff_turned(1)
            with pe.Fori(1, 5) as i:
                for n in (1, 2):
                    ff_unit(n, i)
                    ff_turned(n - 1, i)

            def ff_ready(q):
                def go_on():
                    if q == 1:
                        ff_turned(10)
                    for n in range(2 * q, min(2 * q + 2, FFN // 256)):
                        wait_operand(f"ffT{n}", (0,))
                return go_on

            product("ffd0", (ffTh, ffTl), before={q: ff_ready(q) for q in range(6)})
            product("ffd1", (ffTh, ffTl), leave=RING)
            tile_by_tile(steps_of(["ffd1"], (ffTh, ffTl)), {(1, 1): next_tile("x2T", x, added("ffd1"), 0)})
            begin(["ret0", "ret1"], "x2T", x, added("ffd1"))
            product("ret2", (xTh, xTl))

            def turn_rot(name, rows, key, j):
                pe.wait_ge(sem(key), j + 1)
                for b in range(2):
                    turn(f"{name}{j}", b, [(kk * TOK + t * P, rows[:, t, j * C + (2 * b + kk) * P:j * C + (2 * b + kk + 1) * P])
                                           for kk in range(2) for t in range(2)])

            turn_rot("rqT", RQ, "rq_rot", 0)
            product("ret3", (xTh, xTl))
            turn_rot("rqT", RQ, "rq_rot", 1)
            product("ret4", (xTh, xTl))
            turn_rot("rkT", RK, "rk_rot", 0)
            product("ret5", (xTh, xTl))
            turn_rot("rkT", RK, "rk_rot", 1)
            product("ret6", (xTh, xTl))
            for j in range(2):
                wait_operand(f"rqT{j}", range(2))
                wait_operand(f"rkT{j}", range(2))
            for h in range(4):
                o = open_aux("rsc", h)
                for j, (q0, at0) in enumerate(((0, 0), (P, TOK))):
                    for kk in range(2):
                        mm = nc.tensor.matmul(o[:, at0:at0 + TOK - q0], rkT[:, 2 * h + kk, j * P:(j + 1) * P],
                                              rqT[:, 2 * h + kk, q0:TOK], start=(kk == 0), stop=(kk == 1))
                done(mm, "rsc", h)
            product("ret7", (xTh, xTl))

            def ret_out(h):
                wait_drained(pe, f"ret{4 + h}", 1)
                wait_read(pe, "rsc", h)
                for t in range(2):
                    o = open_aux(f"ro{h}", t)
                    if t == 0:
                        mm = nc.tensor.matmul(o[:, :], rscT[:, h, 0:P], RV[:, h, 0, :], start=True, stop=True)
                    else:
                        nc.tensor.matmul(o[:, :], rscT[:, h, P:TOK], RV[:, h, 0, :], start=True, stop=False)
                        mm = nc.tensor.matmul(o[:, :], rscT[:, h, TOK:384], RV[:, h, 1, :], start=False, stop=True)
                    done(mm, f"ro{h}", t)

            ret_out(0)
            ret_out(1)
            product("ret8", (xTh, xTl))
            ret_out(2)
            ret_out(3)
            product("ret9", (xTh, xTl))
            product("ret10", (xTh, xTl))

            def turn_ret(h):
                pe.wait_ge(sem("ry_rows"), 2 * h + 2)
                for b in range(2):
                    turn(f"ryT{h}", b, [(kk * TOK + t * P, RO[:, t, h, (2 * b + kk) * P:(2 * b + kk + 1) * P])
                                        for kk in range(2) for t in range(2)])

            turn_ret(0)
            product("ret11", (xTh, xTl))
            turn_ret(1)

            def ret_half0(h):
                def go_on():
                    if 1 <= h < 3:
                        turn_ret(h + 1)
                    wait_operand(f"ryT{h}", range(2))
                return go_on

            product("reto0", (ryTh, ryTl), before={h: ret_half0(h) for h in range(4)})
            tile_by_tile(steps_of(["reto1"], (ryTh, ryTl)), {(1, 2): next_tile("x3T", x, rows_ready("x3"), 0)})

            def mlp(m, xname, after):
                begin([f"up{m}_0", f"up{m}_1"], f"{xname}T", x, rows_ready(xname))

                def up(n, i):
                    name = f"up{m}_{n}"

                    def read_out(t):
                        pe.wait_ge(drained["act"], i * 4 + (reads(name, t) - 4))

                    for q in range(2):
                        g = G[name] + q
                        granule(g % RING, i * 4 + (g + 1), xTh, xTl, range(4 * q, 4 * q + 4), U[name] % 2, q == 0, q == 1,
                                read_out)

                def turned(n, i=None):
                    pe.wait_ge(sem(f"h{m}_rows"), n + 1 if i is None else i * 2 + (n + 1))
                    for b in range(2):
                        k, use = AUX[(f"h{m}T{n % 2}", b)]
                        base = use - 1 + (n - n % 2) // 2
                        pe.wait_ge(aux_free[k], base if i is None else i + base)
                        for kk in range(2):
                            for t in range(2):
                                c0 = (2 * b + kk) * P
                                tr = nc.tensor.transpose(aux[k][:, kk * TOK + t * P:kk * TOK + (t + 1) * P],
                                                         hrow[:, n % 2, t, c0:c0 + P], ident)
                        tr.then_inc(aux_ready[k], 1)

                turned(0)
                with pe.Fori(1, 4) as i:
                    up(0, i)
                    turned(-1, i)
                    up(1, i)
                    turned(0, i)

                def before(q):
                    def go_on():
                        if q == 1:
                            turned(7)
                        wait_operand(f"h{m}T{q}", range(2))
                    return go_on

                product(f"down{m}_0", (hTh, hTl), before={q: before(q) for q in range(8)})
                product(f"down{m}_1", (hTh, hTl), leave=RING)
                tile_by_tile(steps_of([f"down{m}_1"], (hTh, hTl)),
                             {(1, 2): next_tile(f"{after}T", x, rows_ready(after), 0)} if after else {})

            mlp(0, "x3", "x4")
            begin(["moba0", "moba1"], "x4T", x, rows_ready("x4"))
            product("moba2", (xTh, xTl))

            def turn_moba(name, rows, key, j):
                pe.wait_ge(sem(key), j + 1)
                for b in range(2):
                    turn_rows(f"{name}{j}", rows[:, j, :, :], b)

            turn_moba("bqT", BQ, "bq_rot", 0)
            turn_moba("bkT", BK, "bk_rot", 0)
            product("moba3", (xTh, xTl))
            wait_operand("bqT0", range(2))
            wait_operand("bkT0", range(2))
            for h in range(4):
                scores("bsc", h, bqT, bkT)

            def turn_second():
                turn_moba("bqT", BQ, "bq_rot", 1)
                turn_moba("bkT", BK, "bk_rot", 1)

            product("moba4", (xTh, xTl), before={1: turn_second})
            for h in range(4):
                turn_probs("bpT", h, bprob, "b_prob")

            def second_scores():
                wait_operand("bqT1", range(2))
                wait_operand("bkT1", range(2))
                for h in range(4):
                    scores("bsc", h, bqT, bkT, 4)

            product("moba5", (xTh, xTl), before={1: second_scores})

            def moba_out(h):
                wait_read(pe, "bpT", h)
                attend("boT", h, lambda ks: BV[:, h // 4, ks, (h % 4) * HD:(h % 4 + 1) * HD], bpT)

            wait_drained(pe, "moba4", 1)
            for h in range(4):
                moba_out(h)

            def second_heads():
                for h in range(4, 8):
                    turn_probs("bpT", h, bprob2, "b_prob")
                wait_drained(pe, "moba5", 1)
                for h in range(4, 8):
                    moba_out(h)

            out_steps = steps_of(["mobao0", "mobao1"], (byTh, byTl))
            tile_by_tile(out_steps, {(0, 2): second_heads, (1, 2): next_tile("x5T", x, rows_ready("x5"), 0)},
                         [out_steps[k] for k in (0, 2, 1, 3)], lambda head: wait_operand("boT", (head,)))
            mlp(1, "x5", None)

        @block.scalar
        def _(act):
            chain = [0]

            def link(ins):
                chain[0] += 1
                ins.then_inc(sem("act_chain"), 1)
                act.wait_ge(sem("act_chain"), chain[0])

            def log_part(rows):
                link(nc.scalar.activation(rows, rows, ACT.Exp, scale=-1.0))
                nc.scalar.activation(rows, rows, ACT.Ln, bias=1.0).then_inc(sem("log_ready"), 1)

            def sigmoid(rows, count, signal):
                act.wait_ge(sem("lsig_ready"), count)
                nc.scalar.activation(rows, rows, ACT.Exp).then_inc(signal, 1)

            def split(g, i=None):
                if g >= NG:
                    return
                slot, nk = g % RING, KTS[g]
                land, used = 16 * (g // RING + 1), g + 1 - RING
                act.wait_ge(landed[slot], land if i is None else i * 16 + land)
                if g >= RING:
                    act.wait_ge(gran_used, used if i is None else i * RING + used)
                nc.scalar.activation(Wh[:, slot, 0:nk, :], raw[:, slot, 0:nk, :], ACT.Copy).then_inc(hi_ready, 1)

            def unit(name, read_out=None, *urgent):
                for g in range(G[name], GEND[name] - 1):
                    split(g + RING)
                if read_out:
                    read_out()
                for step in urgent:
                    step()
                split(GEND[name] - 1 + RING)

            def rows(name, dst, key):
                def go():
                    act.wait_ge(sem(f"{key}_rstd"), 1)
                    for t in range(2):
                        wait_unit(act, name, t)
                        nc.scalar.activation(dst(t), bank(name, t), ACT.Copy,
                                             scale=S(f"{key}_rstd", t, t + 1)).then_inc(drained["act"], 1)
                return go

            def high(name, b, dst, kts, gain=None):
                o = wait_aux(act, name, b)
                if gain is None:
                    nc.scalar.activation(dst[:, kts[0]:kts[-1] + 1, :], o[:, 0:TOK * len(kts)], ACT.Copy)\
                        .then_inc(sem(f"{name}_hi"), 1)
                    return
                for j, kt in enumerate(kts):
                    nc.scalar.activation(dst[:, kt, :], o[:, j * TOK:(j + 1) * TOK], ACT.Copy,
                                         scale=gcol(gain, kt)).then_inc(sem(f"{name}_hi"), 1)

            def high_tile(name, t, dst, gain=None):
                for b in (2 * t, 2 * t + 1):
                    o = wait_aux(act, name, b)
                    k0 = 4 * (b - 2 * t)
                    if gain is None:
                        nc.scalar.activation(dst[:, k0:k0 + 4, t * P:(t + 1) * P], o[:, :].rearrange("p (k t) -> p k t", t=P),
                                             ACT.Copy).then_inc(sem(f"{name}_hi"), 1)
                        continue
                    for j in range(4):
                        nc.scalar.activation(dst[:, k0 + j, t * P:(t + 1) * P], o[:, j * P:(j + 1) * P], ACT.Copy,
                                             scale=gcol(gain, k0 + j)).then_inc(sem(f"{name}_hi"), 1)

            def cross(g, name, gain, squares=None):
                if squares:
                    squares(0)
                split(g)
                high_tile(name, 0, xTh, gain)
                split(g + 1)
                split(g + 2)
                if squares:
                    squares(1)
                split(g + 3)
                high_tile(name, 1, xTh, gain)

            squared = []

            def square(scratch, src, total, signal, count, scale=1.0):
                if squared:
                    act.wait_ge(*squared.pop())
                nc.scalar.activation(scratch, src, ACT.Square, scale=scale, accum_out=total).then_inc(signal, 1)
                squared.append((signal, count))

            def square_sums(key, rows_of, scratch):
                for t in range(2):
                    square(scratch, rows_of[:, t, :], S(f"{key}_ss", t, t + 1), sem(f"{key}_ss"), t + 1)

            nc.scalar.add_instruction(mybir.InstLoadActFuncSet(name=nc.get_next_instruction_name(), act_func_set_id=EXP_AND_LN,
                                                               engine=mybir.EngineType.Activation))
            act.wait_ge(sem("gains_in"), 16)
            for b in range(4):
                if b == 2:
                    split(0)
                high("memT", b, memTh, (2 * b, 2 * b + 1), "g_mem")
            split(1)
            split(2)
            for b in range(4):
                high("xT", b, xTh, (2 * b, 2 * b + 1), "g_mix")
            square_sums("mem", mrows, junk[:, :])
            act.wait_ge(sem("small_in"), 64)
            nc.scalar.activation(wsmh[:, :, :], wsm[:, :, :], ACT.Copy).then_inc(sem("wsm_hi"), 1)
            split(3)
            square_sums("x0", x, junk[:, :])
            unit("mk", rows("mk", lambda t: MK[:, t, :], "mem"))

            def forget_logs():
                wait_read(act, "small")
                link(nc.scalar.activation(S("ffa"), S("ffz"), ACT.Abs))
                link(nc.scalar.activation(S("ffa"), S("ffa"), ACT.Exp, scale=-1.0))
                nc.scalar.activation(S("ffl"), S("ffa"), ACT.Ln, bias=1.0).then_inc(sem("ffl"), 1)

            unit("mv", forget_logs, rows("mv", lambda t: MV[:, t, :], "mem"))
            o = wait_aux(act, "gaT")
            free(nc.scalar.activation(gaT[:, :], o[0:16, 0:TOK], ACT.Copy), "gaT")
            for b in range(2):
                o = wait_aux(act, "mkT", b)
                free(nc.scalar.activation(mkT[:, 2 * b:2 * b + 2, :], o[:, :], ACT.Copy, scale=gcol("g_mk")), "mkT", b)
            unit("mq", rows("mq", lambda t: MQ[:, t, :], "x0"))
            o = wait_aux(act, "z")
            link(nc.scalar.activation(gla_e[:, 1, :, :], o[:, :], ACT.Abs))
            link(nc.scalar.activation(gla_e[:, 2, :, :], gla_e[:, 1, :, :], ACT.Exp, scale=-1.0))
            nc.scalar.activation(gla_e[:, 3, :, :], gla_e[:, 2, :, :], ACT.Ln, bias=1.0).then_inc(sem("gla_l"), 1)
            unit("gqk", rows("gqk", lambda t: GQK[:, t, :], "x0"))
            tau = 1.0 / 16.0
            o = wait_aux(act, "cum")
            nc.scalar.activation(gla_e[:, 1, :, :], o[:, :], ACT.Exp, scale=tau)
            free(nc.scalar.activation(gla_e[:, 2, :, :], o[:, :], ACT.Exp, scale=-tau), "cum")
            o = wait_aux(act, "suf")
            free(nc.scalar.activation(gla_e[:, 3, :, :], o[:, :], ACT.Exp, scale=tau), "suf")
            o = wait_aux(act, "dec")
            free(nc.scalar.activation(S("dec"), o[:, 0:8], ACT.Exp, scale=tau), "dec")
            act.wait_ge(sem("q_gains"), 1)
            for b in range(2):
                o = wait_aux(act, "mqT", b)
                free(nc.scalar.activation(mqT[:, 2 * b:2 * b + 2, :], o[:, :], ACT.Copy, scale=S("gmq_s")), "mqT", b)
            unit("gv", rows("gv", lambda t: GV[:, t, :], "x0"))
            o = wait_aux(act, "gqT")
            free(nc.scalar.activation(gqT[:, :, :], o[:, :], ACT.Copy, scale=64.0 ** -0.5), "gqT")

            def gg_rows():
                act.wait_ge(sem("x0_rstd"), 1)
                for t in range(2):
                    wait_unit(act, "gg", t)
                    nc.scalar.activation(gexp[:, t, :], bank("gg", t), ACT.Abs, scale=S("x0_rstd", t, t + 1))
                    nc.scalar.activation(GG[:, t, :], bank("gg", t), ACT.Copy,
                                         scale=S("x0_rstd", t, t + 1)).then_inc(drained["act"], 1)
                wait_drained(act, "gg", 1)
                log_part(gexp[:, :, :])

            unit("gg", gg_rows)
            sigmoid(gexp[:, :, :], 1, sem("gg_rec"))
            unit("fq", rows("fq", lambda t: FQ[:, t, :], "x0"))
            for t in range(2):
                o = wait_aux(act, "o", t)
                by_parity = go[:, :, :].rearrange("p t (r q c) -> p t r q c", r=2, q=2)
                free(nc.scalar.activation(by_parity[:, :, :, t, :], o[:, :].rearrange("p (t r c) -> p t r c", t=2, r=2),
                                          ACT.Copy), "o", t)
            unit("fk", rows("fk", lambda t: FK[:, t, :], "x0"))

            def exps(k, name, h, pr, src, nm, total):
                act.wait_ge(sem(f"{k}_max"), h + 1)
                for t in range(2):
                    i = nc.scalar.activation(pr[:, h % 4, t, 0:src(t).shape[1]], src(t), ACT.Exp, bias=nm(t), accum_out=total(t))
                    if name == "msc" and t == 1:
                        free(i, name, h)
                    elif name != "msc":
                        i.then_inc(sem(f"{k}_exp"), 1)

            for h in range(4):
                o = aux[AUX[("msc", h)][0]]
                exps("m", "msc", h, prob, lambda t: o[:, t * TOK:(t + 1) * TOK],
                     lambda t: S("ms_nm", 2 * h + t, 2 * h + t + 1), lambda t: S("ms_sum", 2 * h + t, 2 * h + t + 1))
            unit("fv", rows("fv", lambda t: FV[:, t, :], "x0"))

            def probs_T(name, h, dst, causal=False):
                o = wait_aux(act, name, h)
                if causal:
                    nc.scalar.activation(dst[:, h % 4, 0, :], o[:, 0:TOK], ACT.Copy)
                    i = nc.scalar.activation(dst[:, h % 4, 1, P:TOK], o[:, TOK + P:2 * TOK], ACT.Copy)
                else:
                    i = nc.scalar.activation(dst[:, h % 4, :, :], o[:, :], ACT.Copy)
                free(i, name, h)

            def gate_log(b, n, tiles=(0, 1)):
                def go():
                    k = 3 * n + BRANCHES.index(b)
                    for t in tiles:
                        o = bank(f"gate_{b}{n}", t)
                        act.wait_ge(sem("gate_z"), 2 * k + t + 1)
                        link(nc.scalar.activation(o, gate[b][:, t, :], ACT.Abs))
                        link(nc.scalar.activation(o, o, ACT.Exp, scale=-1.0))
                        nc.scalar.activation(o, o, ACT.Ln, bias=1.0).then_inc(sem("gate_log"), 1)
                return go

            def gate_sigmoid(b, n):
                wait_drained(act, f"gate_{b}{n}", 1)
                nc.scalar.activation(gate[b][:, :, :], gate[b][:, :, :], ACT.Exp).then_inc(sem("gate_rec"), 1)

            def mem_high():
                for h in range(4):
                    high("moT", h, yT["mem"][0], (h,))

            def fq_turned():
                act.wait_ge(sem("q_gains"), 2)
                for b in range(2):
                    o = wait_aux(act, "fqT", b)
                    free(nc.scalar.activation(fqT[:, 2 * b:2 * b + 2, :], o[:, :], ACT.Copy, scale=S("gfq_s")), "fqT", b)

            def mem_probs():
                for h in (0, 2):
                    probs_T("mpT", h, mpT)

            unit("gate_mem0", mem_probs, gate_log("mem", 0, (0,)), mem_high, gate_log("mem", 0, (1,)), fq_turned)

            def gla_high():
                for b in range(2):
                    high("gyT", b, yT["gla"][0], (2 * b, 2 * b + 1), "g_gla")
                gate_sigmoid("mem", 0)
                gate_log("gla", 0)()

            unit("gate_gla0", gla_high)
            for h in range(4):
                exps("f", "fsc", h, prob, lambda t: prob[:, h, t, 0:P * (t + 1)],
                     lambda t: S("fs_nm", 2 * h + t, 2 * h + t + 1), lambda t: S("fs_sum", 2 * h + t, 2 * h + t + 1))
            def fox_probs():
                for h in (0, 2):
                    probs_T("fpT", h, fpT, causal=True)

            unit("gate_fox0", lambda: gate_sigmoid("gla", 0), gate_log("fox", 0), fox_probs)
            gate_sigmoid("fox", 0)
            for h in range(4):
                high("foT", h, yT["fox"][0], (h,))
            unit("branch_mem0")
            unit("branch_gla0")
            unit("branch_fox0")
            for b in BRANCHES:
                last = BRANCHES.index(b) - 1
                unit(f"gate_{b}1", lambda: gate_sigmoid(BRANCHES[last], 1) if last >= 0 else None, gate_log(b, 1))
            gate_sigmoid("fox", 1)
            unit("branch_mem1")
            high_tile("mgT", 0, xTh)
            split(G["wout0"] + 2)
            split(G["wout0"] + 3)
            high_tile("mgT", 1, xTh)
            cross(GEND["wout1"], "x1T", "g_ffn")
            wait_drained(act, "wout1", 1)
            square_sums("x1", x, junk[:, :])

            def ff(n, i=None):
                name = f"ffn{n}"
                split(G[name] + RING, i)
                count = n if i is None else i * 2 + n
                if n >= 2 or i is not None:
                    act.wait_ge(sem("ff_h"), count - 1)
                for t in range(2):
                    if t == 0:
                        act.wait_ge(half_done, count + (U["ffn0"] + 1))
                    else:
                        act.wait_ge(gran_used, GEND[name] if i is None else i * RING + GEND[name])
                    o = bank(name, t)
                    nc.scalar.activation(fe[:, n % 2, t, :], o[:, 0:256], ACT.Abs,
                                         scale=S("x1_rstd", t, t + 1)).then_inc(sem("ff_abs"), 1)
                    nc.scalar.activation(gu[:, n % 2, t, :], o[:, :], ACT.Copy,
                                         scale=S("x1_rstd", t, t + 1)).then_inc(drained["act"], 1)
                act.wait_ge(sem("ff_abs"), count * 2 + 2)
                nc.scalar.activation(fe[:, n % 2, :, :], fe[:, n % 2, :, :], ACT.Exp, scale=-1.0).then_inc(sem("ff_exp"), 1)
                act.wait_ge(sem("ff_exp"), count + 1)
                nc.scalar.activation(fe[:, n % 2, :, :], fe[:, n % 2, :, :], ACT.Ln, bias=1.0).then_inc(sem("log_ready"), 1)
                split(GEND[name] - 1 + RING, i)
                act.wait_ge(sem("lsig_ready"), count + 2)
                nc.scalar.activation(fe[:, n % 2, :, :], fe[:, n % 2, :, :], ACT.Exp).then_inc(sem("ff_rec"), 1)

            def ff_high(n, i=None):
                k, use = AUX[(f"ffT{n}", 0)]
                act.wait_ge(aux_ready[k], use if i is None else i + use)
                dst = ffTh[:, :, :].rearrange("p (n k) t -> p n k t", k=2)
                nc.scalar.activation(dst[:, n if i is None else i * 2 + n, :, :], aux[k][:, :], ACT.Copy)\
                    .then_inc(sem("ffT_hi"), 1)

            act.wait_ge(sem("x1_rstd"), 1)
            ff(0)
            ff(1)
            ff_high(0)
            ff(2)
            ff_high(1)
            with act.Fori(1, 5) as i:
                for n in (1, 2):
                    ff(n, i)
                    ff_high(n - 1, i)
            split(G["ffd0"] + RING)
            ff_high(10)
            for g in range(G["ffd0"] + 1, GEND["ffd0"]):
                split(g + RING)
            for g in range(G["ffd1"], GEND["ffd1"] - RING):
                split(g + RING)
            cross(GEND["ffd1"], "x2T", "pre0")
            wait_drained(act, "ffd1", 1)
            square_sums("x2", x, junk2[:, :])
            for j in range(2):
                unit(f"ret{j}", rows(f"ret{j}", lambda t: RQ[:, t, j * C:(j + 1) * C], "x2"))
            unit("ret2", rows("ret2", lambda t: RK[:, t, 0:C], "x2"))

            def rq_turned(j):
                for b in range(2):
                    o = wait_aux(act, f"rqT{j}", b)
                    nc.scalar.activation(rqT[:, 4 * j + 2 * b:4 * j + 2 * b + 2, :], o[:, :], ACT.Copy)\
                        .then_inc(aux_free[AUX[(f"rqT{j}", b)][0]], 1)

            rq_turned(0)
            unit("ret3", rows("ret3", lambda t: RK[:, t, C:D], "x2"))
            rq_turned(1)
            for h in range(4):
                unit(f"ret{4 + h}", rows(f"ret{4 + h}", lambda t: RV[:, h, t, :], "x2"))

            def gate_rows(h):
                def go():
                    act.wait_ge(sem("rk_rot"), 2)
                    if h:
                        act.wait_ge(sem("rg_silu"), h)
                    for t in range(2):
                        wait_unit(act, f"ret{8 + h}", t)
                        o = bank(f"ret{8 + h}", t)
                        nc.scalar.activation(rge[:, t, :], o[:, :], ACT.Abs, scale=S("x2_rstd", t, t + 1))
                        nc.scalar.activation(RG[:, h, t, :], o[:, :], ACT.Copy,
                                             scale=S("x2_rstd", t, t + 1)).then_inc(drained["act"], 1)
                    if h < 3:
                        gate_log_rows(h)
                return go

            def gate_log_rows(h):
                wait_drained(act, f"ret{8 + h}", 1)
                log_part(rge[:, :, :])

            def ret_rows(h):
                for t in range(2):
                    o = wait_aux(act, f"ro{h}", t)
                    nc.scalar.activation(RO[:, t, h, :], o[:, :], ACT.Copy)
                    k, n = AUX[(f"ro{h}", t)]
                    square(junk[:, 0:C], o[:, :], S("ro_ss", 2 * h + t, 2 * h + t + 1), aux_free[k], n)

            act.wait_ge(sem("x2_rstd"), 1)
            for h in range(4):
                wait_read(act, "rsc", h)
            ret_rows(0)
            ret_rows(1)
            unit("ret8", gate_rows(0))
            sigmoid(rge[:, :, :], 13, sem("rg_rec"))
            ret_rows(2)
            ret_rows(3)
            unit("ret9", gate_rows(1))
            sigmoid(rge[:, :, :], 14, sem("rg_rec"))
            unit("ret10", gate_rows(2))
            sigmoid(rge[:, :, :], 15, sem("rg_rec"))

            def ry_high(h):
                for b in range(2):
                    k, use = AUX[(f"ryT{h}", b)]
                    act.wait_ge(aux_ready[k], use)
                    nc.scalar.activation(ryTh[:, 4 * h + 2 * b:4 * h + 2 * b + 2, :], aux[k][:, :], ACT.Copy)\
                        .then_inc(sem("ryT_hi"), 1)

            ry_high(0)
            unit("ret11", gate_rows(3), lambda: ry_high(1), lambda: gate_log_rows(3))
            sigmoid(rge[:, :, :], 16, sem("rg_rec"))
            for h in range(4):
                if 1 <= h < 3:
                    ry_high(h + 1)
                if h < 3:
                    split(G["reto0"] + h + RING)

            def down_squares(p, name, n, tiles=(0, 1)):
                for t in tiles:
                    wait_unit(act, name, t)
                    square(junk[:, 0:C], bank(name, t), S(f"{p}_ss", 2 * t + n, 2 * t + n + 1), sem(f"{p}_ss"), ss_count(p, n, t),
                           scale=D ** -0.5)

            down_squares("p2", "reto0", 0)
            split(G["reto0"] + 3 + RING)
            cross(GEND["reto1"], "x3T", "mpre0", lambda t: down_squares("p2", "reto1", 1, (t,)))

            def mlp(m, xname, p, after, gain):
                act.wait_ge(sem(f"{xname}_rows"), 4)
                square_sums(xname, x, junk[:, :])

                def up(n, i=None):
                    name = f"up{m}_{n}"
                    split(G[name] + RING, i)
                    count = n if i is None else i * 2 + n
                    for t in range(2):
                        if t == 0:
                            act.wait_ge(half_done, count + (U[f"up{m}_0"] + 1))
                        else:
                            act.wait_ge(gran_used, GEND[name] if i is None else i * RING + GEND[name])
                        nc.scalar.activation(hrow[:, n % 2, t, :], bank(name, t), ACT.Relu,
                                             scale=S(f"{xname}_rstd", t, t + 1)).then_inc(drained["act"], 1)
                    split(GEND[name] - 1 + RING, i)

                def h_high(n, i=None):
                    dst = hTh[:, :, :].rearrange("p (n b k) t -> p n b k t", b=2, k=2)
                    for b in range(2):
                        k, use = AUX[(f"h{m}T{n % 2}", b)]
                        use += (n - n % 2) // 2
                        act.wait_ge(aux_ready[k], use if i is None else i + use)
                        nc.scalar.activation(dst[:, n if i is None else i * 2 + n, b, :, :], aux[k][:, :], ACT.Copy)\
                            .then_inc(sem(f"h{m}T_hi"), 1)

                act.wait_ge(sem(f"{xname}_rstd"), 1)
                up(0)
                up(1)
                h_high(0)
                with act.Fori(1, 4) as i:
                    up(0, i)
                    h_high(-1, i)
                    up(1, i)
                    h_high(0, i)
                split(G[f"down{m}_0"] + RING)
                h_high(7)
                for g in range(G[f"down{m}_0"] + 1, GEND[f"down{m}_0"] - 1):
                    split(g + RING)
                down_squares(p, f"down{m}_0", 0)
                split(GEND[f"down{m}_0"] - 1 + RING)
                for g in range(G[f"down{m}_1"], GEND[f"down{m}_1"] - RING):
                    split(g + RING)
                if after:
                    cross(GEND[f"down{m}_1"], f"{after}T", gain, lambda t: down_squares(p, f"down{m}_1", 1, (t,)))
                else:
                    down_squares(p, f"down{m}_1", 1)

            mlp(0, "x3", "p3", "x4", "pre1")
            act.wait_ge(sem("x4_rows"), 4)
            square_sums("x4", x, junk[:, :])
            unit("moba0", rows("moba0", lambda t: BQ[:, 0, t, :], "x4"))
            unit("moba1", rows("moba1", lambda t: BK[:, 0, t, :], "x4"))
            unit("moba2", rows("moba2", lambda t: BQ[:, 1, t, :], "x4"))

            def bq_turned(j):
                for b in range(2):
                    o = wait_aux(act, f"bqT{j}", b)
                    free(nc.scalar.activation(bqT[:, 4 * j + 2 * b:4 * j + 2 * b + 2, :], o[:, :], ACT.Copy,
                                              scale=float(HD) ** -0.5), f"bqT{j}", b)

            bq_turned(0)
            unit("moba3", rows("moba3", lambda t: BK[:, 1, t, :], "x4"))

            def moba_exps(h):
                pr = bprob if h < 4 else bprob2
                act.wait_ge(sem("b_max"), h + 1)
                nc.scalar.activation(S("bs_b", 2 * h, 2 * h + 2), S("bs_b", 2 * h, 2 * h + 2), ACT.Exp).then_inc(sem("b_past"), 1)
                for t in range(2):
                    k = 2 * h + t
                    nc.scalar.activation(pr[:, h % 4, t, :], pr[:, h % 4, t, :], ACT.Exp, bias=S("bs_nm", k, k + 1),
                                         accum_out=S("bs_sum", k, k + 1)).then_inc(sem("b_exp"), 1)

            for h in range(4):
                moba_exps(h)

            def second_turned():
                bq_turned(1)
                rows("moba4", lambda t: BV[:, 0, t, :], "x4")()

            unit("moba4", second_turned)

            def moba_probs(hs):
                for h in hs:
                    if h >= 4:
                        wait_aux(act, "boT", h - 4)
                    probs_T("bpT", h, bpT)

            moba_probs((0, 2))

            def second_exps():
                moba_exps(4)
                moba_exps(5)
                rows("moba5", lambda t: BV[:, 1, t, :], "x4")()

            def first_high():
                for h in range(4):
                    high("boT", h, byTh, (h,))

            unit("moba5", second_exps, lambda: moba_exps(6), first_high, lambda: moba_exps(7))
            moba_probs((4, 6))
            for h in range(4, 8):
                high("boT", h, byTh, (h,))

            def out_squares(t):
                for n in range(2):
                    down_squares("p4", f"mobao{n}", n, (t,))

            cross(GEND["mobao1"], "x5T", "mpre1", out_squares)
            mlp(1, "x5", "p5", None, None)

        @block.vector
        def _(dve):
            chain = [0]

            def link(ins):
                chain[0] += 1
                ins.then_inc(sem("dve_chain"), 1)
                dve.wait_ge(sem("dve_chain"), chain[0])

            def split(g, i=None):
                if g >= NG:
                    return
                slot, nk = g % RING, KTS[g]
                dve.wait_ge(hi_ready, g + 1 if i is None else i * RING + (g + 1))
                nc.vector.tensor_tensor(Wl[:, slot, 0:nk, :], raw[:, slot, 0:nk, :], Wh[:, slot, 0:nk, :].bitcast(F32),
                                        ALU.subtract).then_inc(lo_ready, 1)

            def unit(name, read_out=None, *urgent):
                for g in range(G[name], GEND[name] - 1):
                    split(g + RING)
                if read_out:
                    read_out()
                for step in urgent:
                    step()
                split(GEND[name] - 1 + RING)

            def low(name, b, dst, hi, kts, gain=None):
                k, _ = AUX[(name, b)]
                o = aux[k]
                hb = f32(hi)
                if gain is None:
                    dve.wait_ge(sem(f"{name}_hi"), b + 1)
                    i = nc.vector.tensor_tensor(dst[:, kts[0]:kts[-1] + 1, :], per_kt(o, len(kts)), hb[:, kts[0]:kts[-1] + 1, :],
                                                ALU.subtract)
                else:
                    dve.wait_ge(sem(f"{name}_hi"), kts[-1] + 1)
                    for j, kt in enumerate(kts):
                        i = nc.vector.scalar_tensor_tensor(out=dst[:, kt, :], in0=o[:, j * TOK:(j + 1) * TOK],
                                                           scalar=gcol(gain, kt), in1=hb[:, kt, :],
                                                           op0=ALU.mult, op1=ALU.subtract)
                i.then_inc(aux_free[k], 1)

            def f32(t):
                return t[:, :, :].bitcast(F32)

            def low_tile(name, t, dst, hi, gain=None):
                at_t = slice(t * P, (t + 1) * P)
                for b in (2 * t, 2 * t + 1):
                    k, _ = AUX[(name, b)]
                    k0 = 4 * (b - 2 * t)
                    dve.wait_ge(sem(f"{name}_hi"), b + 1 if gain is None else 4 * (b + 1))
                    if gain is None:
                        i = nc.vector.tensor_tensor(dst[:, k0:k0 + 4, at_t], aux[k][:, :].rearrange("p (k t) -> p k t", t=P),
                                                    f32(hi)[:, k0:k0 + 4, at_t], ALU.subtract)
                    else:
                        for j in range(4):
                            i = nc.vector.scalar_tensor_tensor(out=dst[:, k0 + j, at_t], in0=aux[k][:, j * P:(j + 1) * P],
                                                               scalar=gcol(gain, k0 + j), in1=f32(hi)[:, k0 + j, at_t],
                                                               op0=ALU.mult, op1=ALU.subtract)
                    i.then_inc(aux_free[k], 1)

            def cross(g, name, gain, rows):
                rows(0)
                split(g)
                low_tile(name, 0, xTl, xTh, gain)
                split(g + 1)
                split(g + 2)
                rows(1)
                split(g + 3)
                low_tile(name, 1, xTl, xTh, gain)

            def per_kt(o, n):
                return o[:, 0:n * TOK].rearrange("p (k t) -> p k t", t=TOK)

            def power_in(key, n, width, need):
                dve.wait_ge(sem(f"{key}_ss"), need)
                nc.vector.tensor_scalar(S(f"{key}_var", 0, n), S(f"{key}_ss", 0, n), 1.0 / width, EPS, ALU.mult, ALU.add)\
                    .then_inc(sem(f"{key}_var"), 1)

            def head_sums(key):
                dve.wait_ge(sem(f"{key}_sq"), 1)
                link(nc.vector.tensor_reduce(S(f"{key}_ss"), sq[:, :, :].rearrange("p t (h d) -> p (t h) d", d=HD), AX.X, ALU.add))
                nc.vector.tensor_scalar(S(f"{key}_var"), S(f"{key}_ss"), 1.0 / HD, EPS, ALU.mult, ALU.add)\
                    .then_inc(sem(f"{key}_var"), 1)

            def log_sigmoid(rows, z, count):
                dve.wait_ge(sem("log_ready"), count)
                nc.vector.scalar_tensor_tensor(out=rows, in0=z, scalar=0.0, in1=rows, op0=ALU.min, op1=ALU.subtract)\
                    .then_inc(sem("lsig_ready"), 1)

            def x_stats(k):
                power_in(k, 2, D, 2)

            def turned(name, b, dst, scale=None):
                o = wait_aux(dve, name, b)
                if scale is None:
                    free(nc.vector.tensor_copy(dst, o[:, :]), name, b)
                else:
                    free(nc.vector.tensor_scalar(dst, o[:, :], scale, None, ALU.mult), name, b)

            dve.wait_ge(sem("gains_in"), 16)
            for b in range(4):
                if b == 2:
                    split(0)
                low("memT", b, memTl, memTh, (2 * b, 2 * b + 1), "g_mem")
            split(1)
            split(2)
            for b in range(4):
                low("xT", b, xTl, xTh, (2 * b, 2 * b + 1), "g_mix")
            power_in("mem", 2, D, 2)
            dve.wait_ge(sem("wsm_hi"), 1)
            nc.vector.tensor_tensor(wsml[:, :, :], wsm[:, :, :], f32(wsmh), ALU.subtract).then_inc(sem("wsm_lo"), 1)
            split(3)
            nc.vector.tensor_scalar(S("gmq_s"), gcol("g_mq"), float(HD) ** -0.5, None, ALU.mult).then_inc(sem("q_gains"), 1)
            nc.vector.tensor_scalar(S("gfq_s"), gcol("g_fq"), float(HD) ** -0.5, None, ALU.mult).then_inc(sem("q_gains"), 1)
            x_stats("x0")
            unit("mk")
            head_sums("mk")

            def narrow():
                o = wait_aux(dve, "small")
                dve.wait_ge(sem("small_in"), 64)
                dve.wait_ge(sem("x0_rstd"), 1)
                for t in range(2):
                    nc.vector.tensor_scalar(S("ga", 16 * t, 16 * t + 16), o[:, 32 * t:32 * t + 16], S("x0_rstd", t, t + 1), None,
                                            ALU.mult).then_inc(sem("ga_rows"), 1)
                for t in range(2):
                    i = nc.vector.scalar_tensor_tensor(out=S("ffz", 4 * t, 4 * t + 4), in0=o[:, 32 * t + 16:32 * t + 20],
                                                       scalar=S("x0_rstd", t, t + 1), in1=S("b_fox"), op0=ALU.mult, op1=ALU.add)
                    if t == 1:
                        free(i, "small")
                dve.wait_ge(sem("ffl"), 1)
                nc.vector.scalar_tensor_tensor(out=S("lf"), in0=S("ffz"), scalar=0.0, in1=S("ffl"), op0=ALU.min,
                                               op1=ALU.subtract).then_inc(sem("lf"), 2)
                dve.wait_ge(sem("lf"), 2)
                nc.vector.tensor_scalar(S("nlf"), S("lf"), -1.0, None, ALU.mult).then_inc(sem("nlf"), 1)

            unit("mv", narrow)
            unit("mq")
            head_sums("mq")
            dve.wait_ge(sem("gla_l"), 1)
            o = wait_aux(dve, "z")
            free(nc.vector.scalar_tensor_tensor(out=gla_e[:, 0, :, :].rearrange("p t c -> p (t c)"), in0=o[:, :], scalar=0.0,
                                                in1=gla_e[:, 3, :, :].rearrange("p t c -> p (t c)"),
                                                op0=ALU.min, op1=ALU.subtract), "z")
            o = wait_aux(dve, "foxcum")
            free(nc.vector.tensor_copy(S("foxc"), o[:, 0:8]), "foxcum")
            nc.vector.memset(gattn[:, :, :, :], 0.0).then_inc(sem("gattn_zero"), 1)
            unit("gqk")
            unit("gv")
            turned("gkT", 0, gkT[:, :, :])
            unit("gg", lambda: log_sigmoid(gexp[:, :, :], GG[:, :, :], 1))
            dve.wait_ge(sem("gattn_zero"), 1)
            mask = K("chunk_upto").bitcast(U32).unsqueeze(1).broadcast_to([P, 4, P])
            for t in range(2):
                o = wait_aux(dve, "attn", t)
                free(nc.vector.copy_predicated(gattn[:, t, :, :], mask, o[:, :].rearrange("p (h i) -> p h i", h=4)), "attn", t)
            wait_read(dve, "dec")
            o = wait_aux(dve, "cs", 0)
            nc.vector.tensor_copy(state[:, 0, :, :], o[:, 0:256]).then_inc(sem("gla_state"), 1)
            dve.wait_ge(sem("gla_state"), 1)
            for c in (1, 2):
                o = wait_aux(dve, "cs", 2 - c)
                if c == 2:
                    dve.wait_ge(sem("gla_step"), 1)
                for pr in range(2):
                    at0 = (c // 2) * 256 + pr * P
                    i = nc.vector.scalar_tensor_tensor(out=state[:, c, pr, :], in0=state[:, c - 1, pr, :],
                                                       scalar=S("dec", 4 * pr + c, 4 * pr + c + 1), in1=o[:, at0:at0 + P],
                                                       op0=ALU.mult, op1=ALU.add)
                    if pr == 1:
                        free(i, "cs", 2 - c)
                if c == 1:
                    wait_read(dve, "cs", 1)
                    nc.vector.memset(S("ffa"), 0.0).then_inc(sem("gla_step"), 1)
            unit("fq")
            head_sums("go")
            head_sums("fq")
            unit("fk")
            head_sums("fk")
            for h in range(4):
                o = wait_aux(dve, "msc", h)
                nc.vector.tensor_reduce(S("ms_nm", 2 * h, 2 * h + 2), o[:, :].rearrange("p (t k) -> p t k", t=2), AX.X, ALU.max,
                                        negate=True).then_inc(sem("m_max"), 1)

            def normed(k, h, pr, rec, total, widths):
                link(nc.vector.reciprocal(rec(0, 2), total(0, 2)))
                for t in range(2):
                    v = pr[:, h % 4, t, 0:widths[t]]
                    nc.vector.tensor_scalar(v, v, rec(t, t + 1), None, ALU.mult).then_inc(sem(f"{k}_prob"), 1)

            for h in range(4):
                wait_read(dve, "msc", h)
                normed("m", h, prob, lambda a, b: S("ms_rec", 2 * h + a, 2 * h + b),
                       lambda a, b: S("ms_sum", 2 * h + a, 2 * h + b), (TOK, TOK))
            unit("fv")

            def gate_rows(b, n):
                def go():
                    k = 3 * n + BRANCHES.index(b)
                    dve.wait_ge(sem(f"bias{k % 2}"), 16 * (k // 2 + 1))
                    for t in range(2):
                        wait_unit(dve, f"gate_{b}{n}", t)
                        nc.vector.scalar_tensor_tensor(out=gate[b][:, t, :], in0=bank(f"gate_{b}{n}", t),
                                                       scalar=S("x0_rstd", t, t + 1), in1=grow[:, (k % 2) * C:(k % 2 + 1) * C],
                                                       op0=ALU.mult, op1=ALU.add).then_inc(sem("gate_z"), 1)
                    for t in (0, 1) if (b, n) != ("mem", 0) else (0,):
                        gate_lsig(b, n, t)
                return go

            def gate_lsig(b, n, t):
                dve.wait_ge(sem("gate_log"), 2 * (3 * n + BRANCHES.index(b)) + t + 1)
                nc.vector.scalar_tensor_tensor(out=gate[b][:, t, :], in0=gate[b][:, t, :], scalar=0.0,
                                               in1=bank(f"gate_{b}{n}", t), op0=ALU.min,
                                               op1=ALU.subtract).then_inc(drained["dve"], 1)

            def branch_rows(b, n):
                def go(tiles=(0, 1)):
                    dve.wait_ge(sem("gate_rec"), 3 * n + BRANCHES.index(b) + 1)
                    for t in tiles:
                        wait_unit(dve, f"branch_{b}{n}", t)
                        m = merged[:, t, n * C:(n + 1) * C]
                        dst = m if b == "mem" else gate[b][:, t, :]
                        i = nc.vector.tensor_tensor(dst, bank(f"branch_{b}{n}", t), gate[b][:, t, :], ALU.mult)
                        i.then_inc(drained["dve"], 1)
                        if b != "mem":
                            wait_drained(dve, f"branch_{b}{n}", t)
                            if b == "fox":
                                dve.wait_ge(sem("merged"), 5 + 2 * t if n else 1 + t)
                            nc.vector.tensor_tensor(m, m, gate[b][:, t, :], ALU.add).then_inc(sem("merged"), 1)
                        if b == "mem":
                            wait_drained(dve, f"branch_{b}{n}", t)
                return go

            def mem_low():
                for h in range(4):
                    low("moT", h, yT["mem"][1], yT["mem"][0], (h,))

            def fk_turned():
                for b in range(2):
                    turned("fkT", b, fkT[:, 2 * b:2 * b + 2, :], gcol("g_fk"))

            def mem_probs():
                for h in (1, 3):
                    turned("mpT", h, mpT[:, h, :, :])
                gate_rows("mem", 0)()

            unit("gate_mem0", mem_probs, mem_low, lambda: gate_lsig("mem", 0, 1), fk_turned)

            def gla_low():
                for b in range(2):
                    low("gyT", b, yT["gla"][1], yT["gla"][0], (2 * b, 2 * b + 1), "g_gla")
                gate_rows("gla", 0)()

            unit("gate_gla0", gla_low)
            for h in range(4):
                o = wait_aux(dve, "fsc", h)
                nc.vector.scalar_tensor_tensor(out=prob[:, h, 0, 0:P], in0=o[:, 0:P], scalar=S("foxc", h, h + 1),
                                               in1=K("tri_mask"), op0=ALU.add, op1=ALU.add)
                free(nc.vector.scalar_tensor_tensor(out=prob[:, h, 1, :], in0=o[:, TOK:2 * TOK], scalar=S("foxc", 4 + h, 5 + h),
                                                    in1=cst[:, CONST["zero_mask"][0]:CONST["zero_mask"][0] + TOK],
                                                    op0=ALU.add, op1=ALU.add), "fsc", h)
                wait_read(dve, "fsc", h)
                nc.vector.tensor_reduce(S("fs_nm", 2 * h, 2 * h + 1), prob[:, h, 0, 0:P], AX.X, ALU.max, negate=True)
                nc.vector.tensor_reduce(S("fs_nm", 2 * h + 1, 2 * h + 2), prob[:, h, 1, :], AX.X, ALU.max, negate=True)\
                    .then_inc(sem("f_max"), 1)
            for h in range(4):
                dve.wait_ge(sem("f_exp"), 2 * h + 2)
                normed("f", h, prob, lambda a, b: S("fs_rec", 2 * h + a, 2 * h + b),
                       lambda a, b: S("fs_sum", 2 * h + a, 2 * h + b), (P, TOK))
            def fox_probs():
                for h in (1, 3):
                    o = wait_aux(dve, "fpT", h)
                    nc.vector.tensor_copy(fpT[:, h, 0, :], o[:, 0:TOK])
                    free(nc.vector.tensor_copy(fpT[:, h, 1, P:TOK], o[:, TOK + P:2 * TOK]), "fpT", h)

            unit("gate_fox0", gate_rows("fox", 0), fox_probs)
            for h in range(4):
                low("foT", h, yT["fox"][1], yT["fox"][0], (h,))
            unit("branch_mem0", branch_rows("mem", 0))
            unit("branch_gla0", branch_rows("gla", 0))
            unit("branch_fox0", branch_rows("fox", 0))
            for b in BRANCHES:
                unit(f"gate_{b}1", gate_rows(b, 1))
            unit("branch_mem1", branch_rows("mem", 1))

            def last_terms(t):
                branch_rows("gla", 1)((t,))
                branch_rows("fox", 1)((t,))

            last_terms(0)
            low_tile("mgT", 0, xTl, xTh)
            split(G["wout0"] + 2)
            last_terms(1)
            split(G["wout0"] + 3)
            low_tile("mgT", 1, xTl, xTh)

            def add_rows(name, n):
                def go(tiles=(0, 1)):
                    for t in tiles:
                        wait_unit(dve, name, t)
                        v = x[:, t, n * C:(n + 1) * C]
                        nc.vector.tensor_tensor(v, bank(name, t), v, ALU.add).then_inc(drained["dve"], 1)
                return go

            def mixed(t):
                for n in range(2):
                    add_rows(f"wout{n}", n)((t,))

            cross(GEND["wout1"], "x1T", "g_ffn", mixed)
            x_stats("x1")

            def ff(n, i=None):
                name = f"ffn{n}"
                split(G[name] + RING, i)
                log_sigmoid(fe[:, n % 2, :, :], gu[:, n % 2, :, 0:256], n + 2 if i is None else i * 2 + (n + 2))
                split(GEND[name] - 1 + RING, i)

            def ff_low(n, i=None):
                k, use = AUX[(f"ffT{n}", 0)]
                count = n if i is None else i * 2 + n
                dve.wait_ge(sem("ffT_hi"), count + 1)
                lo = ffTl[:, :, :].rearrange("p (n k) t -> p n k t", k=2)
                hi = f32(ffTh).rearrange("p (n k) t -> p n k t", k=2)
                nc.vector.tensor_tensor(lo[:, count, :, :], per_kt(aux[k], 2), hi[:, count, :, :], ALU.subtract)\
                    .then_inc(aux_free[k], 1)

            ff(0)
            ff(1)
            ff_low(0)
            ff(2)
            ff_low(1)
            with dve.Fori(1, 5) as i:
                for n in (1, 2):
                    ff(n, i)
                    ff_low(n - 1, i)
            split(G["ffd0"] + RING)
            ff_low(10)
            for g in range(G["ffd0"] + 1, GEND["ffd0"] - 1):
                split(g + RING)
            add_rows("ffd0", 0)()
            split(GEND["ffd0"] - 1 + RING)
            for g in range(G["ffd1"], GEND["ffd1"] - RING):
                split(g + RING)
            cross(GEND["ffd1"], "x2T", "pre0", lambda t: add_rows("ffd1", 1)((t,)))
            x_stats("x2")
            dve.wait_ge(sem("rtab_in"), 16)

            def rotate(rows, j, key):
                def go():
                    wait_drained(dve, f"ret{j + (2 if key == 'rk_rot' else 0)}", 1)
                    xs = rows[:, :, j * C:(j + 1) * C].rearrange("p t (h c) -> p t h c", c=256)
                    ts = rtmp[:, :, :].rearrange("p t (h c) -> p t h c", c=256)
                    sn = rtab[:, :, 1, :].unsqueeze(2).broadcast_to([P, 2, 2, 256])
                    cs = rtab[:, :, 0, :].unsqueeze(2).broadcast_to([P, 2, 2, 256])
                    for t in range(2):
                        nc.vector.tensor_tensor(ts[:, t, :, 0::2], xs[:, t, :, 1::2], sn[:, t, :, 0::2], ALU.mult)
                        i = nc.vector.tensor_tensor(ts[:, t, :, 1::2], xs[:, t, :, 0::2], sn[:, t, :, 1::2], ALU.mult)
                    link(i)
                    link(nc.vector.tensor_tensor(xs, xs, cs, ALU.mult))
                    nc.vector.tensor_tensor(xs, xs, ts, ALU.add).then_inc(sem(key), 1)
                    dve.wait_ge(sem(key), j + 1)
                return go

            def rk_turned(j):
                for b in range(2):
                    turned(f"rkT{j}", b, rkT[:, 4 * j + 2 * b:4 * j + 2 * b + 2, :], 256.0 ** -0.5)

            unit("ret0", rotate(RQ, 0, "rq_rot"))
            unit("ret1", rotate(RQ, 1, "rq_rot"))
            unit("ret2", rotate(RK, 0, "rk_rot"))
            unit("ret3", rotate(RK, 1, "rk_rot"))
            unit("ret4")
            rk_turned(0)
            unit("ret5")
            rk_turned(1)
            unit("ret6")
            dve.wait_ge(sem("rdm_in"), 16)
            for h in range(4):
                o = wait_aux(dve, "rsc", h)
                free(nc.vector.tensor_tensor(rscT[:, h, :], o[:, 0:384], rdm[:, h, :], ALU.mult), "rsc", h)
            unit("ret7")

            def ry_rows(h):
                dve.wait_ge(sem("rg_silu"), h + 1)
                for t in range(2):
                    nc.vector.scalar_tensor_tensor(out=RO[:, t, h, :], in0=RO[:, t, h, :],
                                                   scalar=S("ro_rstd", 2 * h + t, 2 * h + t + 1), in1=RG[:, h, t, :],
                                                   op0=ALU.mult, op1=ALU.mult).then_inc(sem("ry_rows"), 1)

            def ry_low(h):
                for b in range(2):
                    k, _ = AUX[(f"ryT{h}", b)]
                    dve.wait_ge(sem("ryT_hi"), 2 * h + b + 1)
                    kt = 4 * h + 2 * b
                    nc.vector.tensor_tensor(ryTl[:, kt:kt + 2, :], per_kt(aux[k], 2), f32(ryTh)[:, kt:kt + 2, :],
                                            ALU.subtract).then_inc(aux_free[k], 1)

            unit("ret8", lambda: log_sigmoid(rge[:, :, :], RG[:, 0, :, :], 13))
            for h in range(4):
                for t in range(2):
                    wait_read(dve, f"ro{h}", t)
            nc.vector.tensor_scalar(S("ro_var"), S("ro_ss"), 1.0 / C, EPS, ALU.mult, ALU.add).then_inc(sem("ro_var"), 1)
            unit("ret9", lambda: log_sigmoid(rge[:, :, :], RG[:, 1, :, :], 14))
            dve.wait_ge(sem("ro_rstd"), 1)
            ry_rows(0)
            unit("ret10", lambda: log_sigmoid(rge[:, :, :], RG[:, 2, :, :], 15))
            ry_rows(1)
            ry_low(0)
            ry_rows(2)
            unit("ret11", lambda: ry_low(1), lambda: log_sigmoid(rge[:, :, :], RG[:, 3, :, :], 16))
            ry_rows(3)
            for h in range(3):
                if h < 2:
                    ry_low(h + 2)
                split(G["reto0"] + h + RING)

            def gained(p, name, n, k):
                def go(tiles=(0, 1)):
                    dve.wait_ge(sem("post_in"), 16 * k)
                    for t in tiles:
                        dve.wait_ge(sem(f"{p}_ss"), ss_count(p, n, t))
                        nc.vector.tensor_tensor(ygs(p)[:, t, n * C:(n + 1) * C], bank(name, t), grow[:, n * C:(n + 1) * C],
                                                ALU.mult).then_inc(drained["dve"], 1)
                return go

            def ygs(p):
                return ygr if p in ("p2", "p4") else yg

            def residual(p, name, xname, tiles=(0, 1)):
                for t in tiles:
                    dve.wait_ge(sem(f"{p}_ss"), ss_count(p, 1, t))
                    nc.vector.scalar_tensor_tensor(out=S(f"{p}_var", t, t + 1), in0=S(f"{p}_ss", 2 * t, 2 * t + 1), scalar=EPS,
                                                   in1=S(f"{p}_ss", 2 * t + 1, 2 * t + 2), op0=ALU.add,
                                                   op1=ALU.add).then_inc(sem(f"{p}_var"), 1)
                for t in tiles:
                    wait_drained(dve, name, t)
                    dve.wait_ge(sem(f"{p}_rstd"), t + 1)
                    for n in range(2):
                        v = x[:, t, n * C:(n + 1) * C]
                        nc.vector.scalar_tensor_tensor(out=v, in0=ygs(p)[:, t, n * C:(n + 1) * C], scalar=S(f"{p}_rstd", t, t + 1),
                                                       in1=v, op0=ALU.mult, op1=ALU.add).then_inc(sem(f"{xname}_rows"), 1)

            gained("p2", "reto0", 0, 1)()
            split(G["reto0"] + 3 + RING)

            def normed_rows(p, name, k, after):
                def go(t):
                    gained(p, name, 1, k)((t,))
                    residual(p, name, after, (t,))
                return go

            cross(GEND["reto1"], "x3T", "mpre0", normed_rows("p2", "reto1", 1, "x3"))

            def mlp(m, xname, p, after, gain, post_k):
                x_stats(xname)

                def up(n, i=None):
                    name = f"up{m}_{n}"
                    split(G[name] + RING, i)
                    split(GEND[name] - 1 + RING, i)

                def h_low(n, i=None):
                    lo = hTl[:, :, :].rearrange("p (n b k) t -> p n b k t", b=2, k=2)
                    hi = f32(hTh).rearrange("p (n b k) t -> p n b k t", b=2, k=2)
                    at_n = n if i is None else i * 2 + n
                    for b in range(2):
                        k, _ = AUX[(f"h{m}T{n % 2}", b)]
                        dve.wait_ge(sem(f"h{m}T_hi"), 2 * n + b + 1 if i is None else i * 4 + (2 * n + b + 1))
                        nc.vector.tensor_tensor(lo[:, at_n, b, :, :], per_kt(aux[k], 2), hi[:, at_n, b, :, :], ALU.subtract)\
                            .then_inc(aux_free[k], 1)

                up(0)
                up(1)
                h_low(0)
                with dve.Fori(1, 4) as i:
                    up(0, i)
                    h_low(-1, i)
                    up(1, i)
                    h_low(0, i)
                split(G[f"down{m}_0"] + RING)
                h_low(7)
                for g in range(G[f"down{m}_0"] + 1, GEND[f"down{m}_0"] - 1):
                    split(g + RING)
                gained(p, f"down{m}_0", 0, post_k)()
                split(GEND[f"down{m}_0"] - 1 + RING)
                for g in range(G[f"down{m}_1"], GEND[f"down{m}_1"] - RING):
                    split(g + RING)
                rows = normed_rows(p, f"down{m}_1", post_k, after)
                if gain:
                    cross(GEND[f"down{m}_1"], f"{after}T", gain, rows)
                else:
                    rows(0)
                    rows(1)

            mlp(0, "x3", "p3", "x4", "pre1", 2)
            x_stats("x4")
            unit("moba0")
            unit("moba1")
            unit("moba2")

            def bk_turned(j):
                for b in range(2):
                    turned(f"bkT{j}", b, bkT[:, 4 * j + 2 * b:4 * j + 2 * b + 2, :])

            def masked_max(h):
                pr = bprob if h < 4 else bprob2
                o = wait_aux(dve, "bsc", h)
                z0 = CONST["zero_mask"][0]
                nc.vector.tensor_tensor(pr[:, h % 4, 0, :], o[:, 0:TOK], cst[:, z0 + P:z0 + 3 * P], ALU.add)
                free(nc.vector.tensor_tensor(pr[:, h % 4, 1, :], o[:, TOK:2 * TOK], cst[:, z0:z0 + 2 * P], ALU.add), "bsc", h)
                wait_read(dve, "bsc", h)
                nm, b = S("bs_nm", 2 * h, 2 * h + 2), S("bs_b", 2 * h, 2 * h + 2)
                link(nc.vector.tensor_reduce(nm, pr[:, h % 4, :, :], AX.X, ALU.max, negate=True))
                link(nc.vector.tensor_scalar(nm, nm, -NEG, None, ALU.min))
                nc.vector.tensor_scalar(b, nm, NEG, None, ALU.add).then_inc(sem("b_max"), 1)

            def moba_probs(h):
                pr = bprob if h < 4 else bprob2
                dve.wait_ge(sem("b_exp"), 2 * h + 2)
                ks = (2 * h, 2 * h + 2)
                link(nc.vector.scalar_tensor_tensor(out=S("bs_l", *ks), in0=S("bs_b", *ks), scalar=float(TOK), in1=S("bs_sum", *ks),
                                                    op0=ALU.mult, op1=ALU.add))
                link(nc.vector.reciprocal(S("bs_rec", *ks), S("bs_l", *ks)))
                for t in range(2):
                    v = pr[:, h % 4, t, :]
                    nc.vector.tensor_scalar(v, v, S("bs_b", 2 * h + t, 2 * h + t + 1), S("bs_rec", 2 * h + t, 2 * h + t + 1),
                                            ALU.add, ALU.mult).then_inc(sem("b_prob"), 1)

            bk_turned(0)
            unit("moba3")
            for h in range(4):
                masked_max(h)
            moba_probs(0)
            moba_probs(1)
            bk_turned(1)
            moba_probs(2)
            moba_probs(3)
            unit("moba4")
            for h in (1, 3):
                turned("bpT", h, bpT[:, h, :, :])

            def second_max():
                for h in range(4, 8):
                    masked_max(h)

            def first_low():
                for h in range(4):
                    low("boT", h, byTl, byTh, (h,))

            unit("moba5", second_max, first_low, *(lambda h=h: moba_probs(h) for h in range(4, 8)))
            for h in (5, 7):
                wait_aux(dve, "boT", h - 4)
                turned("bpT", h, bpT[:, h % 4, :, :])
            for h in range(4, 8):
                low("boT", h, byTl, byTh, (h,))

            def out_rows_of(t):
                gained("p4", "mobao0", 0, 3)((t,))
                normed_rows("p4", "mobao1", 3, "x5")(t)

            cross(GEND["mobao1"], "x5T", "mpre1", out_rows_of)
            mlp(1, "x5", "p5", "x6", None, 4)



def kernel(**inputs):
    import concourse.bacc as _bacc
    from concourse.bass_utils import run_bass_kernel_spmd as _run

    I = {k: np.asarray(v) for k, v in inputs.items()}
    stream = np.zeros((NG, P, GK, C), np.float32)

    def put(name, w):
        k0 = 0
        for g in range(G[name], GEND[name]):
            nk = KTS[g]
            stream[g, :, 0:nk] = w[k0 * P:(k0 + nk) * P].reshape(nk, P, C).transpose(1, 0, 2)
            k0 += nk

    w_in, mkv = I["w_in"][0], I["w_mem_kv"][0]
    put("mk", mkv[:, 0:C])
    put("mv", mkv[:, C:2 * C])
    for n, c0 in IN_COLS.items():
        put(n, w_in[:, c0:c0 + C])
    for n in range(2):
        for b in BRANCHES:
            put(f"gate_{b}{n}", w_in[:, GATE_COL[b] + n * C:GATE_COL[b] + (n + 1) * C])
            put(f"branch_{b}{n}", I["w_branch"][0, BRANCH_ROW[b]][:, n * C:(n + 1) * C])
        for name, w in (("wout", I["w_out"][0]), ("ffd", I["w_ffn_down"][0]), ("reto", I["w_out_0_2"]),
                        ("down0_", I["w_down_0_2"]), ("mobao", I["w_out_1_2"]), ("down1_", I["w_down_1_2"])):
            put(f"{name}{n}", w[:, n * C:(n + 1) * C])
    for n in range(FFN // 256):
        s = slice(n * 256, (n + 1) * 256)
        put(f"ffn{n}", np.concatenate([I["w_ffn_gate"][0][:, s], I["w_ffn_up"][0][:, s]], axis=1))
    for n in range(12):
        put(f"ret{n}", I["w_in_0_2"][:, n * C:(n + 1) * C])
    for n, c0 in enumerate(MOBA_COLS):
        put(f"moba{n}", I["w_in_1_2"][:, c0:c0 + C])
    for n in range(8):
        put(f"up0_{n}", I["w_up_0_2"][:, n * C:(n + 1) * C])
        put(f"up1_{n}", I["w_up_1_2"][:, n * C:(n + 1) * C])

    def cols(v):
        return v.reshape(-1, P).T

    gpack = np.concatenate([cols(I[k].reshape(-1)) for k in (
        "g_mix", "g_mem", "g_ffn", "ln_mix_pre_0_2", "ln_mlp_pre_0_2", "ln_mix_pre_1_2", "ln_mlp_pre_1_2",
        "g_gla_out", "g_fox_q", "g_fox_k", "g_mem_q", "g_mem_k")], axis=1)
    narrow = np.concatenate([w_in[:, 1536:1552], w_in[:, 3088:3092]], axis=1).reshape(DK, P, 20).transpose(1, 0, 2)
    rett, mobat, dmask = rotary_tables()
    arrays = {
        "wstream": stream, "x": I["x"][0], "mem": I["mem"][0], "constants": CPACK, "gain_cols": gpack, "w_narrow": narrow,
        "w_gla_a2": I["w_gla_a2"][0], "b_gla_a": I["b_gla_a"], "b_fox_f": I["b_fox_f"], "b_gate": I["b_gate"],
        "post_gains": np.stack([I[k] for k in ("ln_mix_post_0_2", "ln_mlp_post_0_2", "ln_mix_post_1_2", "ln_mlp_post_1_2")]),
        "ret_tables": rett.reshape(P, 2, 2, 256), "moba_tables": mobat.reshape(P, 2, 2, 16), "ret_decays": dmask,
    }
    nc = _bacc.Bacc("TRN2", target_bir_lowering=False, num_devices=1)
    arrays = {f"in_{k}": np.ascontiguousarray(v, dtype=np.float32) for k, v in arrays.items()}
    args = [nc.dram_tensor(k, v.shape, mybir.dt.float32, kind="ExternalInput").ap() for k, v in arrays.items()]
    args.append(nc.dram_tensor("out", (TOK, D), mybir.dt.float32, kind="ExternalOutput").ap())
    build(nc, *args)
    r = _run(nc, [arrays], core_ids=[0])
    return r.results[0]["out"].reshape(1, TOK, D)
```
